# Optimizing a Trainium2 kernel written in Bass

```python
import math
import jax, jax.numpy as jnp
from jax import lax
import numpy as np

D_MODEL = 1024
BATCH = 1
SEQ = 512
DEPTH = 1

CHUNK = 64
Q_BLOCK = 128
MLA_HEADS = 8
MLA_NOPE = 64
MLA_ROPE = 32
MLA_V = 64
MLA_Q_RANK = 384
MLA_KV_RANK = 256
ROPE_THETA = 10000.0
RWKV_HEADS = 8
RWKV_HEAD = 64
RWKV_WIDTH = RWKV_HEADS * RWKV_HEAD
DECAY_RANK = 64
AAA_RANK = 64
GATE_RANK = 128
GN_EPS = 64e-5
N_GROUPS = 4
EXPERTS_PER_GROUP = 8
N_EXPERTS = N_GROUPS * EXPERTS_PER_GROUP
TOP_K_IN_GROUP = 2
EXPERT_FF = 256
RMS_EPS = 1e-6
N_BRANCHES = 2
NEG_INF = -1e30

MLA_IN = MLA_Q_RANK + MLA_KV_RANK + MLA_ROPE
RWKV_IN = 3 * RWKV_WIDTH + DECAY_RANK + AAA_RANK + GATE_RANK
GATE_IN = N_BRANCHES * D_MODEL
IN_WIDTH = MLA_IN + RWKV_IN + GATE_IN
IN_SPLITS = (MLA_Q_RANK, MLA_Q_RANK + MLA_KV_RANK, MLA_IN, MLA_IN + RWKV_IN)
RWKV_SPLITS = (RWKV_WIDTH, 2 * RWKV_WIDTH, 3 * RWKV_WIDTH, 3 * RWKV_WIDTH + DECAY_RANK, 3 * RWKV_WIDTH + DECAY_RANK + AAA_RANK)

kernel_name = 'hybrid_mla_rwkv7_hmoe_block'

def _rmsnorm(x, g):
    xf = x.astype(jnp.float32)
    y = xf * lax.rsqrt(jnp.mean(xf * xf, axis=-1, keepdims=True) + RMS_EPS)
    return (y * g.astype(jnp.float32)).astype(x.dtype)

def _modulate(x, g, shift, scale):
    return _rmsnorm(x, g) * (1.0 + scale) + shift

def _rope_tables(positions):
    inv_freq = jnp.power(ROPE_THETA, -jnp.arange(0, MLA_ROPE, 2, dtype=jnp.float32) / MLA_ROPE)
    ang = positions.astype(jnp.float32)[..., None] * inv_freq
    return jnp.cos(ang), jnp.sin(ang)

def _apply_rope(x, cos, sin):
    xf = x.astype(jnp.float32)
    x1, x2 = jnp.split(xf, 2, axis=-1)
    return jnp.concatenate([x1 * cos - x2 * sin, x2 * cos + x1 * sin], axis=-1).astype(x.dtype)

def _mla_branch(cq, ckv, kr, cos, sin, g_cq, w_uq, g_ckv, w_ukv):
    b, s, _ = cq.shape
    q = (_rmsnorm(cq, g_cq) @ w_uq).reshape(b, s, MLA_HEADS, MLA_NOPE + MLA_ROPE)
    kv = (_rmsnorm(ckv, g_ckv) @ w_ukv).reshape(b, s, MLA_HEADS, MLA_NOPE + MLA_V)
    q_nope, q_rope = q[..., :MLA_NOPE], q[..., MLA_NOPE:]
    k_nope, v = kv[..., :MLA_NOPE], kv[..., MLA_NOPE:]
    q_rope = _apply_rope(q_rope, cos[:, :, None, :], sin[:, :, None, :])
    k_rope = _apply_rope(kr, cos, sin)
    scale = 1.0 / math.sqrt(MLA_NOPE + MLA_ROPE)
    outs = []
    for qb in range(s // Q_BLOCK):
        q0, k_end = qb * Q_BLOCK, (qb + 1) * Q_BLOCK
        scores = (jnp.einsum('bqhd,bkhd->bhqk', q_nope[:, q0:k_end], k_nope[:, :k_end])
                  + jnp.einsum('bqhr,bkr->bhqk', q_rope[:, q0:k_end], k_rope[:, :k_end]))
        scores = scores.astype(jnp.float32) * scale
        q_chunk = (q0 + jnp.arange(Q_BLOCK)) // CHUNK
        k_chunk = jnp.arange(k_end) // CHUNK
        mask = k_chunk[None, :] <= q_chunk[:, None]
        scores = jnp.where(mask, scores, NEG_INF)
        p = jax.nn.softmax(scores, axis=-1).astype(v.dtype)
        outs.append(jnp.einsum('bhqk,bkhd->bqhd', p, v[:, :k_end]))
    return jnp.concatenate(outs, axis=1).reshape(b, s, MLA_HEADS * MLA_V)

def _token_shift(z, mu):
    z_prev = jnp.pad(z, ((0, 0), (1, 0), (0, 0)))[:, :-1]
    return z + (z_prev - z) * mu

def _rwkv7_step(state, inp):
    r, w, k, v, kk, a = inp
    sa = jnp.einsum('bhvk,bhk->bhv', state, -kk)
    state = state * w[:, :, None, :] + sa[..., None] * (kk * a)[:, :, None, :] + v[..., None] * k[:, :, None, :]
    y = jnp.einsum('bhvk,bhk->bhv', state, r)
    return state, y

def _rwkv7_branch(zr, mu_shift, w_decay_up, decay_bias, w_a_up, a_bias, w_g_up, k_k, k_a, r_k, lnx_w, lnx_b):
    b, s, _ = zr.shape
    zs = _token_shift(zr, mu_shift).astype(jnp.float32)
    r, k, v, wd, ad, gd = jnp.split(zs, RWKV_SPLITS, axis=-1)
    w_log = -jax.nn.softplus(-(decay_bias + jnp.tanh(wd) @ w_decay_up)) - 0.5
    decay = jnp.exp(-jnp.exp(w_log))
    a = jax.nn.sigmoid(a_bias + ad @ w_a_up)
    g = jax.nn.sigmoid(gd) @ w_g_up

    def heads(t):
        return t.reshape(b, s, RWKV_HEADS, RWKV_HEAD)

    kk = heads(k * k_k)
    kk = kk / jnp.maximum(jnp.sqrt(jnp.sum(kk * kk, axis=-1, keepdims=True)), 1e-12)
    k = k * (1.0 + (a - 1.0) * k_a)
    r_h, k_h, v_h, w_h, a_h = heads(r), heads(k), heads(v), heads(decay), heads(a)
    xs = (jnp.swapaxes(r_h, 0, 1), jnp.swapaxes(w_h, 0, 1), jnp.swapaxes(k_h, 0, 1),
          jnp.swapaxes(v_h, 0, 1), jnp.swapaxes(kk, 0, 1), jnp.swapaxes(a_h, 0, 1))
    state0 = jnp.zeros((b, RWKV_HEADS, RWKV_HEAD, RWKV_HEAD), jnp.float32)
    _, y = lax.scan(_rwkv7_step, state0, xs)
    y = jnp.swapaxes(y, 0, 1)
    mean = jnp.mean(y, axis=-1, keepdims=True)
    var = jnp.mean(jnp.square(y - mean), axis=-1, keepdims=True)
    y = ((y - mean) * lax.rsqrt(var + GN_EPS)).reshape(b, s, RWKV_WIDTH) * lnx_w + lnx_b
    bonus = jnp.sum(r_h * k_h * r_k, axis=-1, keepdims=True) * v_h
    out = (y + bonus.reshape(b, s, RWKV_WIDTH)) * g
    return out.astype(zr.dtype)

def _hier_moe(h, w_rg, b_rg, w_re, b_re, w_gate, w_up, w_down):
    b, s, d = h.shape
    hf = h.reshape(b * s, d)
    g_logits = (hf @ w_rg).astype(jnp.float32) + b_rg.astype(jnp.float32)
    g_sel = jnp.argmax(g_logits, axis=-1)
    p_sel = jnp.max(jax.nn.softmax(g_logits, axis=-1), axis=-1, keepdims=True)
    e_logits = ((hf @ w_re).astype(jnp.float32) + b_re.astype(jnp.float32)).reshape(-1, N_GROUPS, EXPERTS_PER_GROUP)
    e_in_group = jnp.einsum('tge,tg->te', e_logits, jax.nn.one_hot(g_sel, N_GROUPS, dtype=jnp.float32))
    top_vals, top_idx = lax.top_k(e_in_group, TOP_K_IN_GROUP)
    weights = p_sel * jax.nn.softmax(top_vals, axis=-1)
    expert_id = g_sel[:, None] * EXPERTS_PER_GROUP + top_idx
    combine = jnp.einsum('tke,tk->te', jax.nn.one_hot(expert_id, N_EXPERTS, dtype=jnp.float32), weights).astype(h.dtype)
    y = jnp.zeros_like(hf)
    for e in range(N_EXPERTS):
        act = jax.nn.silu(hf @ w_gate[e]) * (hf @ w_up[e])
        y = y + combine[:, e:e + 1] * (act @ w_down[e])
    return y.reshape(b, s, d)

def _hybrid_layer(x, c, cos, sin, w_ada, b_ada, g_pre_mix, g_post_mix, g_pre_ffn, g_post_ffn,
                  w_in, g_cq, w_uq, g_ckv, w_ukv, w_o_mla, mu_shift, w_decay_up, decay_bias,
                  w_a_up, a_bias, w_g_up, k_k, k_a, r_k, lnx_w, lnx_b, w_o_rwkv, w_out,
                  w_router_group, b_router_group, w_router_expert, b_router_expert,
                  w_exp_gate, w_exp_up, w_exp_down):
    mod = jax.nn.silu(c) @ w_ada + b_ada
    shift1, scale1, gate1, shift2, scale2, gate2 = jnp.split(mod[:, None, :], 6, axis=-1)
    h = _modulate(x, g_pre_mix, shift1, scale1)
    z = h @ w_in
    cq, ckv, kr, zr, gate_logits = jnp.split(z, IN_SPLITS, axis=-1)
    o_mla = _mla_branch(cq, ckv, kr, cos, sin, g_cq, w_uq, g_ckv, w_ukv) @ w_o_mla
    o_rwkv = _rwkv7_branch(zr, mu_shift, w_decay_up, decay_bias, w_a_up, a_bias, w_g_up,
                           k_k, k_a, r_k, lnx_w, lnx_b) @ w_o_rwkv
    gate_a, gate_b = jnp.split(jax.nn.sigmoid(gate_logits), 2, axis=-1)
    y = (gate_a * o_mla + gate_b * o_rwkv) @ w_out
    x = x + gate1 * _rmsnorm(y, g_post_mix)
    h = _modulate(x, g_pre_ffn, shift2, scale2)
    y = _hier_moe(h, w_router_group, b_router_group, w_router_expert, b_router_expert,
                  w_exp_gate, w_exp_up, w_exp_down)
    return x + gate2 * _rmsnorm(y, g_post_ffn)

def setup_inputs(seed: int = 0) -> dict:
    key = jax.random.key(seed)
    ks = iter(jax.random.split(key, 40))
    L, D = DEPTH, D_MODEL

    def nrm(shape, scale):
        return jax.random.normal(next(ks), shape, jnp.float32) * scale

    def gain(shape):
        return 1.0 + nrm(shape, 0.02)

    x = nrm((BATCH, SEQ, D), 1.0)
    c = nrm((BATCH, D), 1.0)
    offsets = jax.random.randint(next(ks), (BATCH, 1), 0, 256, dtype=jnp.int32) * CHUNK
    positions = (offsets + jnp.arange(SEQ, dtype=jnp.int32)[None, :]).astype(jnp.int32)
    return {
        'x': x, 'c': c, 'positions': positions,
        'w_ada': nrm((L, D, 6 * D), 0.5 * D ** -0.5),
        'b_ada': nrm((L, 6 * D), 0.02),
        'g_pre_mix': gain((L, D)), 'g_post_mix': gain((L, D)),
        'g_pre_ffn': gain((L, D)), 'g_post_ffn': gain((L, D)),
        'w_in': nrm((L, D, IN_WIDTH), D ** -0.5),
        'g_cq': gain((L, MLA_Q_RANK)),
        'w_uq': nrm((L, MLA_Q_RANK, MLA_HEADS * (MLA_NOPE + MLA_ROPE)), MLA_Q_RANK ** -0.5),
        'g_ckv': gain((L, MLA_KV_RANK)),
        'w_ukv': nrm((L, MLA_KV_RANK, MLA_HEADS * (MLA_NOPE + MLA_V)), MLA_KV_RANK ** -0.5),
        'w_o_mla': nrm((L, MLA_HEADS * MLA_V, D), (MLA_HEADS * MLA_V) ** -0.5),
        'mu_shift': jax.random.uniform(next(ks), (L, RWKV_IN), jnp.float32),
        'w_decay_up': nrm((L, DECAY_RANK, RWKV_WIDTH), 0.1 * DECAY_RANK ** -0.5),
        'decay_bias': jax.random.uniform(next(ks), (L, RWKV_WIDTH), jnp.float32, -5.0, -1.0),
        'w_a_up': nrm((L, AAA_RANK, RWKV_WIDTH), AAA_RANK ** -0.5),
        'a_bias': nrm((L, RWKV_WIDTH), 0.1),
        'w_g_up': nrm((L, GATE_RANK, RWKV_WIDTH), GATE_RANK ** -0.5),
        'k_k': 0.85 + nrm((L, RWKV_WIDTH), 0.02),
        'k_a': gain((L, RWKV_WIDTH)),
        'r_k': nrm((L, RWKV_HEADS, RWKV_HEAD), 0.1),
        'lnx_w': gain((L, RWKV_WIDTH)),
        'lnx_b': nrm((L, RWKV_WIDTH), 0.02),
        'w_o_rwkv': nrm((L, RWKV_WIDTH, D), RWKV_WIDTH ** -0.5),
        'w_out': nrm((L, D, D), D ** -0.5),
        'w_router_group': nrm((L, D, N_GROUPS), D ** -0.5),
        'b_router_group': nrm((L, N_GROUPS), 0.01),
        'w_router_expert': nrm((L, D, N_EXPERTS), D ** -0.5),
        'b_router_expert': nrm((L, N_EXPERTS), 0.01),
        'w_exp_gate': nrm((L, N_EXPERTS, D, EXPERT_FF), D ** -0.5),
        'w_exp_up': nrm((L, N_EXPERTS, D, EXPERT_FF), D ** -0.5),
        'w_exp_down': nrm((L, N_EXPERTS, EXPERT_FF, D), EXPERT_FF ** -0.5),
    }

def reference(x, c, positions, w_ada, b_ada, g_pre_mix, g_post_mix, g_pre_ffn, g_post_ffn,
              w_in, g_cq, w_uq, g_ckv, w_ukv, w_o_mla, mu_shift, w_decay_up, decay_bias,
              w_a_up, a_bias, w_g_up, k_k, k_a, r_k, lnx_w, lnx_b, w_o_rwkv, w_out,
              w_router_group, b_router_group, w_router_expert, b_router_expert,
              w_exp_gate, w_exp_up, w_exp_down):
    cos, sin = _rope_tables(positions)
    for l in range(DEPTH):
        x = _hybrid_layer(x, c, cos, sin, w_ada[l], b_ada[l], g_pre_mix[l], g_post_mix[l],
                          g_pre_ffn[l], g_post_ffn[l], w_in[l], g_cq[l], w_uq[l], g_ckv[l],
                          w_ukv[l], w_o_mla[l], mu_shift[l], w_decay_up[l], decay_bias[l],
                          w_a_up[l], a_bias[l], w_g_up[l], k_k[l], k_a[l], r_k[l], lnx_w[l],
                          lnx_b[l], w_o_rwkv[l], w_out[l], w_router_group[l], b_router_group[l],
                          w_router_expert[l], b_router_expert[l], w_exp_gate[l], w_exp_up[l],
                          w_exp_down[l])
    return x


_drawn_inputs = setup_inputs


def setup_inputs(seed=0):
    import zlib

    import numpy as np

    out = dict(_drawn_inputs(seed))
    spreads = {}
    factors = {'g_post_ffn': 26.521,
     'g_cq': 4.486,
     'g_ckv': 2.856,
     'lnx_w': 2.749,
     'b_router_expert': 6.1,
     'w_decay_up': 8.0,
     'lnx_b': 8.0}
    for name, (base, spread) in spreads.items():
        noise = np.random.default_rng([zlib.crc32(name.encode()), seed]).standard_normal(out[name].shape)
        drawn = base * np.exp(spread * noise) if base else spread * noise
        out[name] = __import__('jax').numpy.asarray(drawn.astype(out[name].dtype))
    for name, factor in factors.items():
        out[name] = (out[name] * factor).astype(out[name].dtype)
    return out
```

```python
import math
from contextlib import ExitStack

import numpy as np

import concourse.bass as bass
from concourse import mybir

F32 = mybir.dt.float32
I32 = mybir.dt.int32
ALU = mybir.AluOpType
ACT = mybir.ActivationFunctionType
AX = mybir.AxisListType

P = 128
S = 512
D = 1024
NT = S // P
ND = D // P
HEADS = 8
NOPE, ROPE, VD = 64, 32, 64
QR, KVR = 384, 256
RW = 512
NJ = RW // P
ZR = 3 * RW + 64 + 64 + 128
NZ = ZR // P
C_CKV, C_KR, C_ZR = QR, QR + KVR, QR + KVR + ROPE
C_GATE = C_ZR + ZR
NE, NG, EG, FF = 32, 4, 8, 256
ATT_SCALE = 1.0 / math.sqrt(NOPE + ROPE)
RMS_EPS, GN_EPS = 1e-6, 64e-5
DECAY = -math.exp(-0.5)
CH = 128
NC = S // CH
LEVELS = 7
NEG = -1e30
ROPE_THETA = 10000.0
ROUND = 1.5 * 2.0 ** 23
TWO_PI = 2 * math.pi

ROWS = {}
_at = 0
for _n, _k in (("b_ada", 48), ("g_pre_mix", 8), ("g_pre_ffn", 8), ("c", 8), ("g_cq", 3), ("g_ckv", 2),
               ("mu_shift", 14), ("decay_bias", 4), ("a_bias", 4), ("k_k", 4), ("k_a", 4), ("r_k", 4),
               ("lnx_w", 4), ("lnx_b", 4), ("inv_freq", 1)):
    ROWS[_n] = (_at, _k)
    _at += _k
NROWS = _at


def two_pi_parts():
    def short(x, bits):
        m, e = math.frexp(x)
        return math.ldexp(round(m * 2 ** bits) / 2 ** bits, e)
    a = short(TWO_PI, 11)
    b = short(TWO_PI - a, 11)
    return a, b, float(np.float32(TWO_PI - a - b))


def job_list():
    jobs = ["par", "ada0", "ada1", "ada2", "ada3"]
    jobs += [f"xT{j}" for j in range(ND)]
    jobs += ["cq0", "cq1", "cq2", "cqss", "ckv0", "ckv1", "ckvss", "kr", "krs"]
    jobs += ["ada4"]
    jobs += [f"z{j}" for j in range(0, 4)] + ["ada5"]
    jobs += [f"z{j}" for j in range(4, 8)] + ["ada6"]
    jobs += [f"z{j}" for j in range(8, 12)] + ["ada7"]
    jobs += ["z12", "z13"]
    for t in range(2):
        jobs += [f"qr{t}", f"qs{t}"]
    jobs += [f"qn{j}" for j in range(4)] + [f"kn{j}" for j in range(4)] + [f"v{i}" for i in range(NT)]
    jobs += [f"ada{c}" for c in range(8, 12)]
    units = [(h, q) for h in range(HEADS) for q in range(NT)]
    for u in range(len(units) + 2):
        if u < len(units):
            jobs.append("s%d_%d" % units[u])
        if u >= 2:
            h, q = units[u - 2]
            jobs.append(f"t{h}_{q}")
            if q == NT - 1:
                jobs.append(f"o{h}")
    jobs += [f"uw{j}" for j in range(NJ)] + [f"ua{j}" for j in range(NJ)] + [f"ug{j}" for j in range(NJ)]
    jobs += [f"kss{j}" for j in range(NJ)] + [f"bon{j}" for j in range(NJ)]
    for c in range(NC):
        for g in range(2):
            jobs += [f"mr{c}_{g}_{b}" for b in range(2)]
            jobs += [f"nr{c}_{g}_{b}" for b in range(2)]
        jobs += [f"tok{c}_{n}" for n in range(3)]
        jobs += [f"x{c}_{g}" for g in range(2)]
        for l in range(1, LEVELS):
            jobs += [f"p{c}_{l}_{g}" for g in range(2)]
            if l < LEVELS - 1:
                jobs += [f"dx{c}_{l}_{g}" for g in range(2)]
            jobs += [f"dt{c}_{l}_{g}" for g in range(2)]
        jobs += [f"rhs{c}_{g}" for g in range(2)] + [f"sa{c}"] + [f"y{c}_{g}" for g in range(2)]
        if c < NC - 1:
            jobs += [f"st{c}"]
    jobs += [f"gm{j}" for j in range(NJ)] + [f"gv{j}" for j in range(NJ)]
    for hf in range(2):
        for k in ("ga", "gb", "om", "or"):
            jobs += [f"{k}{hf}_{j}" for j in range(4)]
    jobs += [f"yo{i}_{n}" for i in range(NT) for n in range(2)]
    jobs += [f"hT{j}" for j in range(ND)]
    jobs += [f"lg{i}" for i in range(NT)]
    return jobs


def layer(nc, I, out):
    JOBS = {n: i for i, n in enumerate(job_list())}
    TP1, TP2, TP3 = two_pi_parts()

    with ExitStack() as ctx:
        arena = ctx.enter_context(nc.sbuf_tensor("arena", [P, 206 * 256], F32))
        ps = ctx.enter_context(nc.psum_tensor("ps", [P, 8, 512], F32))

        def at(kb, *shape):
            n = 1
            for s in shape:
                n *= s
            v = arena[:, int(kb * 256):int(kb * 256) + n]
            if len(shape) == 1:
                return v
            names = [chr(97 + i) for i in range(len(shape))]
            return v.rearrange(f"p ({' '.join(names)}) -> p {' '.join(names)}", **dict(zip(names, shape)))

        sems = {}

        def sem(name):
            if name not in sems:
                sems[name] = ctx.enter_context(nc.semaphore(name))
            return sems[name]

        psum_full = [sem(f"psum_full{b}") for b in range(8)]
        psum_free = [sem(f"psum_free{b}") for b in range(8)]

        SLOT, NSLOT = 16, 3

        HT = at(48, ND, S)
        X = at(64, NT, D)
        SQ = at(64, 5, S)
        Q, K, V = at(64, HEADS, S), at(80, HEADS, S), at(96, NT, RW)
        CQ, CKV, KR, KRS = at(104, 3, S), at(110, 2, S), at(114, S), at(116, S)
        OT = at(118, NJ, S)
        ZS = at(126, NZ, S)
        RAW = at(154, 4, S + 1)
        PROWS = at(104, P)
        IDXP, IDXF, IDXX = (at(k, P).bitcast(I32) for k in (104.5, 105, 105.5))
        POSI = at(106, S).bitcast(I32)
        ACC = at(163, 2, S)
        TR = at(167, 5, S)
        SWK = at(180, 8, 32)
        COS, SIN = at(181, S), at(183, S)
        PR, PT = at(163, 3, S), at(169, 2, NT, S)
        AR = at(64, NJ, NC, 2, CH)
        CUM = KT = at(80, NJ, S)
        RESET = BT = at(88, NJ, S)
        G, SW, AA = at(96, NJ, S), at(104, NJ, S), at(154, NJ, S)
        T1, KK = at(163, NJ, S), at(171, NJ, S)
        RZ, KZ, VZ = ZS[:, 0:4], ZS[:, 4:8], ZS[:, 8:12]
        XI, XT, SA = at(104, HEADS, CH), at(108, HEADS, CH), at(112, HEADS, VD)
        BTOK, KTOK, VTOK, ST = at(114, RW), at(116, RW), at(150, RW), at(152, NJ, VD)
        TOK = [BTOK, KTOK, VTOK]
        MOFF = at(154, 2, HEADS, CH)
        MR, NR = at(163, HEADS, 2 * CH), at(171, HEADS, 2 * CH)
        P1, RHS = at(179, HEADS, CH), at(183, HEADS, VD)
        BONUS, YT = RZ, KZ
        GA, GB, MIX = at(163, 4, S), at(171, 4, S), at(80, ND, S)
        XN2, YACC, JUNK = at(126, NT, D), at(142, NT, D), at(104, D)
        ACTT, SIL, TUP = at(80, 2, 2, S), at(88, 2, 2, S), at(108, S)
        IDENT, XU, MASKS, MASK2 = at(185, P), at(185.5, P), at(186, LEVELS, P), at(189.5, 2, P)
        BO, BOM, ONES, PAR = at(190.5, P), at(191, P), at(191.5, P), at(192, P)
        GROW = at(192.5, 2, D)
        COLS = at(200.5, 160)
        MODA1, MODB1, MODA2, MODB2 = (COLS[:, 8 * i:8 * i + 8] for i in range(4))
        OMKA, SS2, RS2, SIGN = COLS[:, 32:36], COLS[:, 36:40], COLS[:, 40:44], COLS[:, 44:45]
        SSY, SS4 = COLS[:, 48:56], COLS[:, 56:60]
        SILC, SS, RSTD = COLS[:, 64:72], COLS[:, 72:76], COLS[:, 76:80]
        RSUM, RINV = COLS[:, 96:128], COLS[:, 128:160]
        WR = at(201.25, ND, 36)
        MX, NMX = at(202.5, 32), at(202.75, 32)
        MID, FDEC = at(203, NJ, NC), at(203.25, NJ, NC)
        COMB = at(203.5, NT, NE)
        BR = at(204, 36)
        LOGITS = at(163, NT, 36)
        GHOT, GEXP = at(164, NT, NG), at(164.25, NT, NG)
        EIN, ETMP, HOT1, HOT2 = (at(164.5 + 0.25 * k, NT, EG) for k in range(4))
        GMX, PSEL, EMX1, EMX2, E21, W1, TMX, DUM = (at(165.5 + 0.0625 * k, NT) for k in range(8))
        RANKW, CB = at(166, 8), at(166.25, 2, NT)
        EW = [(at(24 * s, ND, FF), at(24 * s + 8, ND, FF), at(24 * s + 16, 2, D)) for s in range(2)]

        def par(v, j=None):
            a, k = ROWS[v]
            return PAR[:, a:a + k] if j is None else PAR[:, a + j:a + j + 1]

        def wsrc(w, c0, n, k=ND):
            return w[:, c0:c0 + n].rearrange("(k p) n -> p k n", p=P)
        W = {n: I[n][0] for n in ("w_ada", "w_in", "w_uq", "w_ukv", "w_o_mla", "w_o_rwkv", "w_out")}
        items = [(f"ada{c}", "dve", wsrc(W["w_ada"], 512 * c, 512)) for c in range(4)]
        items += [("cq", "pe", wsrc(W["w_in"], 0, 384)), ("kv", "pe", wsrc(W["w_in"], C_CKV, 288)),
                  ("ada4", "dve", wsrc(W["w_ada"], 2048, 512)),
                  ("r", "pe", wsrc(W["w_in"], C_ZR, 512)), ("ada5", "dve", wsrc(W["w_ada"], 2560, 512)),
                  ("k", "pe", wsrc(W["w_in"], C_ZR + 512, 512)), ("ada6", "dve", wsrc(W["w_ada"], 3072, 512)),
                  ("vv", "pe", wsrc(W["w_in"], C_ZR + 1024, 512)), ("ada7", "dve", wsrc(W["w_ada"], 3584, 512)),
                  ("wag", "pe", wsrc(W["w_in"], C_ZR + 1536, 256)),
                  ("uq", "pe", wsrc(W["w_uq"], 0, 768)), ("ukv", "pe", wsrc(W["w_ukv"], 0, 1024))]
        items += [(f"ada{c}", "dve", wsrc(W["w_ada"], 512 * c, 512)) for c in range(8, 12)]
        items += [("ups", "pe", None)]
        for hf in range(2):
            c0 = 512 * hf
            items += [(f"ga{hf}", "pe", wsrc(W["w_in"], C_GATE + c0, 512)),
                      (f"gb{hf}", "pe", wsrc(W["w_in"], C_GATE + D + c0, 512)),
                      (f"oo{hf}", "pe", (wsrc(W["w_o_mla"], c0, 512), wsrc(W["w_o_rwkv"], c0, 512)))]
        items += [(f"wo{n}", "pe", wsrc(W["w_out"], 512 * n, 512)) for n in range(2)]
        SEQ = {n: i for i, (n, _, _) in enumerate(items)}
        NPARTS = {"uq": 12, "ukv": 4, "ups": 3, "oo0": 2, "oo1": 2}
        landed = []
        slot_count = [0] * NSLOT
        for i, (n, _, _) in enumerate(items):
            slot_count[i % NSLOT] += 16 * NPARTS.get(n, 1)
            landed.append(slot_count[i % NSLOT])
        used_n, used_by = {"pe": 0, "dve": 0}, []
        for n, who, _ in items:
            used_n[who] += 1
            used_by.append((who, used_n[who]))

        def wbuf(name, *shape):
            return at(SLOT * (SEQ[name] % NSLOT), *shape)

        def wait_weights(eng, name):
            i = SEQ[name]
            eng.wait_ge(sem(f"w_landed{i % NSLOT}"), landed[i])

        def full(eng, job):
            n = JOBS[job]
            eng.wait_ge(psum_full[n % 8], n // 8 + 1)

        def bank_of(job):
            return JOBS[job] % 8

        def bank(job):
            return ps[:, JOBS[job] % 8, :]

        block = ctx.enter_context(nc.Block())


        LAST_JOB = {"cq": "cq2", "kv": "krs", "r": "z3", "k": "z7", "vv": "z11", "wag": "z13", "uq": "qn3",
                    "ukv": "v3", "ups": "ug3", "ga0": "ga0_3", "ga1": "ga1_3", "gb0": "gb0_3", "gb1": "gb1_3",
                    "oo0": "or0_3", "oo1": "or1_3", "wo0": "yo3_0", "wo1": "yo3_1"}
        UNITS = [(h, q) for h in range(HEADS) for q in range(NT)]
        BASE = [sum(1 for n in JOBS.values() if n % 8 == b) for b in range(8)]
        N0 = len(JOBS)

        def MOE_SEQ(n):
            return sum(1 for m in range(N0, n) if m % 8 == n % 8)

        def drained(eng, job):
            n = JOBS[job]
            eng.wait_ge(psum_free[n % 8], n // 8 + 1)

        def flat(name):
            v = I[name]
            return v.rearrange("a h c -> a (h c)") if len(v.shape) == 3 else v

        @block.sync
        def _(sp):
            for name, (a, k) in ROWS.items():
                sp.dma_start(PROWS[a:a + k, :], flat(name).rearrange("a (k p) -> (a k) p", p=P)).then_inc(sem("rows_landed"), 16)
            sp.dma_start(POSI, I["positions"].partition_broadcast(P).rearrange("p a s -> p (a s)")).then_inc(sem("pos_landed"), 16)
            sp.dma_start(X, I["x"][0].rearrange("(i p) d -> p i d", p=P)).then_inc(sem("x_landed"), 16)
            for i, (name, who, src) in enumerate(items):
                if i >= NSLOT:
                    before = items[i - NSLOT][0]
                    if items[i - NSLOT][1] == "pe":
                        full(sp, LAST_JOB[before])
                    else:
                        sp.wait_ge(sem("ada_ready"), int(before[3:]) + 1)
                landed_sem = sem(f"w_landed{i % NSLOT}")
                if name == "ups":
                    u = wbuf(name, 2, 512)
                    sp.dma_start(u[0:64, 0, :], I["w_decay_up"][0]).then_inc(landed_sem, 16)
                    sp.dma_start(u[64:128, 0, :], I["w_a_up"][0]).then_inc(landed_sem, 16)
                    sp.dma_start(u[:, 1, :], I["w_g_up"][0]).then_inc(landed_sem, 16)
                elif name == "uq":
                    u, w4 = wbuf(name, 3, 1024), src.rearrange("p k (h c) -> p k h c", h=HEADS)
                    for k in range(3):
                        for dst, c0, n in ((u[:, k, 0:256].rearrange("p (h c) -> p h c", h=HEADS), 64, 32),
                                           (u[:, k, 256:512].rearrange("p (h c) -> p h c", h=HEADS)[:, :, 0:16], 80, 16),
                                           (u[:, k, 256:512].rearrange("p (h c) -> p h c", h=HEADS)[:, :, 16:32], 64, 16),
                                           (u[:, k, 512:1024].rearrange("p (h c) -> p h c", h=HEADS), 0, 64)):
                            sp.dma_start(dst, w4[:, k, :, c0:c0 + n]).then_inc(landed_sem, 16)
                elif name == "ukv":
                    u, w4 = wbuf(name, 2, 2, 512), src.rearrange("p k (h c) -> p k h c", h=HEADS)
                    for k in range(2):
                        for n in range(2):
                            sp.dma_start(u[:, k, n, :].rearrange("p (h c) -> p h c", h=HEADS),
                                         w4[:, k, :, 64 * n:64 * n + 64]).then_inc(landed_sem, 16)
                elif name[:2] == "oo":
                    u = wbuf(name, 2, 4, 512)
                    for n in range(2):
                        sp.dma_start(u[:, n], src[n]).then_inc(landed_sem, 16)
                else:
                    sp.dma_start(wbuf(name, src.shape[1], src.shape[2]), src).then_inc(landed_sem, 16)
                if name == "ada3":
                    sp.dma_start(GROW[:, 0, :], I["g_post_mix"].partition_broadcast(P).rearrange("p a s -> p (a s)")).then_inc(sem("grow_landed"), 16)
                    sp.dma_start(GROW[:, 1, :], I["g_post_ffn"].partition_broadcast(P).rearrange("p a s -> p (a s)")).then_inc(sem("grow_landed"), 16)
                    sp.dma_start(WR[:, :, 0:NG], wsrc(I["w_router_group"][0], 0, NG)).then_inc(sem("wr_landed"), 16)
                    sp.dma_start(WR[:, :, NG:], wsrc(I["w_router_expert"][0], 0, NE)).then_inc(sem("wr_landed"), 16)
                    sp.dma_start(BR[0:1, 0:NG], I["b_router_group"]).then_inc(sem("wr_landed"), 16)
                    sp.dma_start(BR[0:1, NG:], I["b_router_expert"]).then_inc(sem("wr_landed"), 16)
            full(sp, f"y{NC - 1}_1")
            sp.dma_start(X, I["x"][0].rearrange("(i p) d -> p i d", p=P)).then_inc(sem("x_landed"), 16)
            full(sp, "yo3_1")
            with sp.Fori(0, NE // 2) as i:
                for s in range(2):
                    last = N0 + 12 * s + 11
                    sp.wait_ge(psum_full[last % 8], BASE[last % 8] + 3 * i + MOE_SEQ(last) - 2)
                    e = i * 2 + s
                    ew = sem(f"expert_landed{s}")
                    sp.dma_start(EW[s][0], I["w_exp_gate"][0, bass.ds(e, 1)].rearrange("a (k p) n -> p (a k) n", p=P)).then_inc(ew, 16)
                    sp.dma_start(EW[s][1], I["w_exp_up"][0, bass.ds(e, 1)].rearrange("a (k p) n -> p (a k) n", p=P)).then_inc(ew, 16)
                    sp.dma_start(EW[s][2], I["w_exp_down"][0, bass.ds(e, 1)].rearrange("a (k p) n -> p (a k) n", p=P)).then_inc(ew, 16)
            for i in range(NT):
                sp.wait_ge(sem("out_ready"), i + 1)
                sp.dma_start(out[0, i * P:(i + 1) * P, :], X[:, i, :]).then_inc(sem("out_stored"), 16)
            sp.wait_ge(sem("out_stored"), 16 * NT)

        @block.gpsimd
        def _(pool):
            step = [0]

            def link(ins):
                step[0] += 1
                ins.then_inc(sem("pool_step"), 1)
                pool.wait_ge(sem("pool_step"), step[0])

            nc.gpsimd.iota(IDXP, [[0, P]], base=0, channel_multiplier=1).then_inc(sem("iota"), 1)
            pool.wait_ge(sem("iota"), 1)
            nc.gpsimd.iota(IDXF, [[1, P]], base=0, channel_multiplier=0).then_inc(sem("iota"), 1)
            pool.wait_ge(sem("iota"), 2)
            nc.gpsimd.memset(ONES, 1.0).then_inc(sem("ones"), 1)
            pool.wait_ge(sem("ones"), 1)
            link(nc.gpsimd.memset(RAW[:, :, 0:1], 0.0))
            wait_weights(pool, "kv")
            kv = wbuf("kv", ND, 288)
            link(nc.gpsimd.tensor_copy(SWK[:, :, 0:16], kv[:, :, 272:288]))
            nc.gpsimd.tensor_copy(SWK[:, :, 16:32], kv[:, :, 256:272]).then_inc(sem("swk"), 1)
            pool.wait_ge(sem("swk"), 1)
            full(pool, "z0")
            link(nc.gpsimd.memset(Q[96:100], 1.0))
            link(nc.gpsimd.affine_select(out=Q[96:100], in_=Q[96:100], compare_op=ALU.is_ge, fill=0.0, base=0,
                                        pattern=[[0, HEADS], [1, S]], channel_multiplier=-P))
            link(nc.gpsimd.affine_select(out=Q[96:100], in_=Q[96:100], compare_op=ALU.is_ge, fill=0.0, base=63,
                                        pattern=[[0, HEADS], [-1, S]], channel_multiplier=P))
            link(nc.gpsimd.memset(K[96:100], NEG))
            link(nc.gpsimd.affine_select(out=K[96:100], in_=K[96:100], compare_op=ALU.is_ge, fill=0.0, base=-64,
                                        pattern=[[0, HEADS], [1, S]], channel_multiplier=-P))
            nc.gpsimd.affine_select(out=K[96:100], in_=K[96:100], compare_op=ALU.is_ge, fill=0.0, base=127, pattern=[[0, HEADS], [-1, S]], channel_multiplier=P).then_inc(sem("chunk_mask"), 1)
            pool.wait_ge(sem("chunk_mask"), 1)
            pool.wait_ge(sem("k_rope0"), 1)
            nc.gpsimd.tensor_copy(K[64:96, 1:HEADS, :], K[64:96, 0:1, :].to_broadcast([32, HEADS - 1, S])).then_inc(sem("k_rope"), 1)
            pool.wait_ge(sem("k_rope"), 1)
            for c in range(NC):
                if c > 0:
                    full(pool, f"sa{c - 1}")
                for g in range(2):
                    drained(pool, f"mr{c}_{g}_0")
                    drained(pool, f"mr{c}_{g}_1")
                    mt = MR[:, 4 * g:4 * g + 4, 0:CH]
                    xt = XT[:, 4 * g:4 * g + 4, :]
                    link(nc.gpsimd.tensor_tensor(xt, mt, MASKS[:, 0:1, :].to_broadcast([P, 4, CH]), ALU.mult))
                    nc.gpsimd.tensor_tensor(xt, xt, IDENT.unsqueeze(1).to_broadcast([P, 4, CH]), ALU.add).then_inc(sem("xt_start"), 1)
                    pool.wait_ge(sem("xt_start"), 2 * c + g + 1)
                for l in range(1, LEVELS):
                    for g in range(2):
                        if l > 2:
                            full(pool, f"p{c}_{l - 2}_{g}")
                        nc.gpsimd.tensor_tensor(MOFF[:, l % 2, 4 * g:4 * g + 4, :], MR[:, 4 * g:4 * g + 4, 0:CH], MASKS[:, l:l + 1, :].to_broadcast([P, 4, CH]), ALU.mult).then_inc(sem("moff"), 1)
                        pool.wait_ge(sem("moff"), 2 * ((LEVELS - 1) * c + l - 1) + g + 1)

        @block.tensor
        def _(pe):
            T = nc.tensor
            state = {"n": 0}

            def fill(job):
                n = JOBS[job]
                assert n == state["n"], (job, n, state["n"])
                state["n"] += 1
                if n >= 8:
                    pe.wait_ge(psum_free[n % 8], n // 8)
                return ps[:, n % 8, :]

            def project(job, lhs, rhs, n_k, o=None):
                b = fill(job)
                o = b if o is None else o(b)
                for k in range(n_k):
                    mm = T.matmul(o, lhs(k), rhs(k), start=(k == 0), stop=(k == n_k - 1))
                mm.then_inc(psum_full[bank_of(job)], 1)

            def ada(c):
                job = f"ada{c}"
                b = fill(job)
                pe.wait_ge(sem("ada_ready"), c + 1)
                a = ACC[:, c % 2, :]
                if c in (4, 5, 10, 11):
                    mm = T.matmul(b, ONES, a, start=True, stop=False)
                    for n in range(4):
                        mm = T.matmul(b[:, n * P:(n + 1) * P], par("b_ada", 4 * c + n).to_broadcast([P, P]), IDENT,
                                      start=False, stop=(n == 3))
                else:
                    for n in range(4):
                        mm = T.matmul(b[:, n:n + 1], a[:, n * P:(n + 1) * P], ONES[:, 0:1], start=True, stop=True)
                mm.then_inc(psum_full[bank_of(job)], 1)

            pe.wait_ge(sem("rows_landed"), 16 * len(ROWS))
            pe.wait_ge(sem("masks"), 1)
            b = fill("par")
            mm = T.transpose(b[:, 0:NROWS], PROWS[0:NROWS, :], IDENT[0:NROWS, 0:NROWS])
            mm.then_inc(psum_full[bank_of("par")], 1)
            pe.wait_ge(sem("ones"), 1)
            for c in range(4):
                ada(c)
            pe.wait_ge(sem("xn"), 1)
            for j in range(ND):
                b = fill(f"xT{j}")
                for i in range(NT):
                    mm = T.transpose(b[:, i * P:(i + 1) * P], X[:, i, j * P:(j + 1) * P], IDENT)
                mm.then_inc(psum_full[bank_of(f"xT{j}")], 1)
            for j in range(ND):
                drained(pe, f"xT{j}")
            h = lambda k: HT[:, k, :]
            wait_weights(pe, "cq")
            w = wbuf("cq", ND, 384)
            for t in range(3):
                project(f"cq{t}", lambda k: w[:, k, t * P:(t + 1) * P], h, ND)
            for t in range(3):
                drained(pe, f"cq{t}")
            project("cqss", lambda k: ONES, lambda k: SQ[:, k, :], 3)
            wait_weights(pe, "kv")
            wk = wbuf("kv", ND, 288)
            for t in range(2):
                project(f"ckv{t}", lambda k: wk[:, k, t * P:(t + 1) * P], h, ND)
            for t in range(2):
                drained(pe, f"ckv{t}")
            project("ckvss", lambda k: ONES, lambda k: SQ[:, 3 + k, :], 2)
            project("kr", lambda k: wk[:, k, 256:288], h, ND, lambda b: b[64:96, :])
            pe.wait_ge(sem("swk"), 1)
            project("krs", lambda k: SWK[:, k, :], h, ND, lambda b: b[64:96, :])
            ada(4)
            for n, name in enumerate(("r", "k", "vv")):
                wait_weights(pe, name)
                w = wbuf(name, ND, 512)
                for t in range(4):
                    project(f"z{4 * n + t}", lambda k: w[:, k, t * P:(t + 1) * P], h, ND)
                ada(5 + n)
            wait_weights(pe, "wag")
            w = wbuf("wag", ND, 256)
            for t in range(2):
                project(f"z{12 + t}", lambda k: w[:, k, t * P:(t + 1) * P], h, ND)
            pe.wait_ge(sem("cqn"), 1)
            wait_weights(pe, "uq")
            uq = wbuf("uq", 3, 1024)
            for t in range(2):
                project(f"qr{t}", lambda k: uq[:, k, P * t:P * t + P], lambda k: CQ[:, k, :], 3)
                project(f"qs{t}", lambda k: uq[:, k, 256 + P * t:256 + P * t + P], lambda k: CQ[:, k, :], 3)
            for j in range(4):
                project(f"qn{j}", lambda k: uq[:, k, 512 + P * j:512 + P * j + P], lambda k: CQ[:, k, :], 3)
            pe.wait_ge(sem("ckvn"), 1)
            wait_weights(pe, "ukv")
            ukv = wbuf("ukv", 2, 2, 512)
            for j in range(4):
                project(f"kn{j}", lambda k: ukv[:, k, 0, P * j:P * j + P], lambda k: CKV[:, k, :], 2)
            for i in range(NT):
                project(f"v{i}", lambda k: CKV[:, k, i * P:(i + 1) * P], lambda k: ukv[:, k, 1, :], 2)
            for c in range(8, 12):
                ada(c)
            pe.wait_ge(sem("q_rope"), 8)
            pe.wait_ge(sem("k_rope"), 1)
            pe.wait_ge(sem("chunk_mask"), 1)
            for j in range(4):
                drained(pe, f"qn{j}")
                drained(pe, f"kn{j}")
                drained(pe, f"v{j}")
            for u in range(len(UNITS) + 2):
                if u < len(UNITS):
                    hd, q = UNITS[u]
                    project(f"s{hd}_{q}", lambda k: Q[0:100, hd, q * P:(q + 1) * P],
                            lambda k: K[0:100, hd, 0:(q + 1) * P], 1, lambda b: b[:, 0:(q + 1) * P])
                if u >= 2:
                    hd, q = UNITS[u - 2]
                    b = fill(f"t{hd}_{q}")
                    pe.wait_ge(sem("p_ready"), u - 1)
                    for kb in range(q + 1):
                        mm = T.transpose(b[:, kb * P:(kb + 1) * P], PR[:, (u - 2) % 3, kb * P:(kb + 1) * P], IDENT)
                    mm.then_inc(psum_full[bank_of(f"t{hd}_{q}")], 1)
                    if q == NT - 1:
                        b = fill(f"o{hd}")
                        drained(pe, f"t{hd}_{q}")
                        r = slice(64 * (hd % 2), 64 * (hd % 2) + 64)
                        for kb in range(NT):
                            mm = T.matmul(b[r, kb * P:], V[:, kb, hd * VD:(hd + 1) * VD], PT[:, hd % 2, kb, kb * P:],
                                          start=(kb == 0), stop=(kb == NT - 1))
                        mm.then_inc(psum_full[bank_of(f"o{hd}")], 1)
            wait_weights(pe, "ups")
            up = wbuf("ups", 2, 512)
            pe.wait_ge(sem("lowrank"), 2)
            for j in range(NJ):
                project(f"uw{j}", lambda k: up[0:64, 0, j * P:(j + 1) * P], lambda k: ZS[0:64, 12, :], 1)
            for j in range(NJ):
                project(f"ua{j}", lambda k: up[64:128, 0, j * P:(j + 1) * P], lambda k: ZS[64:128, 12, :], 1)
            for j in range(NJ):
                project(f"ug{j}", lambda k: up[:, 1, j * P:(j + 1) * P], lambda k: ZS[:, 13, :], 1)
            for j in range(NJ):
                pe.wait_ge(sem("kk_sq"), j + 1)
                project(f"kss{j}", lambda k: BO, lambda k: T1[:, j, :], 1)
            for j in range(NJ):
                pe.wait_ge(sem("rk"), j + 1)
                project(f"bon{j}", lambda k: BO, lambda k: RZ[:, j, :], 1)
            pe.wait_ge(sem("rwkv_in"), 1)
            for c in range(NC):
                cs = slice(c * CH, (c + 1) * CH)
                for g in range(2):
                    r = slice(64 * g, 64 * g + 64)
                    for name, src in (("mr", BT), ("nr", KT)):
                        for n in range(2):
                            b = fill(f"{name}{c}_{g}_{n}")
                            for m in range(2):
                                j = 2 * n + m
                                mm = T.matmul(b[:, m * 256:(m + 1) * 256], src[r, j, cs],
                                              AR[r, j, c, :, :].rearrange("p a t -> p (a t)"), start=True, stop=True)
                            mm.then_inc(psum_full[bank_of(f"{name}{c}_{g}_{n}")], 1)
                for n, src in enumerate((BT, KT, VZ)):
                    b = fill(f"tok{c}_{n}")
                    for j in range(NJ):
                        mm = T.transpose(b[:, j * P:(j + 1) * P], src[:, j, cs], IDENT)
                    mm.then_inc(psum_full[bank_of(f"tok{c}_{n}")], 1)
                for g in range(2):
                    b = fill(f"x{c}_{g}")
                    pe.wait_ge(sem("xt_start"), 2 * c + g + 1)
                    for j in range(4):
                        mm = T.transpose(b[:, j * P:(j + 1) * P], XT[:, 4 * g + j, :], IDENT)
                    mm.then_inc(psum_full[bank_of(f"x{c}_{g}")], 1)

                def stage(job, g, lhs, rhs):
                    b = fill(job)
                    for j in range(4):
                        mm = T.matmul(b[:, j * P:(j + 1) * P], lhs[:, 4 * g + j, :], rhs[:, 4 * g + j, :], start=True, stop=True)
                    mm.then_inc(psum_full[bank_of(job)], 1)
                for l in range(1, LEVELS):
                    for g in range(2):
                        pe.wait_ge(sem("moff"), 2 * ((LEVELS - 1) * c + l - 1) + g + 1)
                        drained(pe, f"x{c}_{g}" if l == 1 else f"dx{c}_{l - 1}_{g}")
                        stage(f"p{c}_{l}_{g}", g, MOFF[:, l % 2], XI)
                    if l < LEVELS - 1:
                        for g in range(2):
                            drained(pe, f"p{c}_{l}_{g}")
                            if l > 1:
                                drained(pe, f"dt{c}_{l - 1}_{g}")
                            stage(f"dx{c}_{l}_{g}", g, XT, P1)
                    for g in range(2):
                        drained(pe, f"p{c}_{l}_{g}")
                        if l > 1:
                            drained(pe, f"dt{c}_{l - 1}_{g}")
                        stage(f"dt{c}_{l}_{g}", g, P1, XT)
                for n in range(3):
                    drained(pe, f"tok{c}_{n}")
                for g in range(2):
                    r = slice(64 * g, 64 * g + 64)
                    b = fill(f"rhs{c}_{g}")
                    if c > 0:
                        drained(pe, f"st{c - 1}")
                        for j in range(4):
                            T.matmul(b[:, j * 64:j * 64 + 64], AR[r, j, c, 0, :], ST[r, j, :], start=(j == 0),
                                     stop=False, skip_group_check=True)
                    for j in range(4):
                        hd = 2 * j + g
                        mm = T.matmul(b[:, j * 64:j * 64 + 64], NR[:, 4 * g + j, 0:CH], VTOK[:, hd * 64:hd * 64 + 64],
                                      start=(c == 0), stop=True, skip_group_check=c > 0)
                    mm.then_inc(psum_full[bank_of(f"rhs{c}_{g}")], 1)
                b = fill(f"sa{c}")
                for g in range(2):
                    drained(pe, f"rhs{c}_{g}")
                    drained(pe, f"dt{c}_{LEVELS - 1}_{g}")
                    for j in range(4):
                        q = 4 * g + j
                        mm = T.matmul(b[:, q * 64:q * 64 + 64], XT[:, q, :], RHS[:, q, :], start=True, stop=True)
                mm.then_inc(psum_full[bank_of(f"sa{c}")], 1)
                drained(pe, f"sa{c}")
                for g in range(2):
                    r = slice(64 * g, 64 * g + 64)
                    b = fill(f"y{c}_{g}")
                    if c > 0:
                        for j in range(4):
                            T.matmul(b[r, j * P:(j + 1) * P], ST[r, j, :], AR[r, j, c, 1, :], start=(j == 0), stop=False,
                                     skip_group_check=True)
                    for j in range(4):
                        q, hd = 4 * g + j, 2 * j + g
                        T.matmul(b[r, j * P:(j + 1) * P], SA[:, q, :], MR[:, q, CH:], start=(c == 0), stop=False,
                                 skip_group_check=c > 0)
                        mm = T.matmul(b[r, j * P:(j + 1) * P], VTOK[:, hd * 64:hd * 64 + 64], NR[:, q, CH:], start=False,
                                      stop=True, skip_group_check=c > 0)
                    mm.then_inc(psum_full[bank_of(f"y{c}_{g}")], 1)
                if c < NC - 1:
                    b = fill(f"st{c}")
                    for g in range(2):
                        for j in range(4):
                            q, hd = 4 * g + j, 2 * j + g
                            o = b[64 * g:64 * g + 64, j * 64:j * 64 + 64]
                            T.matmul(o, BTOK[:, hd * 64:hd * 64 + 64], SA[:, q, :], start=True, stop=False)
                            mm = T.matmul(o, KTOK[:, hd * 64:hd * 64 + 64], VTOK[:, hd * 64:hd * 64 + 64], start=False, stop=True)
                    mm.then_inc(psum_full[bank_of(f"st{c}")], 1)
            for g in range(2):
                drained(pe, f"y{NC - 1}_{g}")
            for j in range(NJ):
                project(f"gm{j}", lambda k: BOM, lambda k: YT[:, j, :], 1)
            for j in range(NJ):
                pe.wait_ge(sem("y_sq"), j + 1)
                project(f"gv{j}", lambda k: BOM, lambda k: T1[:, j, :], 1)
            for hf in range(2):
                for name in ("ga", "gb"):
                    wait_weights(pe, f"{name}{hf}")
                    w = wbuf(f"{name}{hf}", ND, 512)
                    for j in range(4):
                        project(f"{name}{hf}_{j}", lambda k: w[:, k, j * P:(j + 1) * P], h, ND)
                wait_weights(pe, f"oo{hf}")
                w = wbuf(f"oo{hf}", 2, 4, 512)
                for j in range(4):
                    project(f"om{hf}_{j}", lambda k: w[:, 0, k, j * P:(j + 1) * P], lambda k: OT[:, k, :], NJ)
                pe.wait_ge(sem("rwkv_out"), 1)
                for j in range(4):
                    project(f"or{hf}_{j}", lambda k: w[:, 1, k, j * P:(j + 1) * P], lambda k: YT[:, k, :], NJ)
            for n in range(2):
                wait_weights(pe, f"wo{n}")
            pe.wait_ge(sem("mix"), 8)
            for i in range(NT):
                for n in range(2):
                    w = wbuf(f"wo{n}", ND, 512)
                    project(f"yo{i}_{n}", lambda k: MIX[:, k, i * P:(i + 1) * P], lambda k: w[:, k, :], ND)
            pe.wait_ge(sem("xn2"), 4)
            for j in range(ND):
                b = fill(f"hT{j}")
                for i in range(NT):
                    mm = T.transpose(b[:, i * P:(i + 1) * P], XN2[:, i, j * P:(j + 1) * P], IDENT)
                mm.then_inc(psum_full[bank_of(f"hT{j}")], 1)
            for j in range(ND):
                drained(pe, f"hT{j}")
            pe.wait_ge(sem("wr_landed"), 64)
            for i in range(NT):
                b = fill(f"lg{i}")
                for k in range(ND):
                    T.matmul(b[:, 0:36], HT[:, k, i * P:(i + 1) * P], WR[:, k, :], start=(k == 0), stop=False)
                mm = T.matmul(b[:, 0:36], ONES[0:1, :], BR[0:1, :], start=False, stop=True)
                mm.then_inc(psum_full[bank_of(f"lg{i}")], 1)
            with pe.Fori(0, NE // 2) as it:
                for s in range(2):
                    pe.wait_ge(sem(f"expert_landed{s}"), 48 * it + 48)
                    for m in range(12):
                        n = N0 + 12 * s + m
                        pe.wait_ge(psum_free[n % 8], BASE[n % 8] + 3 * it + MOE_SEQ(n))
                        b = ps[:, n % 8, :]
                        if m < 4:
                            w, t = EW[s][m // 2], m % 2
                            for k in range(ND):
                                mm = T.matmul(b, w[:, k, t * P:(t + 1) * P], HT[:, k, :], start=(k == 0), stop=(k == ND - 1))
                        else:
                            i, hf = (m - 4) // 2, (m - 4) % 2
                            if m == 4:
                                pe.wait_ge(sem("act_ready"), 4 * it + 2 * s + 2)
                            for k in range(2):
                                mm = T.matmul(b, ACTT[:, s, k, i * P:(i + 1) * P], EW[s][2][:, k, hf * 512:(hf + 1) * 512],
                                              start=(k == 0), stop=(k == 1))
                        mm.then_inc(psum_full[n % 8], 1)

        @block.scalar
        def _(act):
            step = [0]

            def link(ins):
                step[0] += 1
                ins.then_inc(sem("act_step"), 1)
                act.wait_ge(sem("act_step"), step[0])

            A = nc.scalar.activation
            for i in range(NT):
                if i == 0:
                    act.wait_ge(sem("x_landed"), 16)
                link(A(K[:, 0:2, :].rearrange("p a s -> p (a s)"), X[:, i, :], ACT.Square, accum_out=SS[:, i:i + 1]))
            nc.scalar.copy(SS[:, 0:4], SS[:, 0:4]).then_inc(sem("x_ss"), 1)
            act.wait_ge(sem("x_ss"), 1)
            act.wait_ge(sem("x_var"), 1)
            A(RSTD, SS, ACT.Sqrt).then_inc(sem("x_sqrt"), 1)
            act.wait_ge(sem("x_sqrt"), 1)
            drained(act, "par")
            A(SILC, par("c"), ACT.Silu).then_inc(sem("silc"), 1)
            act.wait_ge(sem("silc"), 1)
            drained(act, "ada3")
            for j in range(1, ND, 2):
                full(act, f"xT{j}")
                A(HT[:, j, :], bank(f"xT{j}"), ACT.Identity, bias=MODB1[:, j:j + 1], scale=MODA1[:, j:j + 1]).then_inc(psum_free[bank_of(f"xT{j}")], 1)
                drained(act, f"xT{j}")

            for k, t in enumerate((SIN, COS)):
                act.wait_ge(sem("angle"), k + 1)
                A(t, t, ACT.Sin).then_inc(sem("sincos"), 1)
                act.wait_ge(sem("sincos"), k + 1)

            def latent(name, tiles, dst, sq0, n):
                for t in range(tiles):
                    job = f"{name}{t}"
                    full(act, job)
                    link(nc.scalar.copy(dst[:, t, :], bank(job)))
                    A(SQ[:, sq0 + t, :], bank(job), ACT.Square).then_inc(psum_free[bank_of(job)], 1)
                    drained(act, job)
                act.wait_ge(sem("lat_var"), n)
                A(TR[:, n - 1, :], TR[:, n - 1, :], ACT.Sqrt).then_inc(sem("lat_sqrt"), 1)
                act.wait_ge(sem("lat_sqrt"), n)
            latent("cq", 3, CQ, 0, 1)
            latent("ckv", 2, CKV, 3, 2)
            for j in range(NZ):
                full(act, f"z{j}")
                if j >= 4:
                    act.wait_ge(sem("zs"), j - 3)
                nc.scalar.copy(RAW[:, j % 4, 1:], bank(f"z{j}")).then_inc(psum_free[bank_of(f"z{j}")], 1)
                drained(act, f"z{j}")
            act.wait_ge(sem("zs"), 13)
            A(ZS[0:64, 12, :], ZS[0:64, 12, :], ACT.Tanh).then_inc(sem("lowrank"), 1)
            act.wait_ge(sem("lowrank"), 1)
            act.wait_ge(sem("zs"), 14)
            A(ZS[:, 13, :], ZS[:, 13, :], ACT.Sigmoid).then_inc(sem("lowrank"), 1)
            act.wait_ge(sem("lowrank"), 2)
            for name, dst in (("qn", Q), ("kn", K)):
                for j in range(4):
                    full(act, f"{name}{j}")
                    b = bank(f"{name}{j}")
                    link(nc.scalar.copy(dst[0:64, 2 * j, :], b[0:64, :]))
                    nc.scalar.copy(dst[0:64, 2 * j + 1, :], b[64:128, :]).then_inc(psum_free[bank_of(f"{name}{j}")], 1)
                    drained(act, f"{name}{j}")
            for i in range(NT):
                full(act, f"v{i}")
                nc.scalar.copy(V[:, i, :], bank(f"v{i}")).then_inc(psum_free[bank_of(f"v{i}")], 1)
                drained(act, f"v{i}")
            for u in range(len(UNITS) + 2):
                if u < len(UNITS):
                    hd, q = UNITS[u]
                    job = f"s{hd}_{q}"
                    n = (q + 1) * P
                    act.wait_ge(sem("row_max"), u + 1)
                    if u >= 3:
                        full(act, "t%d_%d" % UNITS[u - 3])
                    A(PR[:, u % 3, 0:n], bank(job)[:, 0:n], ACT.Exp, bias=NMX[:, u:u + 1], scale=ATT_SCALE).then_inc(psum_free[bank_of(job)], 1)
                    drained(act, job)
                if u >= 2:
                    hd, q = UNITS[u - 2]
                    job = f"t{hd}_{q}"
                    full(act, job)
                    if q == 0 and hd >= 2:
                        full(act, f"o{hd - 2}")
                    nc.scalar.copy(PT[:, hd % 2, 0:q + 1, q * P:(q + 1) * P], bank(job)[:, 0:(q + 1) * P].rearrange("p (k t) -> p k t", t=P)).then_inc(psum_free[bank_of(job)], 1)
                    drained(act, job)
            for name, dst, vec in (("uw", SW, "decay_bias"), ("ua", AA, "a_bias")):
                for j in range(NJ):
                    job = f"{name}{j}"
                    full(act, job)
                    A(dst[:, j, :], bank(job), ACT.Sigmoid, bias=par(vec, j)).then_inc(psum_free[bank_of(job)], 1)
                    drained(act, job)
            for j in range(NJ):
                full(act, f"ug{j}")
                nc.scalar.copy(G[:, j, :], bank(f"ug{j}")).then_inc(psum_free[bank_of(f"ug{j}")], 1)
                drained(act, f"ug{j}")
            for j in range(NJ):
                act.wait_ge(sem("kk0"), j + 1)
                A(T1[:, j, :], KK[:, j, :], ACT.Square).then_inc(sem("kk_sq"), 1)
                act.wait_ge(sem("kk_sq"), j + 1)
            for j in range(NJ):
                full(act, f"kss{j}")
                A(T1[:, j, :], bank(f"kss{j}"), ACT.Sqrt).then_inc(psum_free[bank_of(f"kss{j}")], 1)
                drained(act, f"kss{j}")
            act.wait_ge(sem("decay"), 1)
            A(FDEC, FDEC, ACT.Exp, scale=DECAY).then_inc(sem("e_f"), 1)
            act.wait_ge(sem("e_f"), 1)
            act.wait_ge(sem("decay"), 2)
            A(SW, SW, ACT.Exp, scale=DECAY).then_inc(sem("e_a"), 1)
            act.wait_ge(sem("e_a"), 1)
            act.wait_ge(sem("kkn"), 1)
            A(T1, CUM, ACT.Exp, scale=DECAY).then_inc(sem("e_r"), 1)
            act.wait_ge(sem("e_r"), 1)
            act.wait_ge(sem("r_done"), 1)
            A(T1, CUM, ACT.Exp, scale=-DECAY).then_inc(sem("e_b"), 1)
            act.wait_ge(sem("e_b"), 1)

            for c in range(NC):
                for n in range(3):
                    full(act, f"tok{c}_{n}")
                    nc.scalar.copy(TOK[n], bank(f"tok{c}_{n}")).then_inc(psum_free[bank_of(f"tok{c}_{n}")], 1)
                    drained(act, f"tok{c}_{n}")
                for g in range(2):
                    full(act, f"x{c}_{g}")
                    nc.scalar.copy(XI[:, 4 * g:4 * g + 4].rearrange("p a b -> p (a b)"), bank(f"x{c}_{g}")).then_inc(psum_free[bank_of(f"x{c}_{g}")], 1)
                    drained(act, f"x{c}_{g}")
                for l in range(1, LEVELS):
                    for g in range(2):
                        job = f"p{c}_{l}_{g}"
                        full(act, job)
                        nc.scalar.copy(P1[:, 4 * g:4 * g + 4].rearrange("p a b -> p (a b)"), bank(job)).then_inc(psum_free[bank_of(job)], 1)
                        drained(act, job)
                for g in range(2):
                    job = f"rhs{c}_{g}"
                    full(act, job)
                    nc.scalar.copy(RHS[:, 4 * g:4 * g + 4].rearrange("p a b -> p (a b)"), bank(job)[:, 0:256]).then_inc(psum_free[bank_of(job)], 1)
                    drained(act, job)
                for g in range(2):
                    job = f"y{c}_{g}"
                    full(act, job)
                    r = slice(64 * g, 64 * g + 64)
                    nc.scalar.copy(YT[r, :, c * CH:(c + 1) * CH], bank(job)[r].rearrange("p (j t) -> p j t", t=CH)).then_inc(psum_free[bank_of(job)], 1)
                    drained(act, job)
            for j in range(NJ):
                act.wait_ge(sem("y_c"), j + 1)
                A(T1[:, j, :], YT[:, j, :], ACT.Square).then_inc(sem("y_sq"), 1)
                act.wait_ge(sem("y_sq"), j + 1)
            for j in range(NJ):
                act.wait_ge(sem("y_var"), j + 1)
                A(KK[:, j, :], KK[:, j, :], ACT.Sqrt).then_inc(sem("y_sqrt"), 1)
                act.wait_ge(sem("y_sqrt"), j + 1)
            act.wait_ge(sem("rwkv_out"), 1)
            for hf in range(2):
                for name, dst in (("ga", GA), ("gb", GB)):
                    for j in range(4):
                        job = f"{name}{hf}_{j}"
                        full(act, job)
                        if hf:
                            act.wait_ge(sem("mix"), j + 1)
                        A(dst[:, j, :], bank(job), ACT.Sigmoid).then_inc(psum_free[bank_of(job)], 1)
                        drained(act, job)
            for i in range(NT):
                for n in range(2):
                    job = f"yo{i}_{n}"
                    full(act, job)
                    link(A(JUNK[:, n * 512:(n + 1) * 512], bank(job), ACT.Square, accum_out=SSY[:, 2 * i + n:2 * i + n + 1]))
                nc.scalar.copy(SS4[:, i:i + 1], SSY[:, 2 * i:2 * i + 1]).then_inc(sem("y_ss"), 1)
                act.wait_ge(sem("y_ss"), i + 1)
                act.wait_ge(sem("yo_var"), i + 1)
                A(SS4[:, i:i + 1], SS4[:, i:i + 1], ACT.Sqrt).then_inc(sem("yo_sqrt"), 1)
                act.wait_ge(sem("yo_sqrt"), i + 1)
            for i in range(NT):
                act.wait_ge(sem("x1"), i + 1)
                link(A(JUNK, X[:, i, :], ACT.Square, accum_out=SS2[:, i:i + 1]))
                nc.scalar.copy(SS2[:, i:i + 1], SS2[:, i:i + 1]).then_inc(sem("x1_ss"), 1)
                act.wait_ge(sem("x1_ss"), i + 1)
                act.wait_ge(sem("x1_var"), i + 1)
                A(RS2[:, i:i + 1], SS2[:, i:i + 1], ACT.Sqrt).then_inc(sem("x1_sqrt"), 1)
                act.wait_ge(sem("x1_sqrt"), i + 1)
            for j in range(1, ND, 2):
                full(act, f"hT{j}")
                A(HT[:, j, :], bank(f"hT{j}"), ACT.Identity, bias=MODB2[:, j:j + 1], scale=MODA2[:, j:j + 1]).then_inc(psum_free[bank_of(f"hT{j}")], 1)
                drained(act, f"hT{j}")
            act.wait_ge(sem("gmax"), 1)
            A(GEXP, GEXP, ACT.Exp).then_inc(sem("gexp"), 1)
            act.wait_ge(sem("gexp"), 1)
            act.wait_ge(sem("emax"), 1)
            A(E21, E21, ACT.Exp).then_inc(sem("eexp"), 1)
            act.wait_ge(sem("eexp"), 1)
            with act.Fori(0, NE // 2) as it:
                for s in range(2):
                    for m in range(2):
                        n = N0 + 12 * s + m
                        act.wait_ge(psum_full[n % 8], BASE[n % 8] + 3 * it + MOE_SEQ(n) + 1)
                        A(SIL[:, s, m, :], ps[:, n % 8, :], ACT.Silu).then_inc(psum_free[n % 8], 1)
            act.wait_ge(sem("y_fin"), 1)
            for i in range(NT):
                link(A(JUNK, YACC[:, i, :], ACT.Square, accum_out=SS[:, i:i + 1]))
            nc.scalar.copy(SS, SS).then_inc(sem("fin_ss"), 1)
            act.wait_ge(sem("fin_ss"), 1)
            act.wait_ge(sem("fin_var"), 1)
            A(SS, SS, ACT.Sqrt).then_inc(sem("fin_sqrt"), 1)
            act.wait_ge(sem("fin_sqrt"), 1)

        @block.vector
        def _(dve):
            step = [0]

            def link(ins):
                step[0] += 1
                ins.then_inc(sem("dve_step"), 1)
                dve.wait_ge(sem("dve_step"), step[0])

            v = nc.vector
            dve.wait_ge(sem("iota"), 2)
            link(v.tensor_tensor(IDXX, IDXP, IDXF, ALU.bitwise_xor))
            link(v.tensor_copy(XU, IDXX))
            link(v.tensor_scalar(IDENT, XU, 0.5, None, ALU.is_lt))
            link(v.tensor_scalar(BO, XU, 63.5, None, ALU.is_lt))
            link(v.tensor_scalar(BOM, BO, 1.0 / 64, None, ALU.mult))
            link(v.tensor_tensor(MASK2[:, 0, :], IDXF, IDXP, ALU.is_gt))
            link(v.tensor_tensor(MASK2[:, 1, :], IDXF, IDXP, ALU.is_ge))
            link(v.tensor_tensor(XU, XU, MASK2[:, 0, :], ALU.mult))
            for l in range(LEVELS):
                link(v.tensor_scalar(MASKS[:, l, :], XU, 2 ** l - 0.5, None, ALU.is_gt))
                link(v.tensor_scalar(TR[:, 0, 0:P], XU, 2 ** (l + 1) - 0.5, None, ALU.is_gt))
                link(v.tensor_tensor(MASKS[:, l, :], MASKS[:, l, :], TR[:, 0, 0:P], ALU.subtract))
            link(v.tensor_scalar(IDXX[:, 0:1], IDXP[:, 0:1], 16, None, ALU.bitwise_and))
            link(v.tensor_copy(SIGN, IDXX[:, 0:1]))
            v.tensor_scalar(SIGN, SIGN, 0.125, -1.0, ALU.mult, ALU.add).then_inc(sem("masks"), 1)
            dve.wait_ge(sem("masks"), 1)
            full(dve, "par")
            v.tensor_copy(PAR[:, 0:NROWS], bank("par")[:, 0:NROWS]).then_inc(psum_free[bank_of("par")], 1)
            drained(dve, "par")
            dve.wait_ge(sem("x_ss"), 1)
            v.tensor_scalar(SS, SS, 1.0 / D, RMS_EPS, ALU.mult, ALU.add).then_inc(sem("x_var"), 1)
            dve.wait_ge(sem("x_var"), 1)
            dve.wait_ge(sem("x_sqrt"), 1)
            link(v.reciprocal(RSTD, RSTD))
            for i in range(NT):
                ins = v.tensor_scalar(X[:, i, :], X[:, i, :], RSTD[:, i:i + 1], None, ALU.mult)
                if i < NT - 1:
                    link(ins)
                else:
                    ins.then_inc(sem("xn"), 1)
                    dve.wait_ge(sem("xn"), 1)
            link(v.tensor_scalar(OMKA, par("k_a"), -1.0, 1.0, ALU.mult, ALU.add))
            dve.wait_ge(sem("silc"), 1)

            def ada_products(c):
                wait_weights(dve, f"ada{c}")
                if c >= 2:
                    full(dve, f"ada{c - 2}")
                w, a = wbuf(f"ada{c}", ND, 512), ACC[:, c % 2, :]
                link(v.tensor_scalar(a, w[:, 0, :], SILC[:, 0:1], None, ALU.mult))
                for k in range(1, ND):
                    ins = v.scalar_tensor_tensor(a, w[:, k, :], SILC[:, k:k + 1], a, ALU.mult, ALU.add)
                    if k < ND - 1:
                        link(ins)
                    else:
                        ins.then_inc(sem("ada_ready"), 1)
                        dve.wait_ge(sem("ada_ready"), c + 1)

            def ada_take(c):
                job = f"ada{c}"
                full(dve, job)
                hf = c % 2
                b = bank(job)
                bias = par("b_ada")[:, 4 * c:4 * c + 4]
                s = slice(4 * hf, 4 * hf + 4)
                kind = c // 2
                if kind in (0, 3):
                    v.tensor_tensor((MODB1 if kind == 0 else MODB2)[:, s], b[:, 0:4], bias, ALU.add).then_inc(psum_free[bank_of(job)], 1)
                    drained(dve, job)
                elif kind in (1, 4):
                    m, gv = (MODA1, par("g_pre_mix")) if kind == 1 else (MODA2, par("g_pre_ffn"))
                    link(v.tensor_tensor(m[:, s], b[:, 0:4], bias, ALU.add))
                    v.scalar_tensor_tensor(m[:, s], m[:, s], 1.0, gv[:, s], ALU.add, ALU.mult).then_inc(psum_free[bank_of(job)], 1)
                    drained(dve, job)
                else:
                    dve.wait_ge(sem("grow_landed"), 32)
                    gr = GROW[:, 0 if kind == 2 else 1, hf * 512:(hf + 1) * 512]
                    v.tensor_tensor(gr, b, gr, ALU.mult).then_inc(psum_free[bank_of(job)], 1)
                    drained(dve, job)

            for c in range(4):
                ada_products(c)
                ada_take(c)
            for j in range(0, ND, 2):
                full(dve, f"xT{j}")
                v.tensor_scalar(HT[:, j, :], bank(f"xT{j}"), MODA1[:, j:j + 1], MODB1[:, j:j + 1], ALU.mult, ALU.add).then_inc(psum_free[bank_of(f"xT{j}")], 1)
                drained(dve, f"xT{j}")
            dve.wait_ge(sem("pos_landed"), 16)
            ang, n, t = TR[:, 2, :], TR[:, 3, :], TR[:, 4, :]
            link(v.tensor_copy(ang, POSI))
            link(v.tensor_scalar(ang, ang, par("inv_freq"), None, ALU.mult))
            for k, dst in enumerate((SIN, COS)):
                link(v.tensor_scalar(n, ang, 1.0 / TWO_PI, 0.25 * k, ALU.mult, ALU.add))
                link(v.tensor_scalar(n, n, ROUND, None, ALU.add))
                link(v.tensor_scalar(n, n, ROUND, None, ALU.subtract))
                link(v.scalar_tensor_tensor(t, n, -TP1, ang, ALU.mult, ALU.add))
                link(v.scalar_tensor_tensor(t, n, -TP2, t, ALU.mult, ALU.add))
                link(v.scalar_tensor_tensor(t, n, -TP3, t, ALU.mult, ALU.add))
                link(v.tensor_scalar(t, t, 0.5 * math.pi * k, math.pi, ALU.add, ALU.min))
                v.tensor_scalar(dst, t, -3.1415925, None, ALU.max).then_inc(sem("angle"), 1)
                dve.wait_ge(sem("angle"), k + 1)
            dve.wait_ge(sem("sincos"), 2)
            link(v.tensor_scalar(SIN, SIN, SIGN, None, ALU.mult))

            def latent(job, n, dst, tiles, width, vec, name):
                full(dve, job)
                t = TR[:, n - 1, :]
                v.tensor_scalar(t, bank(job), 1.0 / width, RMS_EPS, ALU.mult, ALU.add).then_inc(psum_free[bank_of(job)], 1)
                drained(dve, job)
                ins = v.tensor_copy(t[:, 0:1], t[:, 0:1])
                ins.then_inc(sem("lat_var"), 1)
                dve.wait_ge(sem("lat_var"), n)
                dve.wait_ge(sem("lat_sqrt"), n)
                link(v.reciprocal(t, t))
                for k in range(tiles):
                    ins = v.scalar_tensor_tensor(dst[:, k, :], dst[:, k, :], par(vec, k), t, ALU.mult, ALU.mult)
                    if k < tiles - 1:
                        link(ins)
                    else:
                        ins.then_inc(sem(name), 1)
                        dve.wait_ge(sem(name), 1)
            latent("cqss", 1, CQ, 3, QR, "g_cq", "cqn")
            latent("ckvss", 2, CKV, 2, KVR, "g_ckv", "ckvn")
            full(dve, "kr")
            v.tensor_tensor(TR[64:96, 2, :], bank("kr")[64:96], COS[64:96], ALU.mult).then_inc(psum_free[bank_of("kr")], 1)
            drained(dve, "kr")
            full(dve, "krs")
            v.tensor_tensor(TR[64:96, 3, :], bank("krs")[64:96], SIN[64:96], ALU.mult).then_inc(psum_free[bank_of("krs")], 1)
            drained(dve, "krs")
            v.tensor_tensor(K[64:96, 0, :], TR[64:96, 2, :], TR[64:96, 3, :], ALU.add).then_inc(sem("k_rope0"), 1)
            dve.wait_ge(sem("k_rope0"), 1)
            ada_products(4)
            ada_take(4)

            def shift(j):
                drained(dve, f"z{j}")
                raw = RAW[:, j % 4, :]
                link(v.tensor_tensor(ZS[:, j, :], raw[:, 0:S], raw[:, 1:], ALU.subtract))
                v.scalar_tensor_tensor(ZS[:, j, :], ZS[:, j, :], par("mu_shift", j), raw[:, 1:], ALU.mult, ALU.add).then_inc(sem("zs"), 1)
                dve.wait_ge(sem("zs"), j + 1)
            for n in range(3):
                for j in range(4 * n, 4 * n + 4):
                    shift(j)
                ada_products(5 + n)
                ada_take(5 + n)
            shift(12)
            shift(13)
            for t in range(2):
                full(dve, f"qr{t}")
                v.tensor_tensor(TR[:, 2, :], bank(f"qr{t}"), COS, ALU.mult).then_inc(psum_free[bank_of(f"qr{t}")], 1)
                drained(dve, f"qr{t}")
                full(dve, f"qs{t}")
                v.tensor_tensor(TR[:, 3, :], bank(f"qs{t}"), SIN, ALU.mult).then_inc(psum_free[bank_of(f"qs{t}")], 1)
                drained(dve, f"qs{t}")
                for j in range(4):
                    r = slice(32 * j, 32 * j + 32)
                    v.tensor_tensor(Q[64:96, 4 * t + j, :], TR[r, 2, :], TR[r, 3, :], ALU.add).then_inc(sem("q_rope"), 1)
                    dve.wait_ge(sem("q_rope"), 4 * t + j + 1)
            for c in range(8, 12):
                ada_products(c)
                ada_take(c)
            for u in range(len(UNITS) + 2):
                if u < len(UNITS):
                    hd, q = UNITS[u]
                    full(dve, f"s{hd}_{q}")
                    link(v.tensor_reduce(MX[:, u:u + 1], bank(f"s{hd}_{q}")[:, 0:(q + 1) * P], AX.X, ALU.max))
                    v.tensor_scalar(NMX[:, u:u + 1], MX[:, u:u + 1], -ATT_SCALE, None, ALU.mult).then_inc(sem("row_max"), 1)
                    dve.wait_ge(sem("row_max"), u + 1)
                if 1 <= u <= len(UNITS):
                    w = u - 1
                    hd, q = UNITS[w]
                    drained(dve, f"s{hd}_{q}")
                    p = PR[:, w % 3, 0:(q + 1) * P]
                    link(v.tensor_reduce(RSUM[:, w:w + 1], p, AX.X, ALU.add))
                    link(v.reciprocal(RINV[:, w:w + 1], RSUM[:, w:w + 1]))
                    v.tensor_scalar(p, p, RINV[:, w:w + 1], None, ALU.mult).then_inc(sem("p_ready"), 1)
                    dve.wait_ge(sem("p_ready"), w + 1)
                if u >= 2:
                    hd, q = UNITS[u - 2]
                    if q == NT - 1:
                        full(dve, f"o{hd}")
                        r = slice(64 * (hd % 2), 64 * (hd % 2) + 64)
                        v.tensor_copy(OT[r, hd // 2, :], bank(f"o{hd}")[r]).then_inc(psum_free[bank_of(f"o{hd}")], 1)
                        drained(dve, f"o{hd}")
            for j in range(NJ):
                if j == 0:
                    drained(dve, f"t{HEADS - 1}_{NT - 1}")
                v.tensor_scalar(KK[:, j, :], KZ[:, j, :], par("k_k", j), None, ALU.mult).then_inc(sem("kk0"), 1)
                dve.wait_ge(sem("kk0"), j + 1)
            full(dve, "uw0")
            link(v.memset(RESET, 1.0))
            link(v.memset(RESET.rearrange("p j (c t) -> p (j c) t", t=CH)[:, :, 0:1], 0.0))
            for j in range(NJ):
                drained(dve, f"uw{j}")
                drained(dve, f"ua{j}")
            link(v.tensor_tensor_scan(CUM.rearrange("p j s -> p (j s)"), RESET.rearrange("p j s -> p (j s)"),
                                     SW.rearrange("p j s -> p (j s)"), 0.0, ALU.mult, ALU.add))
            cum = CUM.rearrange("p j (c t) -> p (j c) t", t=CH)
            mid = MID.rearrange("p j c -> p (j c)")
            link(v.tensor_copy(mid.unsqueeze(2), cum[:, :, CH // 2:CH // 2 + 1]))
            link(v.tensor_tensor(cum, cum, mid.unsqueeze(2).to_broadcast([P, NJ * NC, CH]), ALU.subtract))
            link(v.tensor_copy(FDEC.rearrange("p j c -> p (j c)").unsqueeze(2), cum[:, :, CH - 1:CH]))
            v.tensor_tensor(FDEC[:, :, 0:NC - 1], FDEC[:, :, 0:NC - 1], MID[:, :, 1:NC], ALU.add).then_inc(sem("decay"), 1)
            dve.wait_ge(sem("decay"), 1)
            v.tensor_tensor(SW, CUM, SW, ALU.subtract).then_inc(sem("decay"), 1)
            dve.wait_ge(sem("decay"), 2)
            for j in range(NJ):
                drained(dve, f"kss{j}")
                link(v.tensor_scalar(T1[:, j, :], T1[:, j, :], 1e-12, None, ALU.max))
                link(v.reciprocal(T1[:, j, :], T1[:, j, :]))
                ins = v.tensor_tensor(KK[:, j, :], KK[:, j, :], T1[:, j, :], ALU.mult)
                if j < NJ - 1:
                    link(ins)
                else:
                    ins.then_inc(sem("kkn"), 1)
                    dve.wait_ge(sem("kkn"), 1)
            a4 = AR.rearrange("p j c a t -> p (j c) a t")
            fold = lambda x: x.rearrange("p j (c t) -> p (j c) t", t=CH)
            dve.wait_ge(sem("e_a"), 1)
            link(v.scalar_tensor_tensor(a4[:, :, 0, :], fold(KK), -1.0, fold(SW), ALU.mult, ALU.mult))
            link(v.tensor_tensor(KK, KK, AA, ALU.mult))
            dve.wait_ge(sem("e_r"), 1)
            v.tensor_tensor(a4[:, :, 1, :], fold(RZ), fold(T1), ALU.mult).then_inc(sem("r_done"), 1)
            dve.wait_ge(sem("r_done"), 1)
            for j in range(NJ):
                link(v.tensor_scalar(AA[:, j, :], AA[:, j, :], par("k_a", j), OMKA[:, j:j + 1], ALU.mult, ALU.add))
                link(v.tensor_tensor(KZ[:, j, :], KZ[:, j, :], AA[:, j, :], ALU.mult))
                v.scalar_tensor_tensor(RZ[:, j, :], RZ[:, j, :], par("r_k", j), KZ[:, j, :], ALU.mult, ALU.mult).then_inc(sem("rk"), 1)
                dve.wait_ge(sem("rk"), j + 1)
            dve.wait_ge(sem("e_b"), 1)
            link(v.tensor_tensor(BT, KK, T1, ALU.mult))
            link(v.tensor_tensor(KT, KZ, T1, ALU.mult))
            for j in range(NJ):
                full(dve, f"bon{j}")
                v.tensor_tensor(BONUS[:, j, :], bank(f"bon{j}"), VZ[:, j, :], ALU.mult).then_inc(psum_free[bank_of(f"bon{j}")], 1)
                drained(dve, f"bon{j}")
            dve.wait_ge(sem("e_f"), 1)
            for j in range(NJ):
                drained(dve, f"ug{j}")
            v.tensor_copy(MX[:, 0:1], MX[:, 0:1]).then_inc(sem("rwkv_in"), 1)
            dve.wait_ge(sem("rwkv_in"), 1)
            for c in range(NC):
                for g in range(2):
                    for name, dst in (("mr", MR), ("nr", NR)):
                        for n in range(2):
                            job = f"{name}{c}_{g}_{n}"
                            full(dve, job)
                            q = 4 * g + 2 * n
                            v.tensor_tensor(dst[:, q:q + 2, :], bank(job).rearrange("p (h t) -> p h t", h=2), MASK2.rearrange("p a t -> p (a t)").unsqueeze(1).to_broadcast([P, 2, 2 * CH]), ALU.mult).then_inc(psum_free[bank_of(job)], 1)
                            drained(dve, job)
                for l in range(1, LEVELS):
                    for name, dst in (("dx", XI), ("dt", XT)):
                        if name == "dx" and l == LEVELS - 1:
                            continue
                        for g in range(2):
                            job = f"{name}{c}_{l}_{g}"
                            full(dve, job)
                            d = dst[:, 4 * g:4 * g + 4, :].rearrange("p a b -> p (a b)")
                            v.tensor_tensor(d, bank(job), d, ALU.add).then_inc(psum_free[bank_of(job)], 1)
                            drained(dve, job)
                full(dve, f"sa{c}")
                v.tensor_copy(SA.rearrange("p a b -> p (a b)"), bank(f"sa{c}")).then_inc(psum_free[bank_of(f"sa{c}")], 1)
                drained(dve, f"sa{c}")
                if c < NC - 1:
                    job = f"st{c}"
                    full(dve, job)
                    b = bank(job)[:, 0:NJ * VD].rearrange("p (j v) -> p j v", v=VD)
                    f = FDEC[:, :, c:c + 1].to_broadcast([P, NJ, VD])
                    if c == 0:
                        v.tensor_tensor(ST, b, f, ALU.mult).then_inc(psum_free[bank_of(job)], 1)
                        drained(dve, job)
                    else:
                        link(v.tensor_tensor(ST, b, ST, ALU.add))
                        v.tensor_tensor(ST, ST, f, ALU.mult).then_inc(psum_free[bank_of(job)], 1)
                        drained(dve, job)
            for j in range(NJ):
                full(dve, f"gm{j}")
                v.tensor_tensor(YT[:, j, :], YT[:, j, :], bank(f"gm{j}"), ALU.subtract).then_inc(psum_free[bank_of(f"gm{j}")], 1)
                drained(dve, f"gm{j}")
                v.tensor_copy(MX[:, 1:2], MX[:, 1:2]).then_inc(sem("y_c"), 1)
                dve.wait_ge(sem("y_c"), j + 1)
            for j in range(NJ):
                full(dve, f"gv{j}")
                v.tensor_scalar(KK[:, j, :], bank(f"gv{j}"), GN_EPS, None, ALU.add).then_inc(psum_free[bank_of(f"gv{j}")], 1)
                drained(dve, f"gv{j}")
                v.tensor_copy(MX[:, 1:2], MX[:, 1:2]).then_inc(sem("y_var"), 1)
                dve.wait_ge(sem("y_var"), j + 1)
            for j in range(NJ):
                dve.wait_ge(sem("y_sqrt"), j + 1)
                link(v.reciprocal(KK[:, j, :], KK[:, j, :]))
                link(v.tensor_tensor(YT[:, j, :], YT[:, j, :], KK[:, j, :], ALU.mult))
                link(v.tensor_scalar(YT[:, j, :], YT[:, j, :], par("lnx_w", j), par("lnx_b", j), ALU.mult, ALU.add))
                link(v.tensor_tensor(YT[:, j, :], YT[:, j, :], BONUS[:, j, :], ALU.add))
                ins = v.tensor_tensor(YT[:, j, :], YT[:, j, :], G[:, j, :], ALU.mult)
                if j < NJ - 1:
                    link(ins)
                else:
                    ins.then_inc(sem("rwkv_out"), 1)
                    dve.wait_ge(sem("rwkv_out"), 1)
            for hf in range(2):
                for j in range(4):
                    job = f"om{hf}_{j}"
                    full(dve, job)
                    drained(dve, f"gb{hf}_{j}")
                    v.tensor_tensor(GA[:, j, :], bank(job), GA[:, j, :], ALU.mult).then_inc(psum_free[bank_of(job)], 1)
                    drained(dve, job)
                for j in range(4):
                    job = f"or{hf}_{j}"
                    full(dve, job)
                    v.tensor_tensor(GB[:, j, :], bank(job), GB[:, j, :], ALU.mult).then_inc(psum_free[bank_of(job)], 1)
                    drained(dve, job)
                    v.tensor_tensor(MIX[:, 4 * hf + j, :], GA[:, j, :], GB[:, j, :], ALU.add).then_inc(sem("mix"), 1)
                    dve.wait_ge(sem("mix"), 4 * hf + j + 1)
            dve.wait_ge(sem("x_landed"), 32)
            for i in range(NT):
                dve.wait_ge(sem("y_ss"), i + 1)
                link(v.tensor_tensor(SS4[:, i:i + 1], SSY[:, 2 * i:2 * i + 1], SSY[:, 2 * i + 1:2 * i + 2], ALU.add))
                v.tensor_scalar(SS4[:, i:i + 1], SS4[:, i:i + 1], 1.0 / D, RMS_EPS, ALU.mult, ALU.add).then_inc(sem("yo_var"), 1)
                dve.wait_ge(sem("yo_var"), i + 1)
                dve.wait_ge(sem("yo_sqrt"), i + 1)
                link(v.reciprocal(SS4[:, i:i + 1], SS4[:, i:i + 1]))
                for n in range(2):
                    job = f"yo{i}_{n}"
                    xs = X[:, i, n * 512:(n + 1) * 512]
                    v.scalar_tensor_tensor(TUP, bank(job), SS4[:, i:i + 1], GROW[:, 0, n * 512:(n + 1) * 512], ALU.mult, ALU.mult).then_inc(psum_free[bank_of(job)], 1)
                    drained(dve, job)
                    ins = v.tensor_tensor(xs, xs, TUP, ALU.add)
                    if n == 0:
                        link(ins)
                    else:
                        ins.then_inc(sem("x1"), 1)
                        dve.wait_ge(sem("x1"), i + 1)
            for i in range(NT):
                dve.wait_ge(sem("x1_ss"), i + 1)
                v.tensor_scalar(SS2[:, i:i + 1], SS2[:, i:i + 1], 1.0 / D, RMS_EPS, ALU.mult, ALU.add).then_inc(sem("x1_var"), 1)
                dve.wait_ge(sem("x1_var"), i + 1)
                dve.wait_ge(sem("x1_sqrt"), i + 1)
                link(v.reciprocal(RS2[:, i:i + 1], RS2[:, i:i + 1]))
                v.tensor_scalar(XN2[:, i, :], X[:, i, :], RS2[:, i:i + 1], None, ALU.mult).then_inc(sem("xn2"), 1)
                dve.wait_ge(sem("xn2"), i + 1)
            for j in range(0, ND, 2):
                full(dve, f"hT{j}")
                v.tensor_scalar(HT[:, j, :], bank(f"hT{j}"), MODA2[:, j:j + 1], MODB2[:, j:j + 1], ALU.mult, ALU.add).then_inc(psum_free[bank_of(f"hT{j}")], 1)
                drained(dve, f"hT{j}")
            for i in range(NT):
                full(dve, f"lg{i}")
                v.tensor_copy(LOGITS[:, i, :], bank(f"lg{i}")[:, 0:36]).then_inc(psum_free[bank_of(f"lg{i}")], 1)
                drained(dve, f"lg{i}")
            gl, el = LOGITS[:, :, 0:NG], LOGITS[:, :, NG:].rearrange("p i (g e) -> p i g e", e=EG)

            def first_max(vals, n, mx, hot):
                link(v.tensor_reduce(mx, vals, AX.X, ALU.max))
                link(v.tensor_tensor(hot, vals, mx.unsqueeze(2).to_broadcast([P, NT, n]), ALU.is_equal))
                link(v.tensor_tensor(hot, hot, RANKW[:, 8 - n:8].unsqueeze(1).to_broadcast([P, NT, n]), ALU.mult))
                link(v.tensor_reduce(TMX, hot, AX.X, ALU.max))
                link(v.tensor_tensor(hot, hot, TMX.unsqueeze(2).to_broadcast([P, NT, n]), ALU.is_equal))
            for n in range(8):
                link(v.memset(RANKW[:, n:n + 1], float(8 - n)))
            first_max(gl, NG, GMX, GHOT)
            v.tensor_tensor(GEXP, gl, GMX.unsqueeze(2).to_broadcast([P, NT, NG]), ALU.subtract).then_inc(sem("gmax"), 1)
            dve.wait_ge(sem("gmax"), 1)
            dve.wait_ge(sem("gexp"), 1)
            link(v.tensor_reduce(PSEL, GEXP, AX.X, ALU.add))
            link(v.reciprocal(PSEL, PSEL))
            for g in range(NG):
                hot = GHOT[:, :, g:g + 1].to_broadcast([P, NT, EG])
                if g == 0:
                    link(v.tensor_tensor(EIN, el[:, :, g, :], hot, ALU.mult))
                else:
                    link(v.tensor_tensor(ETMP, el[:, :, g, :], hot, ALU.mult))
                    link(v.tensor_tensor(EIN, EIN, ETMP, ALU.add))
            first_max(EIN, EG, EMX1, HOT1)
            link(v.scalar_tensor_tensor(ETMP, HOT1, NEG, EIN, ALU.mult, ALU.add))
            first_max(ETMP, EG, EMX2, HOT2)
            v.tensor_tensor(E21, EMX2, EMX1, ALU.subtract).then_inc(sem("emax"), 1)
            dve.wait_ge(sem("emax"), 1)
            dve.wait_ge(sem("eexp"), 1)
            link(v.tensor_scalar(W1, E21, 1.0, None, ALU.add))
            link(v.reciprocal(W1, W1))
            link(v.tensor_tensor(W1, W1, PSEL, ALU.mult))
            link(v.tensor_tensor(E21, E21, W1, ALU.mult))
            link(v.tensor_tensor(HOT1, HOT1, W1.unsqueeze(2).to_broadcast([P, NT, EG]), ALU.mult))
            link(v.tensor_tensor(HOT2, HOT2, E21.unsqueeze(2).to_broadcast([P, NT, EG]), ALU.mult))
            link(v.tensor_tensor(HOT1, HOT1, HOT2, ALU.add))
            for g in range(NG):
                link(v.tensor_tensor(COMB[:, :, g * EG:(g + 1) * EG], HOT1, GHOT[:, :, g:g + 1].to_broadcast([P, NT, EG]), ALU.mult))
            link(v.memset(YACC, 0.0))
            with dve.Fori(0, NE // 2) as it:
                for s in range(2):
                    cb = CB[:, s]
                    v.tensor_copy(cb, COMB[:, :, bass.ds(it * 2 + s, 1)].rearrange("p i o -> p (i o)")).then_inc(sem("comb_step"), 1)
                    for m in range(2, 12):
                        n = N0 + 12 * s + m
                        dve.wait_ge(psum_full[n % 8], BASE[n % 8] + 3 * it + MOE_SEQ(n) + 1)
                        b = ps[:, n % 8, :]
                        if m < 4:
                            g = n - 2
                            dve.wait_ge(psum_free[g % 8], BASE[g % 8] + 3 * it + MOE_SEQ(g) + 1)
                            v.tensor_tensor(ACTT[:, s, m - 2, :], b, SIL[:, s, m - 2, :], ALU.mult).then_inc(sem("act_ready"), 1)
                            dve.wait_ge(sem("act_ready"), 4 * it + 2 * s + m - 1)
                            v.tensor_copy(DUM, DUM).then_inc(psum_free[n % 8], 1)
                        else:
                            i, hf = (m - 4) // 2, (m - 4) % 2
                            y = YACC[:, i, hf * 512:(hf + 1) * 512]
                            if m == 4:
                                dve.wait_ge(sem("comb_step"), 2 * it + s + 1)
                            v.scalar_tensor_tensor(y, b, cb[:, i:i + 1], y, ALU.mult, ALU.add).then_inc(psum_free[n % 8], 1)
            v.tensor_copy(DUM, DUM).then_inc(sem("y_fin"), 1)
            dve.wait_ge(sem("y_fin"), 1)
            dve.wait_ge(sem("fin_ss"), 1)
            v.tensor_scalar(SS, SS, 1.0 / D, RMS_EPS, ALU.mult, ALU.add).then_inc(sem("fin_var"), 1)
            dve.wait_ge(sem("fin_var"), 1)
            dve.wait_ge(sem("fin_sqrt"), 1)
            link(v.reciprocal(SS, SS))
            for i in range(NT):
                link(v.scalar_tensor_tensor(YACC[:, i, :], YACC[:, i, :], SS[:, i:i + 1], GROW[:, 1, :], ALU.mult, ALU.mult))
                v.tensor_tensor(X[:, i, :], X[:, i, :], YACC[:, i, :], ALU.add).then_inc(sem("out_ready"), 1)
                dve.wait_ge(sem("out_ready"), i + 1)


_INS = ['x', 'c', 'positions', 'w_ada', 'b_ada', 'g_pre_mix', 'g_post_mix', 'g_pre_ffn', 'g_post_ffn',
        'w_in', 'g_cq', 'w_uq', 'g_ckv', 'w_ukv', 'w_o_mla', 'mu_shift', 'w_decay_up', 'decay_bias',
        'w_a_up', 'a_bias', 'w_g_up', 'k_k', 'k_a', 'r_k', 'lnx_w', 'lnx_b', 'w_o_rwkv', 'w_out',
        'w_router_group', 'b_router_group', 'w_router_expert', 'b_router_expert',
        'w_exp_gate', 'w_exp_up', 'w_exp_down']


def kernel(**inputs):
    import numpy as _np
    import concourse.bacc as _bacc
    from concourse import mybir as _mybir
    from concourse.bass_utils import run_bass_kernel_spmd as _run

    nc = _bacc.Bacc("TRN2", target_bir_lowering=False, num_devices=1)
    arrays, aps = {}, {}
    for name in _INS:
        a = _np.ascontiguousarray(inputs[name])
        arrays[f"in_{name}"] = a
        aps[name] = nc.dram_tensor(f"in_{name}", a.shape, _mybir.dt.from_np(a.dtype), kind="ExternalInput").ap()
    freq = _np.tile((ROPE_THETA ** (-_np.arange(0, ROPE, 2) / ROPE)).astype(_np.float32), 128 // (ROPE // 2))[None, :]
    arrays["rope_inv_freq"] = freq
    aps["inv_freq"] = nc.dram_tensor("rope_inv_freq", freq.shape, _mybir.dt.float32, kind="ExternalInput").ap()
    out = nc.dram_tensor("out_0", (1, S, D), _mybir.dt.float32, kind="ExternalOutput").ap()
    layer(nc, aps, out)
    r = _run(nc, [arrays], core_ids=[0])
    return r.results[0]["out_0"]
```

```python
import math
from contextlib import ExitStack

import numpy as np

import concourse.bass as bass
from concourse import mybir

F32 = mybir.dt.float32
I32 = mybir.dt.int32
U32 = mybir.dt.uint32
ALU = mybir.AluOpType
ACT = mybir.ActivationFunctionType
AX = mybir.AxisListType

P = 128
S = 512
D = 1024
NT = S // P
ND = D // P
HEADS = 8
NOPE, ROPE, VD = 64, 32, 64
QR, KVR = 384, 256
RW = 512
NJ = RW // P
ZR = 3 * RW + 64 + 64 + 128
NZ = ZR // P
C_CKV, C_KR, C_ZR = QR, QR + KVR, QR + KVR + ROPE
C_GATE = C_ZR + ZR
NE, NG, EG, FF = 32, 4, 8, 256
ATT_SCALE = 1.0 / math.sqrt(NOPE + ROPE)
RMS_EPS, GN_EPS = 1e-6, 64e-5
DECAY = -math.exp(-0.5)
CH = 128
NC = S // CH
LEVELS = 7
LAG = 3
CAP = 128
XBLK = (2 * S - 1) // CAP
NBLK = NE + XBLK
FAR = 1 << 20
NEG = -1e30
ROPE_THETA = 10000.0
ROUND = 1.5 * 2.0 ** 23
TWO_PI = 2 * math.pi

ROWS = {}
_at = 0
for _n, _k in (("b_ada", 48), ("g_pre_mix", 8), ("g_pre_ffn", 8), ("c", 8), ("g_cq", 3), ("g_ckv", 2),
               ("mu_shift", 14), ("decay_bias", 4), ("a_bias", 4), ("k_k", 4), ("k_a", 4), ("r_k", 4),
               ("lnx_w", 4), ("lnx_b", 4), ("inv_freq", 1)):
    ROWS[_n] = (_at, _k)
    _at += _k
NROWS = _at


def two_pi_parts():
    def short(x, bits):
        m, e = math.frexp(x)
        return math.ldexp(round(m * 2 ** bits) / 2 ** bits, e)
    a = short(TWO_PI, 11)
    b = short(TWO_PI - a, 11)
    return a, b, float(np.float32(TWO_PI - a - b))


def job_list():
    jobs = ["par", "ada0", "ada1", "ada2", "ada3"]
    jobs += [f"xT{j}" for j in range(ND)]
    jobs += ["cq0", "cq1", "cq2", "ckv0", "cqss", "ckv1", "kr", "ckvss", "krs"]
    jobs += [f"z{j}" for j in range(0, 4)] + ["ada4"]
    jobs += [f"z{j}" for j in range(4, 8)] + ["ada5"]
    jobs += [f"z{j}" for j in range(8, 12)] + ["ada6"]
    jobs += ["z12", "z13"]
    for t in range(2):
        jobs += [f"qr{t}", f"qs{t}"]
    jobs += [f"qn{j}" for j in range(4)] + [f"kn{j}" for j in range(4)] + [f"v{i}" for i in range(NT)]
    jobs += ["ada7"]
    units = [(h, q) for h in range(HEADS) for q in range(NT)]
    for u in range(len(units) + LAG):
        if u < len(units):
            jobs.append("s%d_%d" % units[u])
        if u >= LAG:
            h, q = units[u - LAG]
            jobs.append(f"t{h}_{q}")
            if q == NT - 1:
                jobs.append(f"o{h}")
    jobs += [f"uw{j}" for j in range(NJ)] + [f"ua{j}" for j in range(NJ)] + [f"ug{j}" for j in range(NJ)]
    jobs += [f"kss{j}" for j in range(NJ)] + [f"bon{j}" for j in range(NJ)]
    for c in range(NC):
        for g in range(2):
            jobs += [f"mr{c}_{g}_{b}" for b in range(2)]
            jobs += [f"nr{c}_{g}_{b}" for b in range(2)]
        jobs += [f"tok{c}_{n}" for n in range(3)]
        jobs += [f"x{c}_{g}" for g in range(2)]
        for l in range(1, LEVELS):
            jobs += [f"p{c}_{l}_{g}" for g in range(2)]
            if l < LEVELS - 1:
                jobs += [f"dx{c}_{l}_{g}" for g in range(2)]
            jobs += [f"dt{c}_{l}_{g}" for g in range(2)]
        jobs += [f"rhs{c}_{g}" for g in range(2)] + [f"sa{c}"] + [f"y{c}_{g}" for g in range(2)]
        if c < NC - 1:
            jobs += [f"st{c}"]
    jobs += [f"gm{j}" for j in range(NJ)] + [f"gv{j}" for j in range(NJ)]
    for hf in range(2):
        for k in ("ga", "gb", "om", "or"):
            jobs += [f"{k}{hf}_{j}" for j in range(4)]
            if k in ("gb", "om"):
                jobs.append(f"ada{8 + 2 * hf + (k == 'om')}")
    jobs += [f"yo{i}_{n}" for i in range(NT) for n in range(2)]
    jobs += [f"hT{j}" for j in range(ND)]
    jobs += [f"lg{i}" for i in range(NT)] + ["rank"]
    return jobs


def layer(nc, I, out):
    JOBS = {n: i for i, n in enumerate(job_list())}
    TP1, TP2, TP3 = two_pi_parts()

    with ExitStack() as ctx:
        arena = ctx.enter_context(nc.sbuf_tensor("arena", [P, 206 * 256], F32))
        XD = nc.dram_tensor("normed_tokens", [S, D], F32).ap()
        YD = nc.dram_tensor("expert_rows", [2 * S, D], F32).ap()
        TABD = nc.dram_tensor("block_table", [P * NBLK, 4], I32).ap()
        ps = ctx.enter_context(nc.psum_tensor("ps", [P, 8, 512], F32))

        def at(kb, *shape):
            n = 1
            for s in shape:
                n *= s
            v = arena[:, int(kb * 256):int(kb * 256) + n]
            if len(shape) == 1:
                return v
            names = [chr(97 + i) for i in range(len(shape))]
            return v.rearrange(f"p ({' '.join(names)}) -> p {' '.join(names)}", **dict(zip(names, shape)))

        sems = {}

        def sem(name):
            if name not in sems:
                sems[name] = ctx.enter_context(nc.semaphore(name))
            return sems[name]

        psum_full = [sem(f"psum_full{b}") for b in range(8)]
        psum_free = [sem(f"psum_free{b}") for b in range(8)]

        SLOT, NSLOT = 16, 3

        HT = at(48, ND, S)
        X = at(64, NT, D)
        SQ = at(64, 5, S)
        Q, K, V = at(64, HEADS, S), at(80, HEADS, S), at(96, NT, RW)
        CQ, CKV, KR, KRS = at(104, 3, S), at(110, 2, S), at(114, S), at(116, S)
        OT = at(118, NJ, S)
        ZS = at(126, NZ, S)
        RAW = at(154, 4, S + 1)
        PROWS = at(104, P)
        IDXP, IDXF, IDXX = (at(k, P).bitcast(I32) for k in (104.5, 105, 105.5))
        POSI = at(106, S).bitcast(I32)
        ACC = at(163, 2, S)
        ACC2 = at(104, 2, S)
        TR = at(167, 5, S)
        SWK = at(180, 8, 32)
        COS, SIN = at(181, S), at(183, S)
        NPR = 4
        PR, PT = at(161, NPR, S), at(169, 2, NT, S)
        AR = at(64, NJ, NC, 2, CH)
        CUM = KT = at(80, NJ, S)
        RESET = BT = at(88, NJ, S)
        G, SW, AA = at(96, NJ, S), at(104, NJ, S), at(154, NJ, S)
        T1, KK = at(163, NJ, S), at(171, NJ, S)
        RZ, KZ, VZ = ZS[:, 0:4], ZS[:, 4:8], ZS[:, 8:12]
        XI, XT, SA = at(104, HEADS, CH), at(108, HEADS, CH), at(112, HEADS, VD)
        BTOK, KTOK, VTOK, ST = at(114, RW), at(116, RW), at(150, RW), at(152, NJ, VD)
        TOK = [BTOK, KTOK, VTOK]
        MOFF = at(154, 2, HEADS, CH)
        MR, NR = at(163, HEADS, 2 * CH), at(171, HEADS, 2 * CH)
        P1, RHS = at(179, HEADS, CH), at(183, HEADS, VD)
        BONUS, YT = RZ, KZ
        GA, GB, MIX = at(163, 4, S), at(171, 4, S), at(80, ND, S)
        XN2, YS, JUNK = at(126, NT, D), at(126, NT, D), at(104, D)
        TUP = at(108, S)
        XG, HG, YB = at(48, 3, D), at(104, 3, ND, P), at(142, 3, D)
        SIL, ACTB, ACTT = at(154, 3, FF), at(157, 3, FF), at(160, 3, 2, P)
        EW = [(at(k, ND, 2, FF), at(k + 16, 2, D)) for k in (0, 24, 80)]
        GU_BANK = (2, 3, 7)
        YL = at(0, NT, 2, D)
        IDENT, XU, MASKS, MASK2 = at(185, P), at(185.5, P), at(186, LEVELS, P), at(189.5, 2, P)
        BO, BOM, ONES, PAR = at(190.5, P), at(191, P), at(191.5, P), at(192, P)
        GROW = at(192.5, 2, D)
        COLS = at(200.5, 160)
        MODA1, MODB1, MODA2, MODB2 = (COLS[:, 8 * i:8 * i + 8] for i in range(4))
        OMKA, SS2, RS2, SIGN = COLS[:, 32:36], COLS[:, 36:40], COLS[:, 40:44], COLS[:, 44:45]
        SSY, SS4 = COLS[:, 48:56], COLS[:, 56:60]
        SILC, SS, RSTD = COLS[:, 64:72], COLS[:, 72:76], COLS[:, 76:80]
        RSUM, RINV = COLS[:, 96:128], COLS[:, 128:160]
        WR = at(201.25, ND, 36)
        MX, NMX = at(202.5, 32), at(202.75, 32)
        MID, FDEC = at(203, NJ, NC), at(203.25, NJ, NC)
        COMB = at(203.5, NT, NE)
        BR = at(204, 36)
        LOGITS = at(163, NT, 36)
        GHOT, GEXP = at(164, NT, NG), at(164.25, NT, NG)
        EIN, ETMP, HOT1, HOT2 = (at(164.5 + 0.25 * k, NT, EG) for k in range(4))
        GMX, PSEL, EMX1, EMX2, E21, W1, TMX, DUM = (at(165.5 + 0.0625 * k, NT) for k in range(8))
        RANKW = at(166, 8)
        SEL = at(170, 3, NT, NE)
        RANK, CNT = at(171.5, NT, NE), at(172, NE)
        EXTRA, INCL, EIDX, STMP = at(172.25, NE), at(172.5, NE), at(172.75, NE), at(173, NT, NE)
        RK, EK, XK, QK, QT = (at(173.5 + 0.03125 * k, NT) for k in range(5))
        OVT, OVS, BIDX = at(174, XBLK, NE), at(182, XBLK), at(182.25, XBLK)
        OVE, OVN = at(182.5, XBLK).bitcast(I32), at(182.75, 1).bitcast(I32)
        TOK4, EIDI, BIDI = at(183, NT).bitcast(I32), at(183.25, NE).bitcast(I32), at(183.5, XBLK).bitcast(I32)
        REC = at(184, 2, NT, 4).bitcast(I32)
        ROWI = at(184.25, 2, NT).bitcast(I32)
        GI, SR = at(184.375, 3, 4).bitcast(I32), at(184.5, 3, 4).bitcast(I32)
        TAB = at(166.25, NBLK, 4).bitcast(I32)
        DEFT = at(179, NBLK, 4).bitcast(I32)

        def par(v, j=None):
            a, k = ROWS[v]
            return PAR[:, a:a + k] if j is None else PAR[:, a + j:a + j + 1]

        def wsrc(w, c0, n, k=ND):
            return w[:, c0:c0 + n].rearrange("(k p) n -> p k n", p=P)
        W = {n: I[n][0] for n in ("w_ada", "w_in", "w_uq", "w_ukv", "w_o_mla", "w_o_rwkv", "w_out")}
        items = [(f"ada{c}", "dve", wsrc(W["w_ada"], 512 * c, 512)) for c in range(4)]
        items += [("cq", "pe", wsrc(W["w_in"], 0, 384)), ("kv", "pe", wsrc(W["w_in"], C_CKV, 288)),
                  ("ada4", "dve", wsrc(W["w_ada"], 2048, 512)),
                  ("r", "pe", wsrc(W["w_in"], C_ZR, 512)), ("ada5", "dve", wsrc(W["w_ada"], 2560, 512)),
                  ("k", "pe", wsrc(W["w_in"], C_ZR + 512, 512)), ("ada6", "dve", wsrc(W["w_ada"], 3072, 512)),
                  ("vv", "pe", wsrc(W["w_in"], C_ZR + 1024, 512)), ("ada7", "dve", wsrc(W["w_ada"], 3584, 512)),
                  ("wag", "pe", wsrc(W["w_in"], C_ZR + 1536, 256)),
                  ("uq", "pe", wsrc(W["w_uq"], 0, 768)), ("ukv", "pe", wsrc(W["w_ukv"], 0, 1024))]
        items += [("ups", "pe", None)]
        for hf in range(2):
            c0 = 512 * hf
            items += [(f"ga{hf}", "pe", wsrc(W["w_in"], C_GATE + c0, 512)),
                      (f"gb{hf}", "pe", wsrc(W["w_in"], C_GATE + D + c0, 512))]
            items += [(f"ada{c}", "dve", wsrc(W["w_ada"], 512 * c, 512)) for c in (8 + 2 * hf, 9 + 2 * hf)]
            items += [
                      (f"oo{hf}", "pe", (wsrc(W["w_o_mla"], c0, 512), wsrc(W["w_o_rwkv"], c0, 512)))]
        items += [(f"wo{n}", "pe", wsrc(W["w_out"], 512 * n, 512)) for n in range(2)]
        SEQ = {n: i for i, (n, _, _) in enumerate(items)}
        NPARTS = {"uq": 12, "ukv": 4, "ups": 3, "oo0": 2, "oo1": 2}
        landed = []
        slot_count = [0] * NSLOT
        for i, (n, _, _) in enumerate(items):
            slot_count[i % NSLOT] += 16 * NPARTS.get(n, 1)
            landed.append(slot_count[i % NSLOT])
        used_n, used_by = {"pe": 0, "dve": 0}, []
        for n, who, _ in items:
            used_n[who] += 1
            used_by.append((who, used_n[who]))

        def wbuf(name, *shape):
            return at(SLOT * (SEQ[name] % NSLOT), *shape)

        def wait_weights(eng, name):
            i = SEQ[name]
            eng.wait_ge(sem(f"w_landed{i % NSLOT}"), landed[i])

        def full(eng, job):
            n = JOBS[job]
            eng.wait_ge(psum_full[n % 8], n // 8 + 1)

        def bank_of(job):
            return JOBS[job] % 8

        def bank(job):
            return ps[:, JOBS[job] % 8, :]

        block = ctx.enter_context(nc.Block())


        LAST_JOB = {"cq": "cq2", "kv": "krs", "r": "z3", "k": "z7", "vv": "z11", "wag": "z13", "uq": "qn3",
                    "ukv": "v3", "ups": "ug3", "ga0": "ga0_3", "ga1": "ga1_3", "gb0": "gb0_3", "gb1": "gb1_3",
                    "oo0": "or0_3", "oo1": "or1_3", "wo0": "yo3_0", "wo1": "yo3_1"}
        UNITS = [(h, q) for h in range(HEADS) for q in range(NT)]
        BASE = [sum(1 for n in JOBS.values() if n % 8 == b) for b in range(8)]

        def drained(eng, job):
            n = JOBS[job]
            eng.wait_ge(psum_free[n % 8], n // 8 + 1)

        def flat(name):
            v = I[name]
            return v.rearrange("a h c -> a (h c)") if len(v.shape) == 3 else v

        @block.sync
        def _(sp):
            for name, (a, k) in ROWS.items():
                sp.dma_start(PROWS[a:a + k, :], flat(name).rearrange("a (k p) -> (a k) p", p=P)).then_inc(sem("rows_landed"), 16)
            sp.dma_start(POSI, I["positions"].partition_broadcast(P).rearrange("p a s -> p (a s)")).then_inc(sem("pos_landed"), 16)
            sp.dma_start(X, I["x"][0].rearrange("(i p) d -> p i d", p=P)).then_inc(sem("x_landed"), 16)
            for i, (name, who, src) in enumerate(items):
                if i >= NSLOT:
                    before = items[i - NSLOT][0]
                    if items[i - NSLOT][1] == "pe":
                        full(sp, LAST_JOB[before])
                    else:
                        sp.wait_ge(sem("ada_ready"), int(before[3:]) + 1)
                landed_sem = sem(f"w_landed{i % NSLOT}")
                if name == "ups":
                    u = wbuf(name, 2, 512)
                    sp.dma_start(u[0:64, 0, :], I["w_decay_up"][0]).then_inc(landed_sem, 16)
                    sp.dma_start(u[64:128, 0, :], I["w_a_up"][0]).then_inc(landed_sem, 16)
                    sp.dma_start(u[:, 1, :], I["w_g_up"][0]).then_inc(landed_sem, 16)
                elif name == "uq":
                    u, w4 = wbuf(name, 3, 1024), src.rearrange("p k (h c) -> p k h c", h=HEADS)
                    for k in range(3):
                        for dst, c0, n in ((u[:, k, 0:256].rearrange("p (h c) -> p h c", h=HEADS), 64, 32),
                                           (u[:, k, 256:512].rearrange("p (h c) -> p h c", h=HEADS)[:, :, 0:16], 80, 16),
                                           (u[:, k, 256:512].rearrange("p (h c) -> p h c", h=HEADS)[:, :, 16:32], 64, 16),
                                           (u[:, k, 512:1024].rearrange("p (h c) -> p h c", h=HEADS), 0, 64)):
                            sp.dma_start(dst, w4[:, k, :, c0:c0 + n]).then_inc(landed_sem, 16)
                elif name == "ukv":
                    u, w4 = wbuf(name, 2, 2, 512), src.rearrange("p k (h c) -> p k h c", h=HEADS)
                    for k in range(2):
                        for n in range(2):
                            sp.dma_start(u[:, k, n, :].rearrange("p (h c) -> p h c", h=HEADS),
                                         w4[:, k, :, 64 * n:64 * n + 64]).then_inc(landed_sem, 16)
                elif name[:2] == "oo":
                    u = wbuf(name, 2, 4, 512)
                    for n in range(2):
                        sp.dma_start(u[:, n], src[n]).then_inc(landed_sem, 16)
                else:
                    sp.dma_start(wbuf(name, src.shape[1], src.shape[2]), src).then_inc(landed_sem, 16)
                if name == "ada3":
                    sp.dma_start(GROW[:, 0, :], I["g_post_mix"].partition_broadcast(P).rearrange("p a s -> p (a s)")).then_inc(sem("grow_landed"), 16)
                    sp.dma_start(GROW[:, 1, :], I["g_post_ffn"].partition_broadcast(P).rearrange("p a s -> p (a s)")).then_inc(sem("grow_landed"), 16)
                    sp.dma_start(WR[:, :, 0:NG], wsrc(I["w_router_group"][0], 0, NG)).then_inc(sem("wr_landed"), 16)
                    sp.dma_start(WR[:, :, NG:], wsrc(I["w_router_expert"][0], 0, NE)).then_inc(sem("wr_landed"), 16)
                    sp.dma_start(BR[0:1, 0:NG], I["b_router_group"]).then_inc(sem("wr_landed"), 16)
                    sp.dma_start(BR[0:1, NG:], I["b_router_expert"]).then_inc(sem("wr_landed"), 16)
            full(sp, f"y{NC - 1}_1")
            sp.dma_start(X, I["x"][0].rearrange("(i p) d -> p i d", p=P)).then_inc(sem("x_landed"), 16)

            def load_expert(e, s, landed_sem):
                g, d = EW[s]
                for n, w in enumerate(("w_exp_gate", "w_exp_up")):
                    sp.dma_start(g[:, :, n, :], I[w][0, bass.ds(e, 1)].rearrange("a (k p) n -> p (a k) n", p=P)).then_inc(sem(landed_sem), 16)
                sp.dma_start(d, I["w_exp_down"][0, bass.ds(e, 1)].rearrange("a (k p) n -> p (a k) n", p=P)).then_inc(sem(landed_sem), 16)
            full(sp, "yo3_1")
            for b in range(3):
                load_expert(b, b, f"expert_landed{b}")
            sp.wait_ge(sem("table_default"), 1)
            sp.dma_start(TABD.rearrange("(p b) c -> p b c", p=P), DEFT).then_inc(sem("table_cleared"), 16)
            for i in range(NT):
                sp.wait_ge(sem("xn2"), i + 1)
                sp.dma_start(XD[i * P:(i + 1) * P, :], XN2[:, i, :]).then_inc(sem("xn_stored"), 16)
            sp.wait_ge(sem("table_filled"), 16 * 2 * NT)
            sp.dma_start(TAB, TABD.rearrange("(p b) c -> p b c", p=P)).then_inc(sem("table_landed"), 16)
            with sp.Fori(0, 9) as i:
                for j in range(3):
                    b = i * 3 + 3 + j
                    sp.wait_ge(sem("dn_full"), b * 2 - 4)
                    load_expert(b, j, f"expert_landed{j}")
            for b in (30, 31):
                sp.wait_ge(sem("dn_full"), 2 * b - 4)
                load_expert(b, b % 3, f"expert_landed{b % 3}")
            sp.wait_ge(sem("overflow_known"), 1)
            more = sp.value_load(OVN[0:1, 0:1], min_val=0, max_val=XBLK)
            with sp.If(more > 0):
                with sp.Fori(0, XBLK) as i:
                    sp.wait_ge(sem("dn_full"), i * 2 + 2 * NE)
                    e = sp.value_load(OVE[0:1, bass.ds(i, 1)], min_val=0, max_val=NE - 1)
                    load_expert(e, 0, "more_expert_landed")
            sp.wait_ge(sem("rows_stored"), 1)
            for i in range(NT):
                sp.dma_start(YL[:, i, :, :], YD[2 * P * i:2 * P * (i + 1), :].rearrange("(p c) d -> p c d", c=2)).then_inc(sem(f"rows_landed{i}"), 16)
            for i in range(NT):
                sp.wait_ge(sem("out_ready"), i + 1)
                sp.dma_start(out[0, i * P:(i + 1) * P, :], X[:, i, :]).then_inc(sem("out_stored"), 16)
            sp.wait_ge(sem("out_stored"), 16 * NT)

        @block.gpsimd
        def _(pool):
            step = [0]

            def link(ins):
                step[0] += 1
                ins.then_inc(sem("pool_step"), 1)
                pool.wait_ge(sem("pool_step"), step[0])

            nc.gpsimd.iota(IDXP, [[0, P]], base=0, channel_multiplier=1).then_inc(sem("iota"), 1)
            pool.wait_ge(sem("iota"), 1)
            nc.gpsimd.iota(IDXF, [[1, P]], base=0, channel_multiplier=0).then_inc(sem("iota"), 1)
            pool.wait_ge(sem("iota"), 2)
            nc.gpsimd.memset(ONES, 1.0).then_inc(sem("ones"), 1)
            pool.wait_ge(sem("ones"), 1)
            link(nc.gpsimd.memset(RAW[:, :, 0:1], 0.0))
            wait_weights(pool, "kv")
            kv = wbuf("kv", ND, 288)
            link(nc.gpsimd.tensor_copy(SWK[:, :, 0:16], kv[:, :, 272:288]))
            nc.gpsimd.tensor_copy(SWK[:, :, 16:32], kv[:, :, 256:272]).then_inc(sem("swk"), 1)
            pool.wait_ge(sem("swk"), 1)
            full(pool, "z0")
            link(nc.gpsimd.memset(Q[96:100], 1.0))
            link(nc.gpsimd.affine_select(out=Q[96:100], in_=Q[96:100], compare_op=ALU.is_ge, fill=0.0, base=0,
                                        pattern=[[0, HEADS], [1, S]], channel_multiplier=-P))
            link(nc.gpsimd.affine_select(out=Q[96:100], in_=Q[96:100], compare_op=ALU.is_ge, fill=0.0, base=63,
                                        pattern=[[0, HEADS], [-1, S]], channel_multiplier=P))
            link(nc.gpsimd.memset(K[96:100], NEG))
            link(nc.gpsimd.affine_select(out=K[96:100], in_=K[96:100], compare_op=ALU.is_ge, fill=0.0, base=-64,
                                        pattern=[[0, HEADS], [1, S]], channel_multiplier=-P))
            nc.gpsimd.affine_select(out=K[96:100], in_=K[96:100], compare_op=ALU.is_ge, fill=0.0, base=127, pattern=[[0, HEADS], [-1, S]], channel_multiplier=P).then_inc(sem("chunk_mask"), 1)
            pool.wait_ge(sem("chunk_mask"), 1)
            pool.wait_ge(sem("k_rope0"), 1)
            nc.gpsimd.tensor_copy(K[64:96, 1:HEADS, :], K[64:96, 0:1, :].to_broadcast([32, HEADS - 1, S])).then_inc(sem("k_rope"), 1)
            pool.wait_ge(sem("k_rope"), 1)
            for c in range(NC):
                if c > 0:
                    full(pool, f"sa{c - 1}")
                for g in range(2):
                    drained(pool, f"mr{c}_{g}_0")
                    drained(pool, f"mr{c}_{g}_1")
                    mt = MR[:, 4 * g:4 * g + 4, 0:CH]
                    xt = XT[:, 4 * g:4 * g + 4, :]
                    link(nc.gpsimd.tensor_tensor(xt, mt, MASKS[:, 0:1, :].to_broadcast([P, 4, CH]), ALU.mult))
                    nc.gpsimd.tensor_tensor(xt, xt, IDENT.unsqueeze(1).to_broadcast([P, 4, CH]), ALU.add).then_inc(sem("xt_start"), 1)
                    pool.wait_ge(sem("xt_start"), 2 * c + g + 1)
                for l in range(1, LEVELS):
                    for g in range(2):
                        if l > 2:
                            full(pool, f"p{c}_{l - 2}_{g}")
                        nc.gpsimd.tensor_tensor(MOFF[:, l % 2, 4 * g:4 * g + 4, :], MR[:, 4 * g:4 * g + 4, 0:CH], MASKS[:, l:l + 1, :].to_broadcast([P, 4, CH]), ALU.mult).then_inc(sem("moff"), 1)
                        pool.wait_ge(sem("moff"), 2 * ((LEVELS - 1) * c + l - 1) + g + 1)
            full(pool, "hT0")
            nc.gpsimd.iota(TOK4, [[P, NT]], base=0, channel_multiplier=1).then_inc(sem("route_iota"), 1)
            nc.gpsimd.iota(EIDI, [[1, NE]], base=0, channel_multiplier=0).then_inc(sem("route_iota"), 1)
            nc.gpsimd.iota(BIDI, [[1, XBLK]], base=0, channel_multiplier=0).then_inc(sem("route_iota"), 1)
            nc.gpsimd.iota(DEFT, [[4, NBLK], [1, 4]], base=FAR, channel_multiplier=4 * NBLK).then_inc(sem("table_default"), 1)
            for i in range(NT):
                full(pool, f"lg{i}")
            link(nc.gpsimd.memset(XG, 0.0))
            pool.wait_ge(sem("records"), 1)
            pool.wait_ge(sem("table_cleared"), 16)
            for k in range(2):
                for i in range(NT):
                    nc.gpsimd.indirect_dma_start(TABD, bass.IndirectOffsetOnAxis(ap=ROWI[:, k, i:i + 1].bitcast(U32), axis=0),
                                                 REC[:, k, i, :], None).then_inc(sem("table_filled"), 16)
            pool.wait_ge(sem("table_landed"), 16)
            pool.wait_ge(sem("xn_stored"), 16 * NT)

            def gather(b, s, landed_sem):
                link_to(nc.gpsimd.tensor_copy(GI[:, s, :], TAB[:, b, :]), "gi", b)
                nc.gpsimd.indirect_dma_start(XG[:, s, :], None, XD, bass.IndirectOffsetOnAxis(ap=GI[:, s, 0:1].bitcast(U32), axis=0),
                                             bounds_check=S - 1, oob_is_err=False).then_inc(sem(landed_sem), 16)

            def record(b, s):
                link_to(nc.gpsimd.tensor_copy(SR[:, s, :], TAB[:, b, :]), "sr_ready", b)

            def link_to(ins, name, b):
                ins.then_inc(sem(name), 1)
                pool.wait_ge(sem(name), b + 1)

            def scatter(b, s, stored_sem):
                for n in range(2):
                    pool.wait_ge(sem(f"dn_free{n}"), b + 1)
                nc.gpsimd.indirect_dma_start(YD, bass.IndirectOffsetOnAxis(ap=SR[:, s, 1:2].bitcast(U32), axis=0), YB[:, s, :], None,
                                             bounds_check=2 * S - 1, oob_is_err=False).then_inc(sem(stored_sem), 16)
            for b in range(3):
                gather(b, b, f"xg_landed{b}")
            record(0, 0)
            for b in (1, 2):
                pool.wait_ge(sem("xp_full"), 2 * b)
                gather(b + 2, (b + 2) % 3, f"xg_landed{(b + 2) % 3}")
                record(b, b)
                scatter(b - 1, b - 1, f"yb_stored{b - 1}")
            for b in range(3, 30):
                pool.wait_ge(sem("xp_full"), 2 * b)
                gather(b + 2, (b + 2) % 3, f"xg_landed{(b + 2) % 3}")
                pool.wait_ge(sem(f"yb_stored{b % 3}"), 16 * (b // 3))
                record(b, b % 3)
                scatter(b - 1, (b - 1) % 3, f"yb_stored{(b - 1) % 3}")
            for b in (30, 31):
                pool.wait_ge(sem(f"yb_stored{b % 3}"), 160)
                record(b, b % 3)
                scatter(b - 1, (b - 1) % 3, f"yb_stored{(b - 1) % 3}")
            scatter(31, 1, "yb_stored1")
            for s, n in enumerate((11, 11, 10)):
                pool.wait_ge(sem(f"yb_stored{s}"), 16 * n)
            more = pool.value_load(OVN[0:1, 0:1], min_val=0, max_val=XBLK)
            with pool.If(more > 0):
                for i in range(XBLK):
                    b = NE + i
                    pool.wait_ge(sem("xp_full"), 2 * b)
                    gather(b, 0, "more_landed")
                    record(b, 0)
                    scatter(b, 0, "more_stored")
                    pool.wait_ge(sem("more_stored"), 16 * i + 16)
            nc.gpsimd.tensor_copy(GI[:, 0, 3:4], GI[:, 0, 2:3]).then_inc(sem("rows_stored"), 1)

        @block.tensor
        def _(pe):
            T = nc.tensor
            state = {"n": 0}

            def fill(job):
                n = JOBS[job]
                assert n == state["n"], (job, n, state["n"])
                state["n"] += 1
                if n >= 8:
                    pe.wait_ge(psum_free[n % 8], n // 8)
                return ps[:, n % 8, :]

            def project(job, lhs, rhs, n_k, o=None):
                b = fill(job)
                o = b if o is None else o(b)
                for k in range(n_k):
                    mm = T.matmul(o, lhs(k), rhs(k), start=(k == 0), stop=(k == n_k - 1))
                mm.then_inc(psum_full[bank_of(job)], 1)

            def ada(c):
                job = f"ada{c}"
                b = fill(job)
                pe.wait_ge(sem("ada_ready"), c + 1)
                a = (ACC if c < 8 else ACC2)[:, c % 2, :]
                if c in (4, 5, 10, 11):
                    mm = T.matmul(b, ONES, a, start=True, stop=False)
                    for n in range(4):
                        mm = T.matmul(b[:, n * P:(n + 1) * P], par("b_ada", 4 * c + n).to_broadcast([P, P]), IDENT,
                                      start=False, stop=(n == 3))
                else:
                    for n in range(4):
                        mm = T.matmul(b[:, n:n + 1], a[:, n * P:(n + 1) * P], ONES[:, 0:1], start=True, stop=True)
                mm.then_inc(psum_full[bank_of(job)], 1)

            pe.wait_ge(sem("rows_landed"), 16 * len(ROWS))
            pe.wait_ge(sem("masks"), 1)
            b = fill("par")
            mm = T.transpose(b[:, 0:NROWS], PROWS[0:NROWS, :], IDENT[0:NROWS, 0:NROWS])
            mm.then_inc(psum_full[bank_of("par")], 1)
            pe.wait_ge(sem("ones"), 1)
            for c in range(4):
                ada(c)
            pe.wait_ge(sem("xn"), 1)
            for j in range(ND):
                b = fill(f"xT{j}")
                for i in range(NT):
                    mm = T.transpose(b[:, i * P:(i + 1) * P], X[:, i, j * P:(j + 1) * P], IDENT)
                mm.then_inc(psum_full[bank_of(f"xT{j}")], 1)
            for j in range(ND):
                drained(pe, f"xT{j}")
            h = lambda k: HT[:, k, :]
            wait_weights(pe, "cq")
            w = wbuf("cq", ND, 384)
            for t in range(3):
                project(f"cq{t}", lambda k: w[:, k, t * P:(t + 1) * P], h, ND)
            wait_weights(pe, "kv")
            wk = wbuf("kv", ND, 288)
            project("ckv0", lambda k: wk[:, k, 0:P], h, ND)
            for t in range(3):
                drained(pe, f"cq{t}")
            project("cqss", lambda k: ONES, lambda k: SQ[:, k, :], 3)
            project("ckv1", lambda k: wk[:, k, P:2 * P], h, ND)
            project("kr", lambda k: wk[:, k, 256:288], h, ND, lambda b: b[64:96, :])
            for t in range(2):
                drained(pe, f"ckv{t}")
            project("ckvss", lambda k: ONES, lambda k: SQ[:, 3 + k, :], 2)
            pe.wait_ge(sem("swk"), 1)
            project("krs", lambda k: SWK[:, k, :], h, ND, lambda b: b[64:96, :])
            for n, name in enumerate(("r", "k", "vv")):
                wait_weights(pe, name)
                w = wbuf(name, ND, 512)
                for t in range(4):
                    project(f"z{4 * n + t}", lambda k: w[:, k, t * P:(t + 1) * P], h, ND)
                ada(4 + n)
            wait_weights(pe, "wag")
            w = wbuf("wag", ND, 256)
            for t in range(2):
                project(f"z{12 + t}", lambda k: w[:, k, t * P:(t + 1) * P], h, ND)
            pe.wait_ge(sem("cqn"), 1)
            wait_weights(pe, "uq")
            uq = wbuf("uq", 3, 1024)
            for t in range(2):
                project(f"qr{t}", lambda k: uq[:, k, P * t:P * t + P], lambda k: CQ[:, k, :], 3)
                project(f"qs{t}", lambda k: uq[:, k, 256 + P * t:256 + P * t + P], lambda k: CQ[:, k, :], 3)
            for j in range(4):
                project(f"qn{j}", lambda k: uq[:, k, 512 + P * j:512 + P * j + P], lambda k: CQ[:, k, :], 3)
            pe.wait_ge(sem("ckvn"), 1)
            wait_weights(pe, "ukv")
            ukv = wbuf("ukv", 2, 2, 512)
            for j in range(4):
                project(f"kn{j}", lambda k: ukv[:, k, 0, P * j:P * j + P], lambda k: CKV[:, k, :], 2)
            for i in range(NT):
                project(f"v{i}", lambda k: CKV[:, k, i * P:(i + 1) * P], lambda k: ukv[:, k, 1, :], 2)
            ada(7)
            pe.wait_ge(sem("q_rope"), 8)
            pe.wait_ge(sem("k_rope"), 1)
            pe.wait_ge(sem("chunk_mask"), 1)
            for j in range(4):
                drained(pe, f"qn{j}")
                drained(pe, f"kn{j}")
                drained(pe, f"v{j}")
            for u in range(len(UNITS) + LAG):
                if u < len(UNITS):
                    hd, q = UNITS[u]
                    project(f"s{hd}_{q}", lambda k: Q[0:100, hd, q * P:(q + 1) * P],
                            lambda k: K[0:100, hd, 0:(q + 1) * P], 1, lambda b: b[:, 0:(q + 1) * P])
                if u >= LAG:
                    hd, q = UNITS[u - LAG]
                    b = fill(f"t{hd}_{q}")
                    pe.wait_ge(sem("p_ready"), u - LAG + 1)
                    for kb in range(q + 1):
                        mm = T.transpose(b[:, kb * P:(kb + 1) * P], PR[:, (u - LAG) % NPR, kb * P:(kb + 1) * P], IDENT)
                    mm.then_inc(psum_full[bank_of(f"t{hd}_{q}")], 1)
                    if q == NT - 1:
                        b = fill(f"o{hd}")
                        drained(pe, f"t{hd}_{q}")
                        r = slice(64 * (hd % 2), 64 * (hd % 2) + 64)
                        for kb in range(NT):
                            mm = T.matmul(b[r, kb * P:], V[:, kb, hd * VD:(hd + 1) * VD], PT[:, hd % 2, kb, kb * P:],
                                          start=(kb == 0), stop=(kb == NT - 1))
                        mm.then_inc(psum_full[bank_of(f"o{hd}")], 1)
            wait_weights(pe, "ups")
            up = wbuf("ups", 2, 512)
            pe.wait_ge(sem("lowrank"), 2)
            for j in range(NJ):
                project(f"uw{j}", lambda k: up[0:64, 0, j * P:(j + 1) * P], lambda k: ZS[0:64, 12, :], 1)
            for j in range(NJ):
                project(f"ua{j}", lambda k: up[64:128, 0, j * P:(j + 1) * P], lambda k: ZS[64:128, 12, :], 1)
            for j in range(NJ):
                project(f"ug{j}", lambda k: up[:, 1, j * P:(j + 1) * P], lambda k: ZS[:, 13, :], 1)
            for j in range(NJ):
                pe.wait_ge(sem("kk_sq"), j + 1)
                project(f"kss{j}", lambda k: BO, lambda k: T1[:, j, :], 1)
            for j in range(NJ):
                pe.wait_ge(sem("rk"), j + 1)
                project(f"bon{j}", lambda k: BO, lambda k: RZ[:, j, :], 1)
            pe.wait_ge(sem("rwkv_in"), 1)
            for c in range(NC):
                cs = slice(c * CH, (c + 1) * CH)
                for g in range(2):
                    r = slice(64 * g, 64 * g + 64)
                    for name, src in (("mr", BT), ("nr", KT)):
                        for n in range(2):
                            b = fill(f"{name}{c}_{g}_{n}")
                            for m in range(2):
                                j = 2 * n + m
                                mm = T.matmul(b[:, m * 256:(m + 1) * 256], src[r, j, cs],
                                              AR[r, j, c, :, :].rearrange("p a t -> p (a t)"), start=True, stop=True)
                            mm.then_inc(psum_full[bank_of(f"{name}{c}_{g}_{n}")], 1)
                for n, src in enumerate((BT, KT, VZ)):
                    b = fill(f"tok{c}_{n}")
                    for j in range(NJ):
                        mm = T.transpose(b[:, j * P:(j + 1) * P], src[:, j, cs], IDENT)
                    mm.then_inc(psum_full[bank_of(f"tok{c}_{n}")], 1)
                for g in range(2):
                    b = fill(f"x{c}_{g}")
                    pe.wait_ge(sem("xt_start"), 2 * c + g + 1)
                    for j in range(4):
                        mm = T.transpose(b[:, j * P:(j + 1) * P], XT[:, 4 * g + j, :], IDENT)
                    mm.then_inc(psum_full[bank_of(f"x{c}_{g}")], 1)

                def stage(job, g, lhs, rhs):
                    b = fill(job)
                    for j in range(4):
                        mm = T.matmul(b[:, j * P:(j + 1) * P], lhs[:, 4 * g + j, :], rhs[:, 4 * g + j, :], start=True, stop=True)
                    mm.then_inc(psum_full[bank_of(job)], 1)
                for l in range(1, LEVELS):
                    for g in range(2):
                        pe.wait_ge(sem("moff"), 2 * ((LEVELS - 1) * c + l - 1) + g + 1)
                        drained(pe, f"x{c}_{g}" if l == 1 else f"dx{c}_{l - 1}_{g}")
                        stage(f"p{c}_{l}_{g}", g, MOFF[:, l % 2], XI)
                    if l < LEVELS - 1:
                        for g in range(2):
                            drained(pe, f"p{c}_{l}_{g}")
                            if l > 1:
                                drained(pe, f"dt{c}_{l - 1}_{g}")
                            stage(f"dx{c}_{l}_{g}", g, XT, P1)
                    for g in range(2):
                        drained(pe, f"p{c}_{l}_{g}")
                        if l > 1:
                            drained(pe, f"dt{c}_{l - 1}_{g}")
                        stage(f"dt{c}_{l}_{g}", g, P1, XT)
                for n in range(3):
                    drained(pe, f"tok{c}_{n}")
                for g in range(2):
                    r = slice(64 * g, 64 * g + 64)
                    b = fill(f"rhs{c}_{g}")
                    if c > 0:
                        drained(pe, f"st{c - 1}")
                        for j in range(4):
                            T.matmul(b[:, j * 64:j * 64 + 64], AR[r, j, c, 0, :], ST[r, j, :], start=(j == 0),
                                     stop=False, skip_group_check=True)
                    for j in range(4):
                        hd = 2 * j + g
                        mm = T.matmul(b[:, j * 64:j * 64 + 64], NR[:, 4 * g + j, 0:CH], VTOK[:, hd * 64:hd * 64 + 64],
                                      start=(c == 0), stop=True, skip_group_check=c > 0)
                    mm.then_inc(psum_full[bank_of(f"rhs{c}_{g}")], 1)
                b = fill(f"sa{c}")
                for g in range(2):
                    drained(pe, f"rhs{c}_{g}")
                    drained(pe, f"dt{c}_{LEVELS - 1}_{g}")
                    for j in range(4):
                        q = 4 * g + j
                        mm = T.matmul(b[:, q * 64:q * 64 + 64], XT[:, q, :], RHS[:, q, :], start=True, stop=True)
                mm.then_inc(psum_full[bank_of(f"sa{c}")], 1)
                drained(pe, f"sa{c}")
                for g in range(2):
                    r = slice(64 * g, 64 * g + 64)
                    b = fill(f"y{c}_{g}")
                    if c > 0:
                        for j in range(4):
                            T.matmul(b[r, j * P:(j + 1) * P], ST[r, j, :], AR[r, j, c, 1, :], start=(j == 0), stop=False,
                                     skip_group_check=True)
                    for j in range(4):
                        q, hd = 4 * g + j, 2 * j + g
                        T.matmul(b[r, j * P:(j + 1) * P], SA[:, q, :], MR[:, q, CH:], start=(c == 0), stop=False,
                                 skip_group_check=c > 0)
                        mm = T.matmul(b[r, j * P:(j + 1) * P], VTOK[:, hd * 64:hd * 64 + 64], NR[:, q, CH:], start=False,
                                      stop=True, skip_group_check=c > 0)
                    mm.then_inc(psum_full[bank_of(f"y{c}_{g}")], 1)
                if c < NC - 1:
                    b = fill(f"st{c}")
                    for g in range(2):
                        for j in range(4):
                            q, hd = 4 * g + j, 2 * j + g
                            o = b[64 * g:64 * g + 64, j * 64:j * 64 + 64]
                            T.matmul(o, BTOK[:, hd * 64:hd * 64 + 64], SA[:, q, :], start=True, stop=False)
                            mm = T.matmul(o, KTOK[:, hd * 64:hd * 64 + 64], VTOK[:, hd * 64:hd * 64 + 64], start=False, stop=True)
                    mm.then_inc(psum_full[bank_of(f"st{c}")], 1)
            for g in range(2):
                drained(pe, f"y{NC - 1}_{g}")
            for j in range(NJ):
                project(f"gm{j}", lambda k: BOM, lambda k: YT[:, j, :], 1)
            for j in range(NJ):
                pe.wait_ge(sem("y_sq"), j + 1)
                project(f"gv{j}", lambda k: BOM, lambda k: T1[:, j, :], 1)
            for hf in range(2):
                for name in ("ga", "gb"):
                    wait_weights(pe, f"{name}{hf}")
                    w = wbuf(f"{name}{hf}", ND, 512)
                    for j in range(4):
                        project(f"{name}{hf}_{j}", lambda k: w[:, k, j * P:(j + 1) * P], h, ND)
                ada(8 + 2 * hf)
                wait_weights(pe, f"oo{hf}")
                w = wbuf(f"oo{hf}", 2, 4, 512)
                for j in range(4):
                    project(f"om{hf}_{j}", lambda k: w[:, 0, k, j * P:(j + 1) * P], lambda k: OT[:, k, :], NJ)
                ada(9 + 2 * hf)
                pe.wait_ge(sem("rwkv_out"), 1)
                for j in range(4):
                    project(f"or{hf}_{j}", lambda k: w[:, 1, k, j * P:(j + 1) * P], lambda k: YT[:, k, :], NJ)
            for n in range(2):
                wait_weights(pe, f"wo{n}")
            pe.wait_ge(sem("mix"), 8)
            for i in range(NT):
                for n in range(2):
                    w = wbuf(f"wo{n}", ND, 512)
                    project(f"yo{i}_{n}", lambda k: MIX[:, k, i * P:(i + 1) * P], lambda k: w[:, k, :], ND)
            pe.wait_ge(sem("xn2"), 4)
            for j in range(ND):
                b = fill(f"hT{j}")
                for i in range(NT):
                    mm = T.transpose(b[:, i * P:(i + 1) * P], XN2[:, i, j * P:(j + 1) * P], IDENT)
                mm.then_inc(psum_full[bank_of(f"hT{j}")], 1)
            for j in range(ND):
                drained(pe, f"hT{j}")
            pe.wait_ge(sem("wr_landed"), 64)
            for i in range(NT):
                b = fill(f"lg{i}")
                for k in range(ND):
                    T.matmul(b[:, 0:36], HT[:, k, i * P:(i + 1) * P], WR[:, k, :], start=(k == 0), stop=False)
                mm = T.matmul(b[:, 0:36], ONES[0:1, :], BR[0:1, :], start=False, stop=True)
                mm.then_inc(psum_full[bank_of(f"lg{i}")], 1)
            b = fill("rank")
            pe.wait_ge(sem("sel"), 1)
            for i in range(NT):
                for m in range(i + 1):
                    T.matmul(b[:, i * NE:(i + 1) * NE], ONES if m < i else MASK2[:, 0, :], SEL[:, 2, m, :], start=(m == 0), stop=(m == i))
            for m in range(NT):
                mm = T.matmul(b[:, NT * NE:(NT + 1) * NE], ONES, SEL[:, 2, m, :], start=(m == 0), stop=(m == NT - 1))
            mm.then_inc(psum_full[bank_of("rank")], 1)
            for n in range(8):
                pe.wait_ge(psum_free[n], BASE[n])

            def xp(b, s, first=False):
                for n in range(2):
                    if not first:
                        pe.wait_ge(sem("xp_free"), b * 2 + n - 1)
                    for k in range(4):
                        mm = T.transpose(ps[:, n, k * P:(k + 1) * P], XG[:, s, (4 * n + k) * P:(4 * n + k + 1) * P], IDENT)
                    mm.then_inc(sem("xp_full"), 1)

            def gu(b, s):
                pe.wait_ge(sem("xp_free"), b * 2 + 2)
                for k in range(ND):
                    mm = T.matmul(ps[:, GU_BANK[s], :], HG[:, s, k, :], EW[s][0][:, k].rearrange("p a n -> p (a n)"),
                                  start=(k == 0), stop=(k == ND - 1))
                mm.then_inc(sem("gu_full"), 1)

            def at_(b, s):
                pe.wait_ge(sem("act_ready"), b + 1)
                for k in range(2):
                    mm = T.transpose(ps[:, 4, k * P:(k + 1) * P], ACTB[:, s, k * P:(k + 1) * P], IDENT)
                mm.then_inc(sem("at_full"), 1)

            def dn(b, s, first=False):
                pe.wait_ge(sem("at_free"), b + 1)
                for n in range(2):
                    if not first:
                        pe.wait_ge(sem(f"dn_free{n}"), b)
                    for k in range(2):
                        mm = T.matmul(ps[:, 5 + n, :], ACTT[:, s, k, :], EW[s][1][:, k, n * 512:(n + 1) * 512],
                                      start=(k == 0), stop=(k == 1))
                    mm.then_inc(sem("dn_full"), 1)
            pe.wait_ge(sem("xg_landed0"), 16)
            xp(0, 0, True)
            pe.wait_ge(sem("expert_landed0"), 48)
            gu(0, 0)
            pe.wait_ge(sem("xg_landed1"), 16)
            xp(1, 1)
            pe.wait_ge(sem("expert_landed1"), 48)
            gu(1, 1)
            at_(0, 0)
            pe.wait_ge(sem("xg_landed2"), 16)
            xp(2, 2)
            dn(0, 0, True)
            with pe.Fori(0, 9) as i:
                for j in range(3):
                    b, s = i * 3 + 2 + j, (2 + j) % 3
                    pe.wait_ge(sem(f"expert_landed{s}"), (i + (2 + j) // 3) * 48 + 48)
                    gu(b, s)
                    at_(b - 1, (s + 2) % 3)
                    pe.wait_ge(sem(f"xg_landed{j}"), i * 16 + 32)
                    xp(b + 1, j)
                    dn(b - 1, (s + 2) % 3)
            for b in (29, 30, 31):
                s = b % 3
                pe.wait_ge(sem(f"expert_landed{s}"), 48 * (b // 3 + 1))
                gu(b, s)
                at_(b - 1, (b - 1) % 3)
                if b < 31:
                    pe.wait_ge(sem(f"xg_landed{(b + 1) % 3}"), 16 * ((b + 1) // 3 + 1))
                    xp(b + 1, (b + 1) % 3)
                dn(b - 1, (b - 1) % 3)
            at_(31, 1)
            dn(31, 1)
            pe.wait_ge(sem("overflow_known"), 1)
            more = pe.value_load(OVN[0:1, 0:1], min_val=0, max_val=XBLK)
            with pe.If(more > 0):
                with pe.Fori(0, XBLK) as i:
                    b = i + NE
                    pe.wait_ge(sem("more_landed"), i * 16 + 16)
                    xp(b, 0)
                    pe.wait_ge(sem("more_expert_landed"), i * 48 + 48)
                    gu(b, 0)
                    at_(b, 0)
                    dn(b, 0)

        @block.scalar
        def _(act):
            step = [0]

            def link(ins):
                step[0] += 1
                ins.then_inc(sem("act_step"), 1)
                act.wait_ge(sem("act_step"), step[0])

            A = nc.scalar.activation
            for i in range(NT):
                if i == 0:
                    act.wait_ge(sem("x_landed"), 16)
                link(A(K[:, 0:2, :].rearrange("p a s -> p (a s)"), X[:, i, :], ACT.Square, accum_out=SS[:, i:i + 1]))
            nc.scalar.copy(SS[:, 0:4], SS[:, 0:4]).then_inc(sem("x_ss"), 1)
            act.wait_ge(sem("x_ss"), 1)
            act.wait_ge(sem("x_var"), 1)
            A(RSTD, SS, ACT.Sqrt).then_inc(sem("x_sqrt"), 1)
            act.wait_ge(sem("x_sqrt"), 1)
            drained(act, "par")
            A(SILC, par("c"), ACT.Silu).then_inc(sem("silc"), 1)
            act.wait_ge(sem("silc"), 1)
            drained(act, "ada3")
            for j in range(1, ND, 2):
                full(act, f"xT{j}")
                A(HT[:, j, :], bank(f"xT{j}"), ACT.Identity, bias=MODB1[:, j:j + 1], scale=MODA1[:, j:j + 1]).then_inc(psum_free[bank_of(f"xT{j}")], 1)
                drained(act, f"xT{j}")

            for k, t in enumerate((SIN, COS)):
                act.wait_ge(sem("angle"), k + 1)
                A(t, t, ACT.Sin).then_inc(sem("sincos"), 1)
                act.wait_ge(sem("sincos"), k + 1)

            def latent(name, tiles, dst, sq0, n):
                for t in range(tiles):
                    job = f"{name}{t}"
                    full(act, job)
                    link(nc.scalar.copy(dst[:, t, :], bank(job)))
                    A(SQ[:, sq0 + t, :], bank(job), ACT.Square).then_inc(psum_free[bank_of(job)], 1)
                    drained(act, job)
                act.wait_ge(sem("lat_var"), n)
                A(TR[:, n - 1, :], TR[:, n - 1, :], ACT.Sqrt).then_inc(sem("lat_sqrt"), 1)
                act.wait_ge(sem("lat_sqrt"), n)
            latent("cq", 3, CQ, 0, 1)
            latent("ckv", 2, CKV, 3, 2)
            for j in range(NZ):
                full(act, f"z{j}")
                if j >= 4:
                    act.wait_ge(sem("zs"), j - 3)
                nc.scalar.copy(RAW[:, j % 4, 1:], bank(f"z{j}")).then_inc(psum_free[bank_of(f"z{j}")], 1)
                drained(act, f"z{j}")
            act.wait_ge(sem("zs"), 13)
            A(ZS[0:64, 12, :], ZS[0:64, 12, :], ACT.Tanh).then_inc(sem("lowrank"), 1)
            act.wait_ge(sem("lowrank"), 1)
            act.wait_ge(sem("zs"), 14)
            A(ZS[:, 13, :], ZS[:, 13, :], ACT.Sigmoid).then_inc(sem("lowrank"), 1)
            act.wait_ge(sem("lowrank"), 2)
            for name, dst in (("qn", Q), ("kn", K)):
                for j in range(4):
                    full(act, f"{name}{j}")
                    b = bank(f"{name}{j}")
                    link(nc.scalar.copy(dst[0:64, 2 * j, :], b[0:64, :]))
                    nc.scalar.copy(dst[0:64, 2 * j + 1, :], b[64:128, :]).then_inc(psum_free[bank_of(f"{name}{j}")], 1)
                    drained(act, f"{name}{j}")
            for i in range(NT):
                full(act, f"v{i}")
                nc.scalar.copy(V[:, i, :], bank(f"v{i}")).then_inc(psum_free[bank_of(f"v{i}")], 1)
                drained(act, f"v{i}")
            for u in range(len(UNITS) + LAG):
                if u < len(UNITS):
                    hd, q = UNITS[u]
                    job = f"s{hd}_{q}"
                    n = (q + 1) * P
                    act.wait_ge(sem("row_max"), u + 1)
                    if u >= NPR:
                        full(act, "t%d_%d" % UNITS[u - NPR])
                    A(PR[:, u % NPR, 0:n], bank(job)[:, 0:n], ACT.Exp, bias=NMX[:, u:u + 1], scale=ATT_SCALE).then_inc(psum_free[bank_of(job)], 1)
                    drained(act, job)
                if u >= LAG:
                    hd, q = UNITS[u - LAG]
                    job = f"t{hd}_{q}"
                    full(act, job)
                    if q == 0 and hd >= 2:
                        full(act, f"o{hd - 2}")
                    nc.scalar.copy(PT[:, hd % 2, 0:q + 1, q * P:(q + 1) * P], bank(job)[:, 0:(q + 1) * P].rearrange("p (k t) -> p k t", t=P)).then_inc(psum_free[bank_of(job)], 1)
                    drained(act, job)
            for name, dst, vec in (("uw", SW, "decay_bias"), ("ua", AA, "a_bias")):
                for j in range(NJ):
                    job = f"{name}{j}"
                    full(act, job)
                    A(dst[:, j, :], bank(job), ACT.Sigmoid, bias=par(vec, j)).then_inc(psum_free[bank_of(job)], 1)
                    drained(act, job)
            for j in range(NJ):
                full(act, f"ug{j}")
                nc.scalar.copy(G[:, j, :], bank(f"ug{j}")).then_inc(psum_free[bank_of(f"ug{j}")], 1)
                drained(act, f"ug{j}")
            for j in range(NJ):
                act.wait_ge(sem("kk0"), j + 1)
                A(T1[:, j, :], KK[:, j, :], ACT.Square).then_inc(sem("kk_sq"), 1)
                act.wait_ge(sem("kk_sq"), j + 1)
            for j in range(NJ):
                full(act, f"kss{j}")
                A(T1[:, j, :], bank(f"kss{j}"), ACT.Sqrt).then_inc(psum_free[bank_of(f"kss{j}")], 1)
                drained(act, f"kss{j}")
            act.wait_ge(sem("decay"), 1)
            A(FDEC, FDEC, ACT.Exp, scale=DECAY).then_inc(sem("e_f"), 1)
            act.wait_ge(sem("e_f"), 1)
            act.wait_ge(sem("decay"), 2)
            A(SW, SW, ACT.Exp, scale=DECAY).then_inc(sem("e_a"), 1)
            act.wait_ge(sem("e_a"), 1)
            act.wait_ge(sem("kkn"), 1)
            A(T1, CUM, ACT.Exp, scale=DECAY).then_inc(sem("e_r"), 1)
            act.wait_ge(sem("e_r"), 1)
            act.wait_ge(sem("r_done"), 1)
            A(T1, CUM, ACT.Exp, scale=-DECAY).then_inc(sem("e_b"), 1)
            act.wait_ge(sem("e_b"), 1)

            for c in range(NC):
                for n in range(3):
                    full(act, f"tok{c}_{n}")
                    nc.scalar.copy(TOK[n], bank(f"tok{c}_{n}")).then_inc(psum_free[bank_of(f"tok{c}_{n}")], 1)
                    drained(act, f"tok{c}_{n}")
                for g in range(2):
                    full(act, f"x{c}_{g}")
                    nc.scalar.copy(XI[:, 4 * g:4 * g + 4].rearrange("p a b -> p (a b)"), bank(f"x{c}_{g}")).then_inc(psum_free[bank_of(f"x{c}_{g}")], 1)
                    drained(act, f"x{c}_{g}")
                for l in range(1, LEVELS):
                    for g in range(2):
                        job = f"p{c}_{l}_{g}"
                        full(act, job)
                        nc.scalar.copy(P1[:, 4 * g:4 * g + 4].rearrange("p a b -> p (a b)"), bank(job)).then_inc(psum_free[bank_of(job)], 1)
                        drained(act, job)
                for g in range(2):
                    job = f"rhs{c}_{g}"
                    full(act, job)
                    nc.scalar.copy(RHS[:, 4 * g:4 * g + 4].rearrange("p a b -> p (a b)"), bank(job)[:, 0:256]).then_inc(psum_free[bank_of(job)], 1)
                    drained(act, job)
                for g in range(2):
                    job = f"y{c}_{g}"
                    full(act, job)
                    r = slice(64 * g, 64 * g + 64)
                    nc.scalar.copy(YT[r, :, c * CH:(c + 1) * CH], bank(job)[r].rearrange("p (j t) -> p j t", t=CH)).then_inc(psum_free[bank_of(job)], 1)
                    drained(act, job)
            for j in range(NJ):
                act.wait_ge(sem("y_c"), j + 1)
                A(T1[:, j, :], YT[:, j, :], ACT.Square).then_inc(sem("y_sq"), 1)
                act.wait_ge(sem("y_sq"), j + 1)
            for j in range(NJ):
                act.wait_ge(sem("y_var"), j + 1)
                A(KK[:, j, :], KK[:, j, :], ACT.Sqrt).then_inc(sem("y_sqrt"), 1)
                act.wait_ge(sem("y_sqrt"), j + 1)
            act.wait_ge(sem("rwkv_out"), 1)
            for hf in range(2):
                for name, dst in (("ga", GA), ("gb", GB)):
                    for j in range(4):
                        job = f"{name}{hf}_{j}"
                        full(act, job)
                        if hf:
                            act.wait_ge(sem("mix"), j + 1)
                        A(dst[:, j, :], bank(job), ACT.Sigmoid).then_inc(psum_free[bank_of(job)], 1)
                        drained(act, job)
            for i in range(NT):
                for n in range(2):
                    job = f"yo{i}_{n}"
                    full(act, job)
                    link(A(JUNK[:, n * 512:(n + 1) * 512], bank(job), ACT.Square, accum_out=SSY[:, 2 * i + n:2 * i + n + 1]))
                nc.scalar.copy(SS4[:, i:i + 1], SSY[:, 2 * i:2 * i + 1]).then_inc(sem("y_ss"), 1)
                act.wait_ge(sem("y_ss"), i + 1)
                act.wait_ge(sem("yo_var"), i + 1)
                A(SS4[:, i:i + 1], SS4[:, i:i + 1], ACT.Sqrt).then_inc(sem("yo_sqrt"), 1)
                act.wait_ge(sem("yo_sqrt"), i + 1)
            for i in range(NT):
                act.wait_ge(sem("x1"), i + 1)
                link(A(JUNK, X[:, i, :], ACT.Square, accum_out=SS2[:, i:i + 1]))
                nc.scalar.copy(SS2[:, i:i + 1], SS2[:, i:i + 1]).then_inc(sem("x1_ss"), 1)
                act.wait_ge(sem("x1_ss"), i + 1)
                act.wait_ge(sem("x1_var"), i + 1)
                A(RS2[:, i:i + 1], SS2[:, i:i + 1], ACT.Sqrt).then_inc(sem("x1_sqrt"), 1)
                act.wait_ge(sem("x1_sqrt"), i + 1)
            for j in range(1, ND, 2):
                full(act, f"hT{j}")
                A(HT[:, j, :], bank(f"hT{j}"), ACT.Identity, bias=MODB2[:, j:j + 1], scale=MODA2[:, j:j + 1]).then_inc(psum_free[bank_of(f"hT{j}")], 1)
                drained(act, f"hT{j}")
            act.wait_ge(sem("gmax"), 1)
            A(GEXP, GEXP, ACT.Exp).then_inc(sem("gexp"), 1)
            act.wait_ge(sem("gexp"), 1)
            act.wait_ge(sem("emax"), 1)
            A(E21, E21, ACT.Exp).then_inc(sem("eexp"), 1)
            act.wait_ge(sem("eexp"), 1)

            def silu(b, s):
                act.wait_ge(sem("gu_full"), b + 1)
                A(SIL[:, s, :], ps[:, GU_BANK[s], 0:FF], ACT.Silu).then_inc(sem("sil_ready"), 1)

            def take_x(b, s):
                for n in range(2):
                    act.wait_ge(sem("xp_full"), b * 2 + n + 1)
                    for k in range(4 * n, 4 * n + 4):
                        ins = A(HG[:, s, k, :], ps[:, n, (k % 4) * P:(k % 4 + 1) * P], ACT.Identity, bias=MODB2[:, k:k + 1],
                                scale=MODA2[:, k:k + 1])
                    ins.then_inc(sem("xp_free"), 1)

            def take_y(b, s):
                act.wait_ge(sem("dn_full"), b * 2 + 2)
                act.wait_ge(sem("sr_ready"), b + 1)
                A(YB[:, s, 512:], ps[:, 6, :], ACT.Copy, scale=SR[:, s, 2:3].bitcast(F32)).then_inc(sem("dn_free1"), 1)
            take_x(0, 0)
            silu(0, 0)
            take_x(1, 1)
            with act.Fori(0, 10) as i:
                for j in range(3):
                    b, s = i * 3 + 1 + j, (1 + j) % 3
                    silu(b, s)
                    take_x(b + 1, (s + 1) % 3)
                    take_y(b - 1, j)
            silu(31, 1)
            take_y(30, 0)
            take_y(31, 1)
            act.wait_ge(sem("overflow_known"), 1)
            more = act.value_load(OVN[0:1, 0:1], min_val=0, max_val=XBLK)
            with act.If(more > 0):
                with act.Fori(0, XBLK) as i:
                    b = i + NE
                    take_x(b, 0)
                    silu(b, 0)
                    take_y(b, 0)
            for i in range(NT):
                act.wait_ge(sem("y_fin"), i + 1)
                link(A(JUNK, YS[:, i, :], ACT.Square, accum_out=SS[:, i:i + 1]))
            nc.scalar.copy(SS, SS).then_inc(sem("fin_ss"), 1)
            act.wait_ge(sem("fin_ss"), 1)
            act.wait_ge(sem("fin_var"), 1)
            A(SS, SS, ACT.Sqrt).then_inc(sem("fin_sqrt"), 1)

        @block.vector
        def _(dve):
            step = [0]

            def link(ins):
                step[0] += 1
                ins.then_inc(sem("dve_step"), 1)
                dve.wait_ge(sem("dve_step"), step[0])

            v = nc.vector
            dve.wait_ge(sem("iota"), 2)
            link(v.tensor_tensor(IDXX, IDXP, IDXF, ALU.bitwise_xor))
            link(v.tensor_copy(XU, IDXX))
            link(v.tensor_scalar(IDENT, XU, 0.5, None, ALU.is_lt))
            link(v.tensor_scalar(BO, XU, 63.5, None, ALU.is_lt))
            link(v.tensor_scalar(BOM, BO, 1.0 / 64, None, ALU.mult))
            link(v.tensor_tensor(MASK2[:, 0, :], IDXF, IDXP, ALU.is_gt))
            link(v.tensor_tensor(MASK2[:, 1, :], IDXF, IDXP, ALU.is_ge))
            link(v.tensor_tensor(XU, XU, MASK2[:, 0, :], ALU.mult))
            for l in range(LEVELS):
                link(v.tensor_scalar(MASKS[:, l, :], XU, 2 ** l - 0.5, None, ALU.is_gt))
                link(v.tensor_scalar(TR[:, 0, 0:P], XU, 2 ** (l + 1) - 0.5, None, ALU.is_gt))
                link(v.tensor_tensor(MASKS[:, l, :], MASKS[:, l, :], TR[:, 0, 0:P], ALU.subtract))
            link(v.tensor_scalar(IDXX[:, 0:1], IDXP[:, 0:1], 16, None, ALU.bitwise_and))
            link(v.tensor_copy(SIGN, IDXX[:, 0:1]))
            v.tensor_scalar(SIGN, SIGN, 0.125, -1.0, ALU.mult, ALU.add).then_inc(sem("masks"), 1)
            dve.wait_ge(sem("masks"), 1)
            full(dve, "par")
            v.tensor_copy(PAR[:, 0:NROWS], bank("par")[:, 0:NROWS]).then_inc(psum_free[bank_of("par")], 1)
            drained(dve, "par")
            dve.wait_ge(sem("x_ss"), 1)
            v.tensor_scalar(SS, SS, 1.0 / D, RMS_EPS, ALU.mult, ALU.add).then_inc(sem("x_var"), 1)
            dve.wait_ge(sem("x_var"), 1)
            dve.wait_ge(sem("x_sqrt"), 1)
            link(v.reciprocal(RSTD, RSTD))
            for i in range(NT):
                ins = v.tensor_scalar(X[:, i, :], X[:, i, :], RSTD[:, i:i + 1], None, ALU.mult)
                if i < NT - 1:
                    link(ins)
                else:
                    ins.then_inc(sem("xn"), 1)
                    dve.wait_ge(sem("xn"), 1)
            link(v.tensor_scalar(OMKA, par("k_a"), -1.0, 1.0, ALU.mult, ALU.add))
            dve.wait_ge(sem("silc"), 1)

            def ada_products(c):
                wait_weights(dve, f"ada{c}")
                if c >= 2:
                    full(dve, f"ada{c - 2}")
                w, a = wbuf(f"ada{c}", ND, 512), (ACC if c < 8 else ACC2)[:, c % 2, :]
                link(v.tensor_scalar(a, w[:, 0, :], SILC[:, 0:1], None, ALU.mult))
                for k in range(1, ND):
                    ins = v.scalar_tensor_tensor(a, w[:, k, :], SILC[:, k:k + 1], a, ALU.mult, ALU.add)
                    if k < ND - 1:
                        link(ins)
                    else:
                        ins.then_inc(sem("ada_ready"), 1)
                        dve.wait_ge(sem("ada_ready"), c + 1)

            def ada_take(c):
                job = f"ada{c}"
                full(dve, job)
                hf = c % 2
                b = bank(job)
                bias = par("b_ada")[:, 4 * c:4 * c + 4]
                s = slice(4 * hf, 4 * hf + 4)
                kind = c // 2
                if kind in (0, 3):
                    v.tensor_tensor((MODB1 if kind == 0 else MODB2)[:, s], b[:, 0:4], bias, ALU.add).then_inc(psum_free[bank_of(job)], 1)
                    drained(dve, job)
                elif kind in (1, 4):
                    m, gv = (MODA1, par("g_pre_mix")) if kind == 1 else (MODA2, par("g_pre_ffn"))
                    link(v.tensor_tensor(m[:, s], b[:, 0:4], bias, ALU.add))
                    v.scalar_tensor_tensor(m[:, s], m[:, s], 1.0, gv[:, s], ALU.add, ALU.mult).then_inc(psum_free[bank_of(job)], 1)
                    drained(dve, job)
                else:
                    dve.wait_ge(sem("grow_landed"), 32)
                    gr = GROW[:, 0 if kind == 2 else 1, hf * 512:(hf + 1) * 512]
                    v.tensor_tensor(gr, b, gr, ALU.mult).then_inc(psum_free[bank_of(job)], 1)
                    drained(dve, job)

            for c in range(4):
                ada_products(c)
                ada_take(c)
            for j in range(0, ND, 2):
                full(dve, f"xT{j}")
                v.tensor_scalar(HT[:, j, :], bank(f"xT{j}"), MODA1[:, j:j + 1], MODB1[:, j:j + 1], ALU.mult, ALU.add).then_inc(psum_free[bank_of(f"xT{j}")], 1)
                drained(dve, f"xT{j}")
            dve.wait_ge(sem("pos_landed"), 16)
            ang, n, t = TR[:, 2, :], TR[:, 3, :], TR[:, 4, :]
            link(v.tensor_copy(ang, POSI))
            link(v.tensor_scalar(ang, ang, par("inv_freq"), None, ALU.mult))
            for k, dst in enumerate((SIN, COS)):
                link(v.tensor_scalar(n, ang, 1.0 / TWO_PI, 0.25 * k, ALU.mult, ALU.add))
                link(v.tensor_scalar(n, n, ROUND, None, ALU.add))
                link(v.tensor_scalar(n, n, ROUND, None, ALU.subtract))
                link(v.scalar_tensor_tensor(t, n, -TP1, ang, ALU.mult, ALU.add))
                link(v.scalar_tensor_tensor(t, n, -TP2, t, ALU.mult, ALU.add))
                link(v.scalar_tensor_tensor(t, n, -TP3, t, ALU.mult, ALU.add))
                link(v.tensor_scalar(t, t, 0.5 * math.pi * k, math.pi, ALU.add, ALU.min))
                v.tensor_scalar(dst, t, -3.1415925, None, ALU.max).then_inc(sem("angle"), 1)
                dve.wait_ge(sem("angle"), k + 1)
            dve.wait_ge(sem("sincos"), 2)
            link(v.tensor_scalar(SIN, SIN, SIGN, None, ALU.mult))

            def latent(job, n, dst, tiles, width, vec, name):
                full(dve, job)
                t = TR[:, n - 1, :]
                v.tensor_scalar(t, bank(job), 1.0 / width, RMS_EPS, ALU.mult, ALU.add).then_inc(psum_free[bank_of(job)], 1)
                drained(dve, job)
                ins = v.tensor_copy(t[:, 0:1], t[:, 0:1])
                ins.then_inc(sem("lat_var"), 1)
                dve.wait_ge(sem("lat_var"), n)
                dve.wait_ge(sem("lat_sqrt"), n)
                link(v.reciprocal(t, t))
                for k in range(tiles):
                    ins = v.scalar_tensor_tensor(dst[:, k, :], dst[:, k, :], par(vec, k), t, ALU.mult, ALU.mult)
                    if k < tiles - 1:
                        link(ins)
                    else:
                        ins.then_inc(sem(name), 1)
                        dve.wait_ge(sem(name), 1)
            latent("cqss", 1, CQ, 3, QR, "g_cq", "cqn")
            latent("ckvss", 2, CKV, 2, KVR, "g_ckv", "ckvn")
            full(dve, "kr")
            v.tensor_tensor(TR[64:96, 2, :], bank("kr")[64:96], COS[64:96], ALU.mult).then_inc(psum_free[bank_of("kr")], 1)
            drained(dve, "kr")
            full(dve, "krs")
            v.tensor_tensor(TR[64:96, 3, :], bank("krs")[64:96], SIN[64:96], ALU.mult).then_inc(psum_free[bank_of("krs")], 1)
            drained(dve, "krs")
            v.tensor_tensor(K[64:96, 0, :], TR[64:96, 2, :], TR[64:96, 3, :], ALU.add).then_inc(sem("k_rope0"), 1)
            dve.wait_ge(sem("k_rope0"), 1)
            ada_products(4)

            def shift(j):
                drained(dve, f"z{j}")
                raw = RAW[:, j % 4, :]
                link(v.tensor_tensor(ZS[:, j, :], raw[:, 0:S], raw[:, 1:], ALU.subtract))
                v.scalar_tensor_tensor(ZS[:, j, :], ZS[:, j, :], par("mu_shift", j), raw[:, 1:], ALU.mult, ALU.add).then_inc(sem("zs"), 1)
                dve.wait_ge(sem("zs"), j + 1)
            for n in range(3):
                for j in range(4 * n, 4 * n + 4):
                    shift(j)
                ada_take(4 + n)
                ada_products(5 + n)
            shift(12)
            shift(13)
            for t in range(2):
                full(dve, f"qr{t}")
                v.tensor_tensor(TR[:, 2, :], bank(f"qr{t}"), COS, ALU.mult).then_inc(psum_free[bank_of(f"qr{t}")], 1)
                drained(dve, f"qr{t}")
                full(dve, f"qs{t}")
                v.tensor_tensor(TR[:, 3, :], bank(f"qs{t}"), SIN, ALU.mult).then_inc(psum_free[bank_of(f"qs{t}")], 1)
                drained(dve, f"qs{t}")
                for j in range(4):
                    r = slice(32 * j, 32 * j + 32)
                    v.tensor_tensor(Q[64:96, 4 * t + j, :], TR[r, 2, :], TR[r, 3, :], ALU.add).then_inc(sem("q_rope"), 1)
                    dve.wait_ge(sem("q_rope"), 4 * t + j + 1)
            ada_take(7)
            for u in range(len(UNITS) + LAG):
                if u < len(UNITS):
                    hd, q = UNITS[u]
                    full(dve, f"s{hd}_{q}")
                    link(v.tensor_reduce(MX[:, u:u + 1], bank(f"s{hd}_{q}")[:, 0:(q + 1) * P], AX.X, ALU.max))
                    v.tensor_scalar(NMX[:, u:u + 1], MX[:, u:u + 1], -ATT_SCALE, None, ALU.mult).then_inc(sem("row_max"), 1)
                    dve.wait_ge(sem("row_max"), u + 1)
                if 1 <= u <= len(UNITS):
                    w = u - 1
                    hd, q = UNITS[w]
                    drained(dve, f"s{hd}_{q}")
                    p = PR[:, w % NPR, 0:(q + 1) * P]
                    link(v.tensor_reduce(RSUM[:, w:w + 1], p, AX.X, ALU.add))
                    link(v.reciprocal(RINV[:, w:w + 1], RSUM[:, w:w + 1]))
                    v.tensor_scalar(p, p, RINV[:, w:w + 1], None, ALU.mult).then_inc(sem("p_ready"), 1)
                    dve.wait_ge(sem("p_ready"), w + 1)
                if u >= LAG:
                    hd, q = UNITS[u - LAG]
                    if q == NT - 1:
                        full(dve, f"o{hd}")
                        r = slice(64 * (hd % 2), 64 * (hd % 2) + 64)
                        v.tensor_copy(OT[r, hd // 2, :], bank(f"o{hd}")[r]).then_inc(psum_free[bank_of(f"o{hd}")], 1)
                        drained(dve, f"o{hd}")
            for j in range(NJ):
                if j == 0:
                    drained(dve, f"t{HEADS - 1}_{NT - 1}")
                v.tensor_scalar(KK[:, j, :], KZ[:, j, :], par("k_k", j), None, ALU.mult).then_inc(sem("kk0"), 1)
                dve.wait_ge(sem("kk0"), j + 1)
            full(dve, "uw0")
            link(v.memset(RESET, 1.0))
            link(v.memset(RESET.rearrange("p j (c t) -> p (j c) t", t=CH)[:, :, 0:1], 0.0))
            for j in range(NJ):
                drained(dve, f"uw{j}")
                drained(dve, f"ua{j}")
            link(v.tensor_tensor_scan(CUM.rearrange("p j s -> p (j s)"), RESET.rearrange("p j s -> p (j s)"),
                                     SW.rearrange("p j s -> p (j s)"), 0.0, ALU.mult, ALU.add))
            cum = CUM.rearrange("p j (c t) -> p (j c) t", t=CH)
            mid = MID.rearrange("p j c -> p (j c)")
            link(v.tensor_copy(mid.unsqueeze(2), cum[:, :, CH // 2:CH // 2 + 1]))
            link(v.tensor_tensor(cum, cum, mid.unsqueeze(2).to_broadcast([P, NJ * NC, CH]), ALU.subtract))
            link(v.tensor_copy(FDEC.rearrange("p j c -> p (j c)").unsqueeze(2), cum[:, :, CH - 1:CH]))
            v.tensor_tensor(FDEC[:, :, 0:NC - 1], FDEC[:, :, 0:NC - 1], MID[:, :, 1:NC], ALU.add).then_inc(sem("decay"), 1)
            dve.wait_ge(sem("decay"), 1)
            v.tensor_tensor(SW, CUM, SW, ALU.subtract).then_inc(sem("decay"), 1)
            dve.wait_ge(sem("decay"), 2)
            for j in range(NJ):
                drained(dve, f"kss{j}")
                link(v.tensor_scalar(T1[:, j, :], T1[:, j, :], 1e-12, None, ALU.max))
                link(v.reciprocal(T1[:, j, :], T1[:, j, :]))
                ins = v.tensor_tensor(KK[:, j, :], KK[:, j, :], T1[:, j, :], ALU.mult)
                if j < NJ - 1:
                    link(ins)
                else:
                    ins.then_inc(sem("kkn"), 1)
                    dve.wait_ge(sem("kkn"), 1)
            a4 = AR.rearrange("p j c a t -> p (j c) a t")
            fold = lambda x: x.rearrange("p j (c t) -> p (j c) t", t=CH)
            dve.wait_ge(sem("e_a"), 1)
            link(v.scalar_tensor_tensor(a4[:, :, 0, :], fold(KK), -1.0, fold(SW), ALU.mult, ALU.mult))
            link(v.tensor_tensor(KK, KK, AA, ALU.mult))
            dve.wait_ge(sem("e_r"), 1)
            v.tensor_tensor(a4[:, :, 1, :], fold(RZ), fold(T1), ALU.mult).then_inc(sem("r_done"), 1)
            dve.wait_ge(sem("r_done"), 1)
            for j in range(NJ):
                link(v.tensor_scalar(AA[:, j, :], AA[:, j, :], par("k_a", j), OMKA[:, j:j + 1], ALU.mult, ALU.add))
                link(v.tensor_tensor(KZ[:, j, :], KZ[:, j, :], AA[:, j, :], ALU.mult))
                v.scalar_tensor_tensor(RZ[:, j, :], RZ[:, j, :], par("r_k", j), KZ[:, j, :], ALU.mult, ALU.mult).then_inc(sem("rk"), 1)
                dve.wait_ge(sem("rk"), j + 1)
            dve.wait_ge(sem("e_b"), 1)
            link(v.tensor_tensor(BT, KK, T1, ALU.mult))
            link(v.tensor_tensor(KT, KZ, T1, ALU.mult))
            for j in range(NJ):
                full(dve, f"bon{j}")
                v.tensor_tensor(BONUS[:, j, :], bank(f"bon{j}"), VZ[:, j, :], ALU.mult).then_inc(psum_free[bank_of(f"bon{j}")], 1)
                drained(dve, f"bon{j}")
            dve.wait_ge(sem("e_f"), 1)
            for j in range(NJ):
                drained(dve, f"ug{j}")
            v.tensor_copy(MX[:, 0:1], MX[:, 0:1]).then_inc(sem("rwkv_in"), 1)
            dve.wait_ge(sem("rwkv_in"), 1)
            for c in range(NC):
                for g in range(2):
                    for name, dst in (("mr", MR), ("nr", NR)):
                        for n in range(2):
                            job = f"{name}{c}_{g}_{n}"
                            full(dve, job)
                            q = 4 * g + 2 * n
                            v.tensor_tensor(dst[:, q:q + 2, :], bank(job).rearrange("p (h t) -> p h t", h=2), MASK2.rearrange("p a t -> p (a t)").unsqueeze(1).to_broadcast([P, 2, 2 * CH]), ALU.mult).then_inc(psum_free[bank_of(job)], 1)
                            drained(dve, job)
                for l in range(1, LEVELS):
                    for name, dst in (("dx", XI), ("dt", XT)):
                        if name == "dx" and l == LEVELS - 1:
                            continue
                        for g in range(2):
                            job = f"{name}{c}_{l}_{g}"
                            full(dve, job)
                            d = dst[:, 4 * g:4 * g + 4, :].rearrange("p a b -> p (a b)")
                            v.tensor_tensor(d, bank(job), d, ALU.add).then_inc(psum_free[bank_of(job)], 1)
                            drained(dve, job)
                full(dve, f"sa{c}")
                v.tensor_copy(SA.rearrange("p a b -> p (a b)"), bank(f"sa{c}")).then_inc(psum_free[bank_of(f"sa{c}")], 1)
                drained(dve, f"sa{c}")
                if c < NC - 1:
                    job = f"st{c}"
                    full(dve, job)
                    b = bank(job)[:, 0:NJ * VD].rearrange("p (j v) -> p j v", v=VD)
                    f = FDEC[:, :, c:c + 1].to_broadcast([P, NJ, VD])
                    if c == 0:
                        v.tensor_tensor(ST, b, f, ALU.mult).then_inc(psum_free[bank_of(job)], 1)
                        drained(dve, job)
                    else:
                        link(v.tensor_tensor(ST, b, ST, ALU.add))
                        v.tensor_tensor(ST, ST, f, ALU.mult).then_inc(psum_free[bank_of(job)], 1)
                        drained(dve, job)
            for j in range(NJ):
                full(dve, f"gm{j}")
                v.tensor_tensor(YT[:, j, :], YT[:, j, :], bank(f"gm{j}"), ALU.subtract).then_inc(psum_free[bank_of(f"gm{j}")], 1)
                drained(dve, f"gm{j}")
                v.tensor_copy(MX[:, 1:2], MX[:, 1:2]).then_inc(sem("y_c"), 1)
                dve.wait_ge(sem("y_c"), j + 1)
            for j in range(NJ):
                full(dve, f"gv{j}")
                v.tensor_scalar(KK[:, j, :], bank(f"gv{j}"), GN_EPS, None, ALU.add).then_inc(psum_free[bank_of(f"gv{j}")], 1)
                drained(dve, f"gv{j}")
                v.tensor_copy(MX[:, 1:2], MX[:, 1:2]).then_inc(sem("y_var"), 1)
                dve.wait_ge(sem("y_var"), j + 1)
            for j in range(NJ):
                dve.wait_ge(sem("y_sqrt"), j + 1)
                link(v.reciprocal(KK[:, j, :], KK[:, j, :]))
                link(v.tensor_tensor(YT[:, j, :], YT[:, j, :], KK[:, j, :], ALU.mult))
                link(v.tensor_scalar(YT[:, j, :], YT[:, j, :], par("lnx_w", j), par("lnx_b", j), ALU.mult, ALU.add))
                link(v.tensor_tensor(YT[:, j, :], YT[:, j, :], BONUS[:, j, :], ALU.add))
                ins = v.tensor_tensor(YT[:, j, :], YT[:, j, :], G[:, j, :], ALU.mult)
                if j < NJ - 1:
                    link(ins)
                else:
                    ins.then_inc(sem("rwkv_out"), 1)
                    dve.wait_ge(sem("rwkv_out"), 1)
            for hf in range(2):
                ada_products(8 + 2 * hf)
                ada_products(9 + 2 * hf)
                ada_take(8 + 2 * hf)
                for j in range(4):
                    job = f"om{hf}_{j}"
                    full(dve, job)
                    drained(dve, f"gb{hf}_{j}")
                    v.tensor_tensor(GA[:, j, :], bank(job), GA[:, j, :], ALU.mult).then_inc(psum_free[bank_of(job)], 1)
                    drained(dve, job)
                ada_take(9 + 2 * hf)
                for j in range(4):
                    job = f"or{hf}_{j}"
                    full(dve, job)
                    v.tensor_tensor(GB[:, j, :], bank(job), GB[:, j, :], ALU.mult).then_inc(psum_free[bank_of(job)], 1)
                    drained(dve, job)
                    v.tensor_tensor(MIX[:, 4 * hf + j, :], GA[:, j, :], GB[:, j, :], ALU.add).then_inc(sem("mix"), 1)
                    dve.wait_ge(sem("mix"), 4 * hf + j + 1)
            dve.wait_ge(sem("x_landed"), 32)
            for i in range(NT):
                dve.wait_ge(sem("y_ss"), i + 1)
                link(v.tensor_tensor(SS4[:, i:i + 1], SSY[:, 2 * i:2 * i + 1], SSY[:, 2 * i + 1:2 * i + 2], ALU.add))
                v.tensor_scalar(SS4[:, i:i + 1], SS4[:, i:i + 1], 1.0 / D, RMS_EPS, ALU.mult, ALU.add).then_inc(sem("yo_var"), 1)
                dve.wait_ge(sem("yo_var"), i + 1)
                dve.wait_ge(sem("yo_sqrt"), i + 1)
                link(v.reciprocal(SS4[:, i:i + 1], SS4[:, i:i + 1]))
                for n in range(2):
                    job = f"yo{i}_{n}"
                    xs = X[:, i, n * 512:(n + 1) * 512]
                    v.scalar_tensor_tensor(TUP, bank(job), SS4[:, i:i + 1], GROW[:, 0, n * 512:(n + 1) * 512], ALU.mult, ALU.mult).then_inc(psum_free[bank_of(job)], 1)
                    drained(dve, job)
                    ins = v.tensor_tensor(xs, xs, TUP, ALU.add)
                    if n == 0:
                        link(ins)
                    else:
                        ins.then_inc(sem("x1"), 1)
                        dve.wait_ge(sem("x1"), i + 1)
            for i in range(NT):
                dve.wait_ge(sem("x1_ss"), i + 1)
                v.tensor_scalar(SS2[:, i:i + 1], SS2[:, i:i + 1], 1.0 / D, RMS_EPS, ALU.mult, ALU.add).then_inc(sem("x1_var"), 1)
                dve.wait_ge(sem("x1_var"), i + 1)
                dve.wait_ge(sem("x1_sqrt"), i + 1)
                link(v.reciprocal(RS2[:, i:i + 1], RS2[:, i:i + 1]))
                v.tensor_scalar(XN2[:, i, :], X[:, i, :], RS2[:, i:i + 1], None, ALU.mult).then_inc(sem("xn2"), 1)
                dve.wait_ge(sem("xn2"), i + 1)
            for j in range(0, ND, 2):
                full(dve, f"hT{j}")
                v.tensor_scalar(HT[:, j, :], bank(f"hT{j}"), MODA2[:, j:j + 1], MODB2[:, j:j + 1], ALU.mult, ALU.add).then_inc(psum_free[bank_of(f"hT{j}")], 1)
                drained(dve, f"hT{j}")
            for i in range(NT):
                full(dve, f"lg{i}")
                v.tensor_copy(LOGITS[:, i, :], bank(f"lg{i}")[:, 0:36]).then_inc(psum_free[bank_of(f"lg{i}")], 1)
                drained(dve, f"lg{i}")
            gl, el = LOGITS[:, :, 0:NG], LOGITS[:, :, NG:].rearrange("p i (g e) -> p i g e", e=EG)

            def first_max(vals, n, mx, hot):
                link(v.tensor_reduce(mx, vals, AX.X, ALU.max))
                link(v.tensor_tensor(hot, vals, mx.unsqueeze(2).to_broadcast([P, NT, n]), ALU.is_equal))
                link(v.tensor_tensor(hot, hot, RANKW[:, 8 - n:8].unsqueeze(1).to_broadcast([P, NT, n]), ALU.mult))
                link(v.tensor_reduce(TMX, hot, AX.X, ALU.max))
                link(v.tensor_tensor(hot, hot, TMX.unsqueeze(2).to_broadcast([P, NT, n]), ALU.is_equal))
            for n in range(8):
                link(v.memset(RANKW[:, n:n + 1], float(8 - n)))
            first_max(gl, NG, GMX, GHOT)
            v.tensor_tensor(GEXP, gl, GMX.unsqueeze(2).to_broadcast([P, NT, NG]), ALU.subtract).then_inc(sem("gmax"), 1)
            dve.wait_ge(sem("gmax"), 1)
            dve.wait_ge(sem("gexp"), 1)
            link(v.tensor_reduce(PSEL, GEXP, AX.X, ALU.add))
            link(v.reciprocal(PSEL, PSEL))
            for g in range(NG):
                hot = GHOT[:, :, g:g + 1].to_broadcast([P, NT, EG])
                if g == 0:
                    link(v.tensor_tensor(EIN, el[:, :, g, :], hot, ALU.mult))
                else:
                    link(v.tensor_tensor(ETMP, el[:, :, g, :], hot, ALU.mult))
                    link(v.tensor_tensor(EIN, EIN, ETMP, ALU.add))
            first_max(EIN, EG, EMX1, HOT1)
            link(v.scalar_tensor_tensor(ETMP, HOT1, NEG, EIN, ALU.mult, ALU.add))
            first_max(ETMP, EG, EMX2, HOT2)
            v.tensor_tensor(E21, EMX2, EMX1, ALU.subtract).then_inc(sem("emax"), 1)
            dve.wait_ge(sem("emax"), 1)
            dve.wait_ge(sem("eexp"), 1)
            link(v.tensor_scalar(W1, E21, 1.0, None, ALU.add))
            link(v.reciprocal(W1, W1))
            link(v.tensor_tensor(W1, W1, PSEL, ALU.mult))
            link(v.tensor_tensor(E21, E21, W1, ALU.mult))
            dve.wait_ge(sem("route_iota"), 3)
            link(v.tensor_copy(EIDX, EIDI))
            link(v.tensor_copy(BIDX, BIDI))
            for k, hot in enumerate((HOT1, HOT2)):
                for g in range(NG):
                    link(v.tensor_tensor(SEL[:, k, :, g * EG:(g + 1) * EG], hot, GHOT[:, :, g:g + 1].to_broadcast([P, NT, EG]), ALU.mult))
            v.tensor_tensor(SEL[:, 2], SEL[:, 0], SEL[:, 1], ALU.add).then_inc(sem("sel"), 1)
            full(dve, "rank")
            link(v.tensor_copy(RANK.rearrange("p i e -> p (i e)"), bank("rank")[:, 0:NT * NE]))
            v.tensor_copy(CNT, bank("rank")[:, NT * NE:(NT + 1) * NE]).then_inc(psum_free[bank_of("rank")], 1)
            drained(dve, "rank")

            def steps(out_, x, tmp, most):
                link(v.tensor_scalar(out_, x, CAP - 0.5, None, ALU.is_gt))
                for m in range(2, most // CAP + 1):
                    link(v.tensor_scalar(tmp, x, m * CAP - 0.5, None, ALU.is_gt))
                    link(v.tensor_tensor(out_, out_, tmp, ALU.add))
            link(v.tensor_scalar(CNT, CNT, 1.0, None, ALU.subtract))
            steps(EXTRA, CNT, STMP[:, 0, :], S - 1)
            link(v.tensor_scalar(STMP[:, 0, :], EXTRA, 0.0, 1.0, ALU.mult, ALU.add))
            link(v.tensor_tensor_scan(INCL, STMP[:, 0, :], EXTRA, 0.0, ALU.mult, ALU.add))
            link(v.tensor_tensor(EXTRA, INCL, EXTRA, ALU.subtract))
            link(v.tensor_tensor(OVT, INCL.unsqueeze(1).to_broadcast([P, XBLK, NE]), BIDX.unsqueeze(2).to_broadcast([P, XBLK, NE]), ALU.is_le))
            link(v.tensor_reduce(OVS, OVT, AX.X, ALU.add))
            link(v.tensor_scalar(OVS, OVS, NE - 1.0, None, ALU.min))
            link(v.tensor_copy(OVE, OVS))
            v.tensor_copy(OVN, INCL[:, NE - 1:NE]).then_inc(sem("overflow_known"), 1)
            link(v.memset(REC, 0))
            for k, w in enumerate((W1, E21)):
                for src, dst in ((RANK, RK), (EIDX.unsqueeze(1).to_broadcast([P, NT, NE]), EK),
                                 (EXTRA.unsqueeze(1).to_broadcast([P, NT, NE]), XK)):
                    link(v.tensor_tensor(STMP, SEL[:, k], src, ALU.mult))
                    link(v.tensor_reduce(dst, STMP, AX.X, ALU.add))
                steps(QK, RK, QT, S - 1)
                link(v.scalar_tensor_tensor(RK, QK, -float(CAP), RK, ALU.mult, ALU.add))
                link(v.tensor_scalar(XK, XK, NE - 1.0, None, ALU.add))
                link(v.tensor_tensor(XK, XK, QK, ALU.add))
                link(v.tensor_tensor(XK, XK, EK, ALU.subtract))
                link(v.tensor_scalar(QK, QK, 1.0, None, ALU.min))
                link(v.tensor_tensor(XK, XK, QK, ALU.mult))
                link(v.tensor_tensor(XK, XK, EK, ALU.add))
                link(v.scalar_tensor_tensor(RK, RK, float(NBLK), XK, ALU.mult, ALU.add))
                link(v.tensor_copy(ROWI[:, k, :], RK))
                link(v.tensor_copy(REC[:, k, :, 0], TOK4))
                link(v.tensor_scalar(REC[:, k, :, 1], TOK4, 2.0, float(k), ALU.mult, ALU.add))
                link(v.tensor_copy(REC[:, k, :, 2].bitcast(F32), w))
            v.tensor_copy(DUM, XK).then_inc(sem("records"), 1)

            def act_mul(b, s):
                dve.wait_ge(sem("sil_ready"), b + 1)
                v.tensor_tensor(ACTB[:, s, :], ps[:, GU_BANK[s], FF:], SIL[:, s, :], ALU.mult).then_inc(sem("act_ready"), 1)

            def take_act(b, s):
                dve.wait_ge(sem("at_full"), b + 1)
                v.tensor_copy(ACTT[:, s].rearrange("p k t -> p (k t)"), ps[:, 4, 0:2 * P]).then_inc(sem("at_free"), 1)

            def take_y(b, s):
                dve.wait_ge(sem("dn_full"), b * 2 + 1)
                dve.wait_ge(sem("sr_ready"), b + 1)
                v.tensor_scalar(YB[:, s, 0:512], ps[:, 5, :], SR[:, s, 2:3].bitcast(F32), None, ALU.mult).then_inc(sem("dn_free0"), 1)
            act_mul(0, 0)
            with dve.Fori(0, 10) as i:
                for j in range(3):
                    b, s = i * 3 + 1 + j, (1 + j) % 3
                    take_act(b - 1, j)
                    act_mul(b, s)
                    take_y(b - 1, j)
            take_act(30, 0)
            act_mul(31, 1)
            take_y(30, 0)
            take_act(31, 1)
            take_y(31, 1)
            more = dve.value_load(OVN[0:1, 0:1], min_val=0, max_val=XBLK)
            with dve.If(more > 0):
                with dve.Fori(0, XBLK) as i:
                    b = i + NE
                    act_mul(b, 0)
                    take_act(b, 0)
                    take_y(b, 0)
            for i in range(NT):
                dve.wait_ge(sem(f"rows_landed{i}"), 16)
                v.tensor_tensor(YS[:, i, :], YL[:, i, 0, :], YL[:, i, 1, :], ALU.add).then_inc(sem("y_fin"), 1)
            dve.wait_ge(sem("fin_ss"), 1)
            v.tensor_scalar(SS, SS, 1.0 / D, RMS_EPS, ALU.mult, ALU.add).then_inc(sem("fin_var"), 1)
            dve.wait_ge(sem("fin_var"), 1)
            dve.wait_ge(sem("fin_sqrt"), 1)
            link(v.reciprocal(SS, SS))
            for i in range(NT):
                link(v.scalar_tensor_tensor(YS[:, i, :], YS[:, i, :], SS[:, i:i + 1], GROW[:, 1, :], ALU.mult, ALU.mult))
                v.tensor_tensor(X[:, i, :], X[:, i, :], YS[:, i, :], ALU.add).then_inc(sem("out_ready"), 1)
                dve.wait_ge(sem("out_ready"), i + 1)


_INS = ['x', 'c', 'positions', 'w_ada', 'b_ada', 'g_pre_mix', 'g_post_mix', 'g_pre_ffn', 'g_post_ffn',
        'w_in', 'g_cq', 'w_uq', 'g_ckv', 'w_ukv', 'w_o_mla', 'mu_shift', 'w_decay_up', 'decay_bias',
        'w_a_up', 'a_bias', 'w_g_up', 'k_k', 'k_a', 'r_k', 'lnx_w', 'lnx_b', 'w_o_rwkv', 'w_out',
        'w_router_group', 'b_router_group', 'w_router_expert', 'b_router_expert',
        'w_exp_gate', 'w_exp_up', 'w_exp_down']


def kernel(**inputs):
    import numpy as _np
    import concourse.bacc as _bacc
    from concourse import mybir as _mybir
    from concourse.bass_utils import run_bass_kernel_spmd as _run

    nc = _bacc.Bacc("TRN2", target_bir_lowering=False, num_devices=1)
    arrays, aps = {}, {}
    for name in _INS:
        a = _np.ascontiguousarray(inputs[name])
        arrays[f"in_{name}"] = a
        aps[name] = nc.dram_tensor(f"in_{name}", a.shape, _mybir.dt.from_np(a.dtype), kind="ExternalInput").ap()
    freq = _np.tile((ROPE_THETA ** (-_np.arange(0, ROPE, 2) / ROPE)).astype(_np.float32), 128 // (ROPE // 2))[None, :]
    arrays["rope_inv_freq"] = freq
    aps["inv_freq"] = nc.dram_tensor("rope_inv_freq", freq.shape, _mybir.dt.float32, kind="ExternalInput").ap()
    out = nc.dram_tensor("out_0", (1, S, D), _mybir.dt.float32, kind="ExternalOutput").ap()
    layer(nc, aps, out)
    r = _run(nc, [arrays], core_ids=[0])
    return r.results[0]["out_0"]
```

```python
import math
from contextlib import ExitStack

import numpy as np

import concourse.bass as bass
from concourse import mybir

F32 = mybir.dt.float32
I32 = mybir.dt.int32
U32 = mybir.dt.uint32
ALU = mybir.AluOpType
ACT = mybir.ActivationFunctionType
AX = mybir.AxisListType

P = 128
S = 512
D = 1024
NT = S // P
ND = D // P
HEADS = 8
NOPE, ROPE, VD = 64, 32, 64
QR, KVR = 384, 256
RW = 512
NJ = RW // P
ZR = 3 * RW + 64 + 64 + 128
NZ = ZR // P
C_CKV, C_KR, C_ZR = QR, QR + KVR, QR + KVR + ROPE
C_GATE = C_ZR + ZR
NE, NG, EG, FF = 32, 4, 8, 256
ATT_SCALE = 1.0 / math.sqrt(NOPE + ROPE)
RMS_EPS, GN_EPS = 1e-6, 64e-5
DECAY = -math.exp(-0.5)
CH = 128
NC = S // CH
LEVELS = 7
LAG = 3
CAP = 64
XPAIR = (2 * S - 1) // CAP // 2 + 1
XBLK = 2 * XPAIR
NP1 = NE // 2
NPAIR = NP1 + XPAIR
FAR = 1 << 20
NEG = -1e30
ROPE_THETA = 10000.0
ROUND = 1.5 * 2.0 ** 23
TWO_PI = 2 * math.pi

ROWS = {}
_at = 0
for _n, _k in (("b_ada", 48), ("g_pre_mix", 8), ("g_pre_ffn", 8), ("c", 8), ("g_cq", 3), ("g_ckv", 2),
               ("mu_shift", 14), ("decay_bias", 4), ("a_bias", 4), ("k_k", 4), ("k_a", 4), ("r_k", 4),
               ("lnx_w", 4), ("lnx_b", 4), ("inv_freq", 1)):
    ROWS[_n] = (_at, _k)
    _at += _k
NROWS = _at


def two_pi_parts():
    def short(x, bits):
        m, e = math.frexp(x)
        return math.ldexp(round(m * 2 ** bits) / 2 ** bits, e)
    a = short(TWO_PI, 11)
    b = short(TWO_PI - a, 11)
    return a, b, float(np.float32(TWO_PI - a - b))


def job_list():
    jobs = ["par", "ada0", "ada1", "ada2", "ada3"]
    jobs += [f"xT{j}" for j in range(ND)]
    jobs += ["cq0", "cq1", "cq2", "ckv0", "cqss", "ckv1", "kr", "ckvss", "krs"]
    jobs += [f"z{j}" for j in range(0, 4)] + ["ada4"]
    jobs += [f"z{j}" for j in range(4, 8)] + ["ada5"]
    jobs += [f"z{j}" for j in range(8, 12)] + ["ada6"]
    jobs += ["z12", "z13"]
    for t in range(2):
        jobs += [f"qr{t}", f"qs{t}"]
    jobs += [f"qn{j}" for j in range(4)] + [f"kn{j}" for j in range(4)] + [f"v{i}" for i in range(NT)]
    jobs += ["ada7"]
    units = [(h, q) for h in range(HEADS) for q in range(NT)]
    for u in range(len(units) + LAG):
        if u < len(units):
            jobs.append("s%d_%d" % units[u])
        if u >= LAG:
            h, q = units[u - LAG]
            jobs.append(f"t{h}_{q}")
            if q == NT - 1:
                jobs.append(f"o{h}")
    for name in ("uw", "ua", "kss", "ug", "bon"):
        jobs += [f"{name}{j}" for j in range(NJ)]
    for c in range(NC):
        for g in range(2):
            jobs += [f"mr{c}_{g}_{b}" for b in range(2)]
            jobs += [f"nr{c}_{g}_{b}" for b in range(2)]
        jobs += [f"tok{c}_{n}" for n in range(3)]
        jobs += [f"x{c}_{g}" for g in range(2)]
        for l in range(1, LEVELS):
            jobs += [f"p{c}_{l}_{g}" for g in range(2)]
            if l < LEVELS - 1:
                jobs += [f"dx{c}_{l}_{g}" for g in range(2)]
            jobs += [f"dt{c}_{l}_{g}" for g in range(2)]
        jobs += [f"rhs{c}_{g}" for g in range(2)] + [f"sa{c}"] + [f"y{c}_{g}" for g in range(2)]
        if c < NC - 1:
            jobs += [f"st{c}"]
    jobs += [f"gm{j}" for j in range(NJ)] + [f"gv{j}" for j in range(NJ)]
    for hf in range(2):
        for k in ("ga", "gb", "om", "or"):
            jobs += [f"{k}{hf}_{j}" for j in range(4)]
            if k == "gb":
                jobs.append(f"ada{8 + hf}")
    for i in range(NT):
        jobs += [f"yo{i}_{n}" for n in range(2)]
        if i == 1:
            jobs += ["ada10", "ada11"]
    jobs += [f"hT{j}" for j in range(ND)] + ["lgT", "lg", "rank"]
    return jobs


def layer(nc, I, out):
    JOBS = {n: i for i, n in enumerate(job_list())}
    TP1, TP2, TP3 = two_pi_parts()

    with ExitStack() as ctx:
        arena = ctx.enter_context(nc.sbuf_tensor("arena", [P, 206 * 256], F32))
        XD = nc.dram_tensor("normed_tokens", [S, D], F32).ap()
        YD = nc.dram_tensor("expert_rows", [2 * S, D], F32).ap()
        TABD = nc.dram_tensor("block_table", [P * NPAIR, 4], I32).ap()
        ps = ctx.enter_context(nc.psum_tensor("ps", [P, 8, 512], F32))

        def at(kb, *shape):
            n = 1
            for s in shape:
                n *= s
            v = arena[:, int(kb * 256):int(kb * 256) + n]
            if len(shape) == 1:
                return v
            names = [chr(97 + i) for i in range(len(shape))]
            return v.rearrange(f"p ({' '.join(names)}) -> p {' '.join(names)}", **dict(zip(names, shape)))

        sems = {}

        def sem(name):
            if name not in sems:
                sems[name] = ctx.enter_context(nc.semaphore(name))
            return sems[name]

        psum_full = [sem(f"psum_full{b}") for b in range(8)]
        psum_free = [sem(f"psum_free{b}") for b in range(8)]

        SLOT, NSLOT = 16, 3

        HT = at(48, ND, S)
        X = at(64, NT, D)
        SQ = at(64, 5, S)
        Q, K, V = at(64, HEADS, S), at(80, HEADS, S), at(96, NT, RW)
        CQ, CKV = at(104, 3, S), at(110, 2, S)
        OT = at(118, NJ, S)
        ZS = at(126, NZ, S)
        RAW = at(154, 4, S + 1)
        PROWS = at(104, P)
        IDXP, IDXF, IDXX = (at(k, P).bitcast(I32) for k in (104.5, 105, 105.5))
        POSI = at(106, S).bitcast(I32)
        ACC = at(163, 2, S)
        ACC2 = at(110, 2, S)
        TR = at(167, 5, S)
        SWK = at(180, 8, 32)
        COS, SIN = at(181, S), at(183, S)
        NPR = 4
        PR, PT = at(161, NPR, S), at(169, 2, NT, S)
        AR = at(64, NJ, NC, 2, CH)
        CUM = KT = at(80, NJ, S)
        RESET = BT = at(88, NJ, S)
        G, SW, AA = at(96, NJ, S), at(104, NJ, S), at(154, NJ, S)
        T1, KK = at(163, NJ, S), at(171, NJ, S)
        RZ, KZ, VZ = ZS[:, 0:4], ZS[:, 4:8], ZS[:, 8:12]
        XI, XT, SA = at(104, HEADS, CH), at(108, HEADS, CH), at(112, HEADS, VD)
        BTOK, KTOK, VTOK, ST = at(114, RW), at(116, RW), at(150, RW), at(152, NJ, VD)
        TOK = [BTOK, KTOK, VTOK]
        MOFF = at(154, 2, HEADS, CH)
        MR, NR = at(163, HEADS, 2 * CH), at(171, HEADS, 2 * CH)
        P1, RHS = at(179, HEADS, CH), at(183, HEADS, VD)
        BONUS, YT = RZ, KZ
        GA, GB, MIX = at(163, 4, S), at(171, 4, S), at(80, ND, S)
        XN2, YS, JUNK = at(128, NT, D), at(128, NT, D), at(104, D)
        TUP = at(108, S)
        MODW = at(144, ND, S)
        NB = 4
        XG, HG, YB = at(48, 2, D), at(144, 2, ND, P), at(156, 2, D)
        SIL, ACTB, ACTT = at(152, 2, FF), at(154, 2, FF), at(56, 2, 2, P)
        WG = [at(k, ND, 2, FF) for k in (0, 24, 80, 104)]
        WD = [at(k + 16, 2, D) for k in (0, 24, 80, 104)]
        HALF = (slice(0, CAP), slice(CAP, 2 * CAP))
        X_BANKS, GU_BANK, DN_BANK, AT_BANK = (0, 1), (2, 3), (4, 5), 6
        YL = at(0, NT, 2, D)
        IDENT, XU, MASKS, MASK2 = at(185, P), at(185.5, P), at(186, LEVELS, P), at(189.5, 2, P)
        BO, BOM, ONES, PAR = at(190.5, P), at(191, P), at(191.5, P), at(192, P)
        GROW = at(192.5, 2, D)
        COLS = at(200.5, 160)
        MODA1, MODB1, MODA2, MODB2 = (COLS[:, 8 * i:8 * i + 8] for i in range(4))
        OMKA, SS2, RS2, SIGN = COLS[:, 32:36], COLS[:, 36:40], COLS[:, 40:44], COLS[:, 44:45]
        SSY, SS4 = COLS[:, 48:56], COLS[:, 56:60]
        SILC, SS, RSTD = COLS[:, 64:72], COLS[:, 72:76], COLS[:, 76:80]
        RSUM, RINV = COLS[:, 96:128], COLS[:, 128:160]
        WR = at(201.25, ND, 36)
        MX, NMX = at(202.5, 32), at(202.75, 32)
        MID, FDEC = at(203, NJ, NC), at(203.25, NJ, NC)
        BR = at(204, 36)
        LOGITS = at(163, NT, 36)
        GHOT, GEXP = at(164, NT, NG), at(164.25, NT, NG)
        EIN, ETMP, HOTS = at(164.5, NT, EG), at(164.75, NT, EG), at(165, 2, NT, EG)
        HOT1, HOT2 = HOTS[:, 0], HOTS[:, 1]
        GMX, PSEL, EMX1, EMX2, TMX = (at(165.5 + 0.0625 * k, NT) for k in range(5))
        W12 = at(165.875, 2, NT)
        W1, E21 = W12[:, 0], W12[:, 1]
        RANKW = at(166, 8)
        LT = at(176, S)
        SEL = at(170, 3, NT, NE)
        RANK, CNT = at(171.5, NT, NE), at(172, NE)
        EXTRA, INCL, EIDX, UNIT = at(172.25, NE), at(172.5, NE), at(172.75, NE), at(173, NE)
        STMP = at(168, 2, NT, NE)
        RK, EK, XK, QK, HK = (at(173.5 + 0.03125 * k, 2, NT) for k in range(5))
        OVT, OVS, BIDX = at(174, XBLK, NE), at(182, XBLK), at(182.25, XBLK)
        OVE, OVN, OVA = at(182.5, XBLK).bitcast(I32), at(182.9375, 1).bitcast(I32), at(182.75, XBLK).bitcast(I32)
        TOK4, EIDI, BIDI = at(183, 2, NT).bitcast(I32), at(183.25, NE).bitcast(I32), at(183.5, XBLK).bitcast(I32)
        REC = at(184, 2, NT, 4).bitcast(I32)
        ROWI = at(184.25, 2, NT).bitcast(I32)
        GI, SR = at(184.375, 2, 4).bitcast(I32), at(184.5, 2, 4).bitcast(I32)
        TAB = at(166.25, NPAIR, 4).bitcast(I32)
        DEFT = at(179, NPAIR, 4).bitcast(I32)

        def par(v, j=None):
            a, k = ROWS[v]
            return PAR[:, a:a + k] if j is None else PAR[:, a + j:a + j + 1]

        def wsrc(w, c0, n, k=ND):
            return w[:, c0:c0 + n].rearrange("(k p) n -> p k n", p=P)
        W = {n: I[n][0] for n in ("w_ada", "w_in", "w_uq", "w_ukv", "w_o_mla", "w_o_rwkv", "w_out")}
        items = [(f"ada{c}", "dve", wsrc(W["w_ada"], 512 * c, 512)) for c in range(4)]
        items += [("cq", "pe", wsrc(W["w_in"], 0, 384)), ("kv", "pe", wsrc(W["w_in"], C_CKV, 288)),
                  ("ada4", "dve", wsrc(W["w_ada"], 2048, 512)),
                  ("r", "pe", wsrc(W["w_in"], C_ZR, 512)), ("ada5", "dve", wsrc(W["w_ada"], 2560, 512)),
                  ("k", "pe", wsrc(W["w_in"], C_ZR + 512, 512)), ("ada6", "dve", wsrc(W["w_ada"], 3072, 512)),
                  ("vv", "pe", wsrc(W["w_in"], C_ZR + 1024, 512)), ("ada7", "dve", wsrc(W["w_ada"], 3584, 512)),
                  ("wag", "pe", wsrc(W["w_in"], C_ZR + 1536, 256)),
                  ("uq", "pe", wsrc(W["w_uq"], 0, 768)), ("ukv", "pe", wsrc(W["w_ukv"], 0, 1024))]
        items += [("ups", "pe", None)]
        def half(name, hf):
            c0 = 512 * hf
            return {"ga": (f"ga{hf}", "pe", wsrc(W["w_in"], C_GATE + c0, 512)),
                    "gb": (f"gb{hf}", "pe", wsrc(W["w_in"], C_GATE + D + c0, 512)),
                    "oo": (f"oo{hf}", "pe", (wsrc(W["w_o_mla"], c0, 512), wsrc(W["w_o_rwkv"], c0, 512))),
                    "wo": (f"wo{hf}", "pe", wsrc(W["w_out"], c0, 512))}[name]
        items += [half(name, hf) for hf in range(2) for name in ("ga", "gb", "oo")]
        items += [half("wo", hf) for hf in range(2)]
        SEQ = {n: i for i, (n, _, _) in enumerate(items)}
        NPARTS = {"uq": 12, "ukv": 4, "ups": 3, "oo0": 2, "oo1": 2}
        landed = []
        slot_count = [0] * NSLOT
        for i, (n, _, _) in enumerate(items):
            slot_count[i % NSLOT] += 16 * NPARTS.get(n, 1)
            landed.append(slot_count[i % NSLOT])

        def wbuf(name, *shape):
            return at(SLOT * (SEQ[name] % NSLOT), *shape)

        def wait_weights(eng, name):
            i = SEQ[name]
            eng.wait_ge(sem(f"w_landed{i % NSLOT}"), landed[i])

        def full(eng, job):
            n = JOBS[job]
            eng.wait_ge(psum_full[n % 8], n // 8 + 1)

        def bank_of(job):
            return JOBS[job] % 8

        def bank(job):
            return ps[:, JOBS[job] % 8, :]

        block = ctx.enter_context(nc.Block())


        LAST_JOB = {"cq": "cq2", "kv": "krs", "r": "z3", "k": "z7", "vv": "z11", "wag": "z13", "uq": "qn3",
                    "ukv": "v3", "ups": "ug3", "ga0": "ga0_3", "ga1": "ga1_3", "gb0": "gb0_3", "gb1": "gb1_3",
                    "oo0": "or0_3", "oo1": "or1_3", "wo0": "yo3_0", "wo1": "yo3_1"}
        UNITS = [(h, q) for h in range(HEADS) for q in range(NT)]
        BASE = [sum(1 for n in JOBS.values() if n % 8 == b) for b in range(8)]

        def drained(eng, job):
            n = JOBS[job]
            eng.wait_ge(psum_free[n % 8], n // 8 + 1)

        def flat(name):
            v = I[name]
            return v.rearrange("a h c -> a (h c)") if len(v.shape) == 3 else v

        @block.sync
        def _(sp):
            load_first = lambda c: sp.dma_start(wbuf(f"ada{c}", ND, 512), items[c][2]).then_inc(sem(f"w_landed{c}"), 16)
            load_first(0)
            for name, (a, k) in ROWS.items():
                sp.dma_start(PROWS[a:a + k, :], flat(name).rearrange("a (k p) -> (a k) p", p=P)).then_inc(sem("rows_landed"), 16)
            sp.dma_start(POSI, I["positions"].partition_broadcast(P).rearrange("p a s -> p (a s)")).then_inc(sem("pos_landed"), 16)
            load_first(1)
            sp.dma_start(X, I["x"][0].rearrange("(i p) d -> p i d", p=P)).then_inc(sem("x_landed"), 16)

            def load_modulation(c):
                if c == 8:
                    full(sp, f"y{NC - 1}_1")
                else:
                    sp.wait_ge(sem("ada_ready"), c)
                sp.dma_start(MODW, wsrc(W["w_ada"], 512 * c, 512)).then_inc(sem("modw_landed"), 16)
            for i, (name, who, src) in enumerate(items):
                if i < 2:
                    continue
                if i >= NSLOT:
                    before = items[i - NSLOT][0]
                    if items[i - NSLOT][1] == "pe":
                        full(sp, LAST_JOB[before])
                    else:
                        sp.wait_ge(sem("ada_ready"), int(before[3:]) + 1)
                landed_sem = sem(f"w_landed{i % NSLOT}")
                if name == "ups":
                    u = wbuf(name, 2, 512)
                    sp.dma_start(u[0:64, 0, :], I["w_decay_up"][0]).then_inc(landed_sem, 16)
                    sp.dma_start(u[64:128, 0, :], I["w_a_up"][0]).then_inc(landed_sem, 16)
                    sp.dma_start(u[:, 1, :], I["w_g_up"][0]).then_inc(landed_sem, 16)
                elif name == "uq":
                    u, w4 = wbuf(name, 3, 1024), src.rearrange("p k (h c) -> p k h c", h=HEADS)
                    for k in range(3):
                        for dst, c0, n in ((u[:, k, 0:256].rearrange("p (h c) -> p h c", h=HEADS), 64, 32),
                                           (u[:, k, 256:512].rearrange("p (h c) -> p h c", h=HEADS)[:, :, 0:16], 80, 16),
                                           (u[:, k, 256:512].rearrange("p (h c) -> p h c", h=HEADS)[:, :, 16:32], 64, 16),
                                           (u[:, k, 512:1024].rearrange("p (h c) -> p h c", h=HEADS), 0, 64)):
                            sp.dma_start(dst, w4[:, k, :, c0:c0 + n]).then_inc(landed_sem, 16)
                elif name == "ukv":
                    u, w4 = wbuf(name, 2, 2, 512), src.rearrange("p k (h c) -> p k h c", h=HEADS)
                    for k in range(2):
                        for n in range(2):
                            sp.dma_start(u[:, k, n, :].rearrange("p (h c) -> p h c", h=HEADS),
                                         w4[:, k, :, 64 * n:64 * n + 64]).then_inc(landed_sem, 16)
                elif name[:2] == "oo":
                    u = wbuf(name, 2, 4, 512)
                    for n in range(2):
                        sp.dma_start(u[:, n], src[n]).then_inc(landed_sem, 16)
                else:
                    sp.dma_start(wbuf(name, src.shape[1], src.shape[2]), src).then_inc(landed_sem, 16)
                if name in ("oo0", "ga1", "oo1", "wo1"):
                    load_modulation({"oo0": 8, "ga1": 9, "oo1": 10, "wo1": 11}[name])
                if name == "ada3":
                    sp.dma_start(GROW[:, 0, :], I["g_post_mix"].partition_broadcast(P).rearrange("p a s -> p (a s)")).then_inc(sem("grow_landed"), 16)
                    sp.dma_start(GROW[:, 1, :], I["g_post_ffn"].partition_broadcast(P).rearrange("p a s -> p (a s)")).then_inc(sem("grow_landed"), 16)
                    sp.dma_start(WR[:, :, 0:NG], wsrc(I["w_router_group"][0], 0, NG)).then_inc(sem("wr_landed"), 16)
                    sp.dma_start(WR[:, :, NG:], wsrc(I["w_router_expert"][0], 0, NE)).then_inc(sem("wr_landed"), 16)
                    sp.dma_start(BR[0:1, 0:NG], I["b_router_group"]).then_inc(sem("wr_landed"), 16)
                    sp.dma_start(BR[0:1, NG:], I["b_router_expert"]).then_inc(sem("wr_landed"), 16)
            full(sp, f"y{NC - 1}_1")
            sp.dma_start(X, I["x"][0].rearrange("(i p) d -> p i d", p=P)).then_inc(sem("x_landed"), 16)

            def load_gate_up(e, s, landed_sem):
                for n, w in enumerate(("w_exp_gate", "w_exp_up")):
                    sp.dma_start(WG[s][:, :, n, :], I[w][0, bass.ds(e, 1)].rearrange("a (k p) n -> p (a k) n", p=P)).then_inc(sem(landed_sem), 16)

            def load_down(e, s, landed_sem):
                sp.dma_start(WD[s], I["w_exp_down"][0, bass.ds(e, 1)].rearrange("a (k p) n -> p (a k) n", p=P)).then_inc(sem(landed_sem), 16)
            full(sp, "yo3_1")
            for b in range(3):
                load_gate_up(b, b, f"gate_landed{b}")
                load_down(b, b, f"down_landed{b}")
            sp.wait_ge(sem("table_default"), 1)
            sp.dma_start(TABD.rearrange("(p b) c -> p b c", p=P), DEFT).then_inc(sem("table_cleared"), 16)
            for i in range(NT):
                sp.wait_ge(sem("xn2"), i + 1)
                sp.dma_start(XD[i * P:(i + 1) * P, :], XN2[:, i, :]).then_inc(sem("xn_stored"), 16)
            full(sp, "ada11")
            load_gate_up(3, 3, "gate_landed3")
            load_down(3, 3, "down_landed3")
            sp.wait_ge(sem("table_filled"), 16 * 2 * NT)
            sp.dma_start(TAB, TABD.rearrange("(p b) c -> p b c", p=P)).then_inc(sem("table_landed"), 16)

            def load_pair(m, s):
                sp.wait_ge(sem("gu_full"), m * 2 - 3)
                load_gate_up(m * 2, s, f"gate_landed{s}")
                sp.wait_ge(sem("gu_full"), m * 2 - 2)
                load_gate_up(m * 2 + 1, s + 1, f"gate_landed{s + 1}")
                sp.wait_ge(sem("dn_full"), m * 2 - 2)
                load_down(m * 2, s, f"down_landed{s}")
                load_down(m * 2 + 1, s + 1, f"down_landed{s + 1}")
            with sp.Fori(0, NE // NB - 1) as i:
                load_pair(i * 2 + 2, 0)
                load_pair(i * 2 + 3, 2)
            sp.wait_ge(sem("overflow_known"), 1)
            more = sp.value_load(OVN[0:1, 0:1], min_val=0, max_val=XBLK)
            with sp.If(more > 0):
                with sp.Fori(0, XPAIR) as i:
                    active = sp.value_load(OVA[0:1, bass.ds(i, 1)], min_val=0, max_val=1)
                    with sp.If(active > 0):
                        sp.wait_ge(sem("dn_full"), i * 2 + 2 * NP1)
                        for n in range(2):
                            e = sp.value_load(OVE[0:1, bass.ds(i * 2 + n, 1)], min_val=0, max_val=NE - 1)
                            load_gate_up(e, n, "more_weights_landed")
                            load_down(e, n, "more_weights_landed")
            sp.wait_ge(sem("rows_stored"), 1)
            for i in range(NT):
                sp.dma_start(YL[:, i, :, :], YD[2 * P * i:2 * P * (i + 1), :].rearrange("(p c) d -> p c d", c=2)).then_inc(sem(f"rows_landed{i}"), 16)
            for i in range(NT):
                sp.wait_ge(sem("out_ready"), i + 1)
                sp.dma_start(out[0, i * P:(i + 1) * P, :], X[:, i, :]).then_inc(sem("out_stored"), 16)
            sp.wait_ge(sem("out_stored"), 16 * NT)

        @block.gpsimd
        def _(pool):
            step = [0]

            def link(ins):
                step[0] += 1
                ins.then_inc(sem("pool_step"), 1)
                pool.wait_ge(sem("pool_step"), step[0])

            nc.gpsimd.iota(IDXP, [[0, P]], base=0, channel_multiplier=1).then_inc(sem("iota"), 1)
            pool.wait_ge(sem("iota"), 1)
            nc.gpsimd.iota(IDXF, [[1, P]], base=0, channel_multiplier=0).then_inc(sem("iota"), 1)
            pool.wait_ge(sem("iota"), 2)
            nc.gpsimd.memset(ONES, 1.0).then_inc(sem("ones"), 1)
            pool.wait_ge(sem("ones"), 1)
            link(nc.gpsimd.memset(RAW[:, :, 0:1], 0.0))
            wait_weights(pool, "kv")
            kv = wbuf("kv", ND, 288)
            link(nc.gpsimd.tensor_copy(SWK[:, :, 0:16], kv[:, :, 272:288]))
            nc.gpsimd.tensor_copy(SWK[:, :, 16:32], kv[:, :, 256:272]).then_inc(sem("swk"), 1)
            pool.wait_ge(sem("swk"), 1)
            full(pool, "z0")
            link(nc.gpsimd.memset(Q[96:100], 1.0))
            link(nc.gpsimd.affine_select(out=Q[96:100], in_=Q[96:100], compare_op=ALU.is_ge, fill=0.0, base=0,
                                        pattern=[[0, HEADS], [1, S]], channel_multiplier=-P))
            link(nc.gpsimd.affine_select(out=Q[96:100], in_=Q[96:100], compare_op=ALU.is_ge, fill=0.0, base=63,
                                        pattern=[[0, HEADS], [-1, S]], channel_multiplier=P))
            link(nc.gpsimd.memset(K[96:100], NEG))
            link(nc.gpsimd.affine_select(out=K[96:100], in_=K[96:100], compare_op=ALU.is_ge, fill=0.0, base=-64,
                                        pattern=[[0, HEADS], [1, S]], channel_multiplier=-P))
            nc.gpsimd.affine_select(out=K[96:100], in_=K[96:100], compare_op=ALU.is_ge, fill=0.0, base=127, pattern=[[0, HEADS], [-1, S]], channel_multiplier=P).then_inc(sem("chunk_mask"), 1)
            pool.wait_ge(sem("chunk_mask"), 1)
            pool.wait_ge(sem("k_rope0"), 1)
            nc.gpsimd.tensor_copy(K[64:96, 1:HEADS, :], K[64:96, 0:1, :].to_broadcast([32, HEADS - 1, S])).then_inc(sem("k_rope"), 1)
            pool.wait_ge(sem("k_rope"), 1)
            for j in range(NJ):
                pool.wait_ge(sem("kk0"), j + 1)
            pool.wait_ge(sem("decay"), 1)
            for j in range(NJ):
                drained(pool, f"ua{j}")
                link(nc.gpsimd.tensor_scalar(RESET[:, j, :], AA[:, j, :], par("k_a", j), OMKA[:, j:j + 1], ALU.mult, ALU.add))
                nc.gpsimd.tensor_tensor(KZ[:, j, :], KZ[:, j, :], RESET[:, j, :], ALU.mult).then_inc(sem("k_scaled"), 1)
                pool.wait_ge(sem("k_scaled"), j + 1)
            for c in range(NC):
                if c > 0:
                    full(pool, f"sa{c - 1}")
                for g in range(2):
                    drained(pool, f"mr{c}_{g}_0")
                    drained(pool, f"mr{c}_{g}_1")
                    mt = MR[:, 4 * g:4 * g + 4, 0:CH]
                    xt = XT[:, 4 * g:4 * g + 4, :]
                    link(nc.gpsimd.tensor_tensor(xt, mt, MASKS[:, 0:1, :].to_broadcast([P, 4, CH]), ALU.mult))
                    nc.gpsimd.tensor_tensor(xt, xt, IDENT.unsqueeze(1).to_broadcast([P, 4, CH]), ALU.add).then_inc(sem("xt_start"), 1)
                    pool.wait_ge(sem("xt_start"), 2 * c + g + 1)
                for l in range(1, LEVELS):
                    for g in range(2):
                        if l > 2:
                            full(pool, f"p{c}_{l - 2}_{g}")
                        nc.gpsimd.tensor_tensor(MOFF[:, l % 2, 4 * g:4 * g + 4, :], MR[:, 4 * g:4 * g + 4, 0:CH], MASKS[:, l:l + 1, :].to_broadcast([P, 4, CH]), ALU.mult).then_inc(sem("moff"), 1)
                        pool.wait_ge(sem("moff"), 2 * ((LEVELS - 1) * c + l - 1) + g + 1)
            full(pool, "hT0")
            nc.gpsimd.iota(TOK4, [[0, 2], [P, NT]], base=0, channel_multiplier=1).then_inc(sem("route_iota"), 1)
            nc.gpsimd.iota(EIDI, [[1, NE]], base=0, channel_multiplier=0).then_inc(sem("route_iota"), 1)
            nc.gpsimd.iota(BIDI, [[1, XBLK]], base=0, channel_multiplier=0).then_inc(sem("route_iota"), 1)
            nc.gpsimd.iota(DEFT, [[4, NPAIR], [1, 4]], base=FAR, channel_multiplier=4 * NPAIR).then_inc(sem("table_default"), 1)
            full(pool, "lgT")
            link(nc.gpsimd.memset(XG, 0.0))
            pool.wait_ge(sem("records"), 1)
            pool.wait_ge(sem("table_cleared"), 16)
            for k in range(2):
                for i in range(NT):
                    nc.gpsimd.indirect_dma_start(TABD, bass.IndirectOffsetOnAxis(ap=ROWI[:, k, i:i + 1].bitcast(U32), axis=0),
                                                 REC[:, k, i, :], None).then_inc(sem("table_filled"), 16)
            pool.wait_ge(sem("table_landed"), 16)
            pool.wait_ge(sem("xn_stored"), 16 * NT)

            def gather(m, s, landed_sem):
                link_to(nc.gpsimd.tensor_copy(GI[:, s, :], TAB[:, m, :]), "gi", m)
                nc.gpsimd.indirect_dma_start(XG[:, s, :], None, XD, bass.IndirectOffsetOnAxis(ap=GI[:, s, 0:1].bitcast(U32), axis=0),
                                             bounds_check=S - 1, oob_is_err=False).then_inc(sem(landed_sem), 16)

            def record(m, s):
                link_to(nc.gpsimd.tensor_copy(SR[:, s, :], TAB[:, m, :]), "sr_ready", m)

            def link_to(ins, name, m):
                ins.then_inc(sem(name), 1)
                pool.wait_ge(sem(name), m + 1)

            def scatter(m, s, stored_sem):
                for n in range(2):
                    pool.wait_ge(sem(f"dn_free{n}"), m + 1)
                nc.gpsimd.indirect_dma_start(YD, bass.IndirectOffsetOnAxis(ap=SR[:, s, 1:2].bitcast(U32), axis=0), YB[:, s, :], None,
                                             bounds_check=2 * S - 1, oob_is_err=False).then_inc(sem(stored_sem), 16)
            for m in range(2):
                gather(m, m, f"xg_landed{m}")
                record(m, m)
            for m in range(2, NP1):
                pool.wait_ge(sem("xp_full"), 2 * m - 2)
                gather(m, m % 2, f"xg_landed{m % 2}")
                scatter(m - 2, m % 2, f"yb_stored{m % 2}")
                pool.wait_ge(sem(f"yb_stored{m % 2}"), 16 * (m // 2))
                record(m, m % 2)
            for m in (NP1 - 2, NP1 - 1):
                scatter(m, m % 2, f"yb_stored{m % 2}")
            for s in range(2):
                pool.wait_ge(sem(f"yb_stored{s}"), 16 * (NP1 // 2))
            more = pool.value_load(OVN[0:1, 0:1], min_val=0, max_val=XBLK)
            with pool.If(more > 0):
                for i in range(XPAIR):
                    m = NP1 + i
                    active = pool.value_load(OVA[0:1, i:i + 1], min_val=0, max_val=1)
                    with pool.If(active > 0):
                        pool.wait_ge(sem("xp_full"), 2 * m)
                        gather(m, 0, "more_landed")
                        record(m, 0)
                        scatter(m, 0, "more_stored")
                        pool.wait_ge(sem("more_stored"), 16 * i + 16)
            nc.gpsimd.tensor_copy(GI[:, 0, 3:4], GI[:, 0, 2:3]).then_inc(sem("rows_stored"), 1)

        @block.tensor
        def _(pe):
            T = nc.tensor
            state = {"n": 0}

            def fill(job):
                n = JOBS[job]
                assert n == state["n"], (job, n, state["n"])
                state["n"] += 1
                if n >= 8:
                    pe.wait_ge(psum_free[n % 8], n // 8)
                return ps[:, n % 8, :]

            def project(job, lhs, rhs, n_k, o=None):
                b = fill(job)
                o = b if o is None else o(b)
                for k in range(n_k):
                    mm = T.matmul(o, lhs(k), rhs(k), start=(k == 0), stop=(k == n_k - 1))
                mm.then_inc(psum_full[bank_of(job)], 1)

            def ada(c):
                job = f"ada{c}"
                b = fill(job)
                pe.wait_ge(sem("ada_ready"), c + 1)
                a = (ACC if c < 8 else ACC2)[:, c % 2, :]
                if c in (4, 5, 10, 11):
                    mm = T.matmul(b, ONES, a, start=True, stop=False)
                    for n in range(4):
                        mm = T.matmul(b[:, n * P:(n + 1) * P], par("b_ada", 4 * c + n).to_broadcast([P, P]), IDENT,
                                      start=False, stop=(n == 3))
                else:
                    for n in range(4):
                        mm = T.matmul(b[:, n:n + 1], a[:, n * P:(n + 1) * P], ONES[:, 0:1], start=True, stop=True)
                mm.then_inc(psum_full[bank_of(job)], 1)

            pe.wait_ge(sem("rows_landed"), 16 * len(ROWS))
            pe.wait_ge(sem("masks"), 1)
            b = fill("par")
            mm = T.transpose(b[:, 0:NROWS], PROWS[0:NROWS, :], IDENT[0:NROWS, 0:NROWS])
            mm.then_inc(psum_full[bank_of("par")], 1)
            pe.wait_ge(sem("ones"), 1)
            for c in range(4):
                ada(c)
            pe.wait_ge(sem("xn"), NT)
            for j in range(ND):
                b = fill(f"xT{j}")
                for i in range(NT):
                    mm = T.transpose(b[:, i * P:(i + 1) * P], X[:, i, j * P:(j + 1) * P], IDENT)
                mm.then_inc(psum_full[bank_of(f"xT{j}")], 1)
            for j in range(ND):
                drained(pe, f"xT{j}")
            h = lambda k: HT[:, k, :]
            wait_weights(pe, "cq")
            w = wbuf("cq", ND, 384)
            for t in range(3):
                project(f"cq{t}", lambda k: w[:, k, t * P:(t + 1) * P], h, ND)
            wait_weights(pe, "kv")
            wk = wbuf("kv", ND, 288)
            project("ckv0", lambda k: wk[:, k, 0:P], h, ND)
            for t in range(3):
                drained(pe, f"cq{t}")
            project("cqss", lambda k: ONES, lambda k: SQ[:, k, :], 3)
            project("ckv1", lambda k: wk[:, k, P:2 * P], h, ND)
            project("kr", lambda k: wk[:, k, 256:288], h, ND, lambda b: b[64:96, :])
            for t in range(2):
                drained(pe, f"ckv{t}")
            project("ckvss", lambda k: ONES, lambda k: SQ[:, 3 + k, :], 2)
            pe.wait_ge(sem("swk"), 1)
            project("krs", lambda k: SWK[:, k, :], h, ND, lambda b: b[64:96, :])
            for n, name in enumerate(("r", "k", "vv")):
                wait_weights(pe, name)
                w = wbuf(name, ND, 512)
                for t in range(4):
                    project(f"z{4 * n + t}", lambda k: w[:, k, t * P:(t + 1) * P], h, ND)
                ada(4 + n)
            wait_weights(pe, "wag")
            w = wbuf("wag", ND, 256)
            for t in range(2):
                project(f"z{12 + t}", lambda k: w[:, k, t * P:(t + 1) * P], h, ND)
            pe.wait_ge(sem("cqn"), 1)
            wait_weights(pe, "uq")
            uq = wbuf("uq", 3, 1024)
            for t in range(2):
                project(f"qr{t}", lambda k: uq[:, k, P * t:P * t + P], lambda k: CQ[:, k, :], 3)
                project(f"qs{t}", lambda k: uq[:, k, 256 + P * t:256 + P * t + P], lambda k: CQ[:, k, :], 3)
            for j in range(4):
                project(f"qn{j}", lambda k: uq[:, k, 512 + P * j:512 + P * j + P], lambda k: CQ[:, k, :], 3)
            pe.wait_ge(sem("ckvn"), 1)
            wait_weights(pe, "ukv")
            ukv = wbuf("ukv", 2, 2, 512)
            for j in range(4):
                project(f"kn{j}", lambda k: ukv[:, k, 0, P * j:P * j + P], lambda k: CKV[:, k, :], 2)
            for i in range(NT):
                project(f"v{i}", lambda k: CKV[:, k, i * P:(i + 1) * P], lambda k: ukv[:, k, 1, :], 2)
            ada(7)
            pe.wait_ge(sem("q_rope"), 8)
            pe.wait_ge(sem("k_rope"), 1)
            pe.wait_ge(sem("chunk_mask"), 1)
            for j in range(4):
                drained(pe, f"qn{j}")
                drained(pe, f"kn{j}")
                drained(pe, f"v{j}")
            for u in range(len(UNITS) + LAG):
                if u < len(UNITS):
                    hd, q = UNITS[u]
                    project(f"s{hd}_{q}", lambda k: Q[0:100, hd, q * P:(q + 1) * P],
                            lambda k: K[0:100, hd, 0:(q + 1) * P], 1, lambda b: b[:, 0:(q + 1) * P])
                if u >= LAG:
                    hd, q = UNITS[u - LAG]
                    b = fill(f"t{hd}_{q}")
                    pe.wait_ge(sem("p_ready"), u - LAG + 1)
                    for kb in range(q + 1):
                        mm = T.transpose(b[:, kb * P:(kb + 1) * P], PR[:, (u - LAG) % NPR, kb * P:(kb + 1) * P], IDENT)
                    mm.then_inc(psum_full[bank_of(f"t{hd}_{q}")], 1)
                    if q == NT - 1:
                        b = fill(f"o{hd}")
                        drained(pe, f"t{hd}_{q}")
                        r = slice(64 * (hd % 2), 64 * (hd % 2) + 64)
                        for kb in range(NT):
                            mm = T.matmul(b[r, kb * P:], V[:, kb, hd * VD:(hd + 1) * VD], PT[:, hd % 2, kb, kb * P:],
                                          start=(kb == 0), stop=(kb == NT - 1))
                        mm.then_inc(psum_full[bank_of(f"o{hd}")], 1)
            wait_weights(pe, "ups")
            up = wbuf("ups", 2, 512)
            pe.wait_ge(sem("lowrank"), 2)
            for j in range(NJ):
                project(f"uw{j}", lambda k: up[0:64, 0, j * P:(j + 1) * P], lambda k: ZS[0:64, 12, :], 1)
            for j in range(NJ):
                project(f"ua{j}", lambda k: up[64:128, 0, j * P:(j + 1) * P], lambda k: ZS[64:128, 12, :], 1)
            for j in range(NJ):
                pe.wait_ge(sem("kk_sq"), j + 1)
                project(f"kss{j}", lambda k: BO, lambda k: T1[:, j, :], 1)
            for j in range(NJ):
                project(f"ug{j}", lambda k: up[:, 1, j * P:(j + 1) * P], lambda k: ZS[:, 13, :], 1)
            for j in range(NJ):
                pe.wait_ge(sem("rk"), j + 1)
                project(f"bon{j}", lambda k: BO, lambda k: RZ[:, j, :], 1)
            pe.wait_ge(sem("rwkv_in"), 1)
            for c in range(NC):
                cs = slice(c * CH, (c + 1) * CH)
                for g in range(2):
                    r = slice(64 * g, 64 * g + 64)
                    for name, src in (("mr", BT), ("nr", KT)):
                        for n in range(2):
                            b = fill(f"{name}{c}_{g}_{n}")
                            for m in range(2):
                                j = 2 * n + m
                                mm = T.matmul(b[:, m * 256:(m + 1) * 256], src[r, j, cs],
                                              AR[r, j, c, :, :].rearrange("p a t -> p (a t)"), start=True, stop=True)
                            mm.then_inc(psum_full[bank_of(f"{name}{c}_{g}_{n}")], 1)
                for n, src in enumerate((BT, KT, VZ)):
                    b = fill(f"tok{c}_{n}")
                    for j in range(NJ):
                        mm = T.transpose(b[:, j * P:(j + 1) * P], src[:, j, cs], IDENT)
                    mm.then_inc(psum_full[bank_of(f"tok{c}_{n}")], 1)
                for g in range(2):
                    b = fill(f"x{c}_{g}")
                    pe.wait_ge(sem("xt_start"), 2 * c + g + 1)
                    for j in range(4):
                        mm = T.transpose(b[:, j * P:(j + 1) * P], XT[:, 4 * g + j, :], IDENT)
                    mm.then_inc(psum_full[bank_of(f"x{c}_{g}")], 1)

                def stage(job, g, lhs, rhs):
                    b = fill(job)
                    for j in range(4):
                        mm = T.matmul(b[:, j * P:(j + 1) * P], lhs[:, 4 * g + j, :], rhs[:, 4 * g + j, :], start=True, stop=True)
                    mm.then_inc(psum_full[bank_of(job)], 1)
                for l in range(1, LEVELS):
                    for g in range(2):
                        pe.wait_ge(sem("moff"), 2 * ((LEVELS - 1) * c + l - 1) + g + 1)
                        drained(pe, f"x{c}_{g}" if l == 1 else f"dx{c}_{l - 1}_{g}")
                        stage(f"p{c}_{l}_{g}", g, MOFF[:, l % 2], XI)
                    if l < LEVELS - 1:
                        for g in range(2):
                            drained(pe, f"p{c}_{l}_{g}")
                            if l > 1:
                                drained(pe, f"dt{c}_{l - 1}_{g}")
                            stage(f"dx{c}_{l}_{g}", g, XT, P1)
                    for g in range(2):
                        drained(pe, f"p{c}_{l}_{g}")
                        if l > 1:
                            drained(pe, f"dt{c}_{l - 1}_{g}")
                        stage(f"dt{c}_{l}_{g}", g, P1, XT)
                for n in range(3):
                    drained(pe, f"tok{c}_{n}")
                for g in range(2):
                    r = slice(64 * g, 64 * g + 64)
                    b = fill(f"rhs{c}_{g}")
                    if c > 0:
                        drained(pe, f"st{c - 1}")
                        for j in range(4):
                            T.matmul(b[:, j * 64:j * 64 + 64], AR[r, j, c, 0, :], ST[r, j, :], start=(j == 0),
                                     stop=False, skip_group_check=True)
                    for j in range(4):
                        hd = 2 * j + g
                        mm = T.matmul(b[:, j * 64:j * 64 + 64], NR[:, 4 * g + j, 0:CH], VTOK[:, hd * 64:hd * 64 + 64],
                                      start=(c == 0), stop=True, skip_group_check=c > 0)
                    mm.then_inc(psum_full[bank_of(f"rhs{c}_{g}")], 1)
                b = fill(f"sa{c}")
                for g in range(2):
                    drained(pe, f"rhs{c}_{g}")
                    drained(pe, f"dt{c}_{LEVELS - 1}_{g}")
                    for j in range(4):
                        q = 4 * g + j
                        mm = T.matmul(b[:, q * 64:q * 64 + 64], XT[:, q, :], RHS[:, q, :], start=True, stop=True)
                mm.then_inc(psum_full[bank_of(f"sa{c}")], 1)
                drained(pe, f"sa{c}")
                for g in range(2):
                    r = slice(64 * g, 64 * g + 64)
                    b = fill(f"y{c}_{g}")
                    if c > 0:
                        for j in range(4):
                            T.matmul(b[r, j * P:(j + 1) * P], ST[r, j, :], AR[r, j, c, 1, :], start=(j == 0), stop=False,
                                     skip_group_check=True)
                    for j in range(4):
                        q, hd = 4 * g + j, 2 * j + g
                        T.matmul(b[r, j * P:(j + 1) * P], SA[:, q, :], MR[:, q, CH:], start=(c == 0), stop=False,
                                 skip_group_check=c > 0)
                        mm = T.matmul(b[r, j * P:(j + 1) * P], VTOK[:, hd * 64:hd * 64 + 64], NR[:, q, CH:], start=False,
                                      stop=True, skip_group_check=c > 0)
                    mm.then_inc(psum_full[bank_of(f"y{c}_{g}")], 1)
                if c < NC - 1:
                    b = fill(f"st{c}")
                    for g in range(2):
                        for j in range(4):
                            q, hd = 4 * g + j, 2 * j + g
                            o = b[64 * g:64 * g + 64, j * 64:j * 64 + 64]
                            T.matmul(o, BTOK[:, hd * 64:hd * 64 + 64], SA[:, q, :], start=True, stop=False)
                            mm = T.matmul(o, KTOK[:, hd * 64:hd * 64 + 64], VTOK[:, hd * 64:hd * 64 + 64], start=False, stop=True)
                    mm.then_inc(psum_full[bank_of(f"st{c}")], 1)
            for g in range(2):
                drained(pe, f"y{NC - 1}_{g}")
            for j in range(NJ):
                project(f"gm{j}", lambda k: BOM, lambda k: YT[:, j, :], 1)
            for j in range(NJ):
                pe.wait_ge(sem("y_sq"), j + 1)
                project(f"gv{j}", lambda k: BOM, lambda k: T1[:, j, :], 1)
            for hf in range(2):
                for name in ("ga", "gb"):
                    wait_weights(pe, f"{name}{hf}")
                    w = wbuf(f"{name}{hf}", ND, 512)
                    for j in range(4):
                        project(f"{name}{hf}_{j}", lambda k: w[:, k, j * P:(j + 1) * P], h, ND)
                ada(8 + hf)
                wait_weights(pe, f"oo{hf}")
                w = wbuf(f"oo{hf}", 2, 4, 512)
                for j in range(4):
                    project(f"om{hf}_{j}", lambda k: w[:, 0, k, j * P:(j + 1) * P], lambda k: OT[:, k, :], NJ)
                pe.wait_ge(sem("rwkv_out"), 1)
                for j in range(4):
                    project(f"or{hf}_{j}", lambda k: w[:, 1, k, j * P:(j + 1) * P], lambda k: YT[:, k, :], NJ)
            for n in range(2):
                wait_weights(pe, f"wo{n}")
            pe.wait_ge(sem("mix"), 8)
            for i in range(NT):
                for n in range(2):
                    w = wbuf(f"wo{n}", ND, 512)
                    project(f"yo{i}_{n}", lambda k: MIX[:, k, i * P:(i + 1) * P], lambda k: w[:, k, :], ND)
                if i == 1:
                    ada(10)
                    ada(11)
            hb = {}
            for j in range(ND):
                hb[j] = fill(f"hT{j}")
                for i in range(NT - 1):
                    if j == 0:
                        pe.wait_ge(sem("xn2"), i + 1)
                    T.transpose(hb[j][:, i * P:(i + 1) * P], XN2[:, i, j * P:(j + 1) * P], IDENT)
            pe.wait_ge(sem("xn2"), NT)
            for j in range(ND):
                T.transpose(hb[j][:, (NT - 1) * P:], XN2[:, NT - 1, j * P:(j + 1) * P], IDENT).then_inc(psum_full[bank_of(f"hT{j}")], 1)
            pe.wait_ge(sem("wr_landed"), 64)
            lt = fill("lgT")[0:36, :]
            for k in range(ND):
                drained(pe, f"hT{k}")
                T.matmul(lt, WR[:, k, :], HT[:, k, :], start=(k == 0), stop=False, skip_group_check=True)
            mm = T.matmul(lt, BR[0:1, 0:36], ONES[0:1, 0:1].to_broadcast([1, S]), start=False, stop=True, skip_group_check=True)
            mm.then_inc(psum_full[bank_of("lgT")], 1)
            b = fill("lg")
            drained(pe, "lgT")
            for i in range(NT):
                mm = T.transpose(b[:, i * 36:(i + 1) * 36], LT[0:36, i * P:(i + 1) * P], IDENT[0:36, 0:36])
            mm.then_inc(psum_full[bank_of("lg")], 1)
            b = fill("rank")
            pe.wait_ge(sem("sel"), 1)
            sel = SEL[:, 2].rearrange("p i e -> p (i e)")
            T.matmul(b[:, 0:NT * NE], MASK2[:, 0, :], sel, start=True, stop=False, skip_group_check=True)
            for m in range(1, NT + 1):
                mm = T.matmul(b[:, m * NE:(NT + 1) * NE], ONES, sel[:, 0:(NT + 1 - m) * NE], start=False, stop=(m == NT), skip_group_check=True)
            mm.then_inc(psum_full[bank_of("rank")], 1)
            for n in range(8):
                pe.wait_ge(psum_free[n], BASE[n])

            def xp(m, s, first=False):
                for n in range(2):
                    if not first:
                        pe.wait_ge(sem("xp_free"), m * 2 + n - 1)
                    for k in range(4):
                        mm = T.transpose(ps[:, X_BANKS[n], k * P:(k + 1) * P], XG[:, s, (4 * n + k) * P:(4 * n + k + 1) * P], IDENT)
                    mm.then_inc(sem("xp_full"), 1)

            def gu(m, s, h):
                for k in range(ND):
                    mm = T.matmul(ps[HALF[h], GU_BANK[s // 2 % 2], :], HG[:, s // 2, k, HALF[h]], WG[s + h][:, k].rearrange("p a n -> p (a n)"),
                                  start=(k == 0), stop=(k == ND - 1))
                mm.then_inc(sem("gu_full"), 1)

            def at_(m, p):
                pe.wait_ge(sem("act_ready"), m + 1)
                for k in range(2):
                    mm = T.transpose(ps[:, AT_BANK, k * P:(k + 1) * P], ACTB[:, p, k * P:(k + 1) * P], IDENT)
                mm.then_inc(sem("at_full"), 1)

            def dn(m, s, first=False):
                pe.wait_ge(sem("at_free"), m + 1)
                for n in range(2):
                    if not first:
                        pe.wait_ge(sem(f"dn_free{n}"), m)
                    for h in range(2):
                        for k in range(2):
                            mm = T.matmul(ps[HALF[h], DN_BANK[n], :], ACTT[:, s // 2, k, HALF[h]], WD[s + h][:, k, n * 512:(n + 1) * 512],
                                          start=(k == 0), stop=(k == 1))
                    mm.then_inc(sem("dn_full"), 1)

            def pair(m, s, landed, rows, first=False, second=False):
                pe.wait_ge(sem("xp_free"), m * 2 + 2)
                pe.wait_ge(sem(f"gate_landed{s}"), landed * 2)
                gu(m, s, 0)
                if not first:
                    at_(m - 1, 1 - s // 2)
                    for h in range(2):
                        pe.wait_ge(sem(f"down_landed{2 - s + h}"), landed if s else landed - 16)
                    dn(m - 1, 2 - s, second)
                if rows is not None:
                    pe.wait_ge(sem(f"xg_landed{1 - s // 2}"), rows)
                    xp(m + 1, 1 - s // 2)
                pe.wait_ge(sem(f"gate_landed{s + 1}"), landed * 2)
                gu(m, s, 1)
            pe.wait_ge(sem("xg_landed0"), 16)
            xp(0, 0, True)
            pair(0, 0, 16, 16, first=True)
            pair(1, 2, 16, 32, second=True)
            with pe.Fori(0, NE // NB - 2) as i:
                pair(i * 2 + 2, 0, i * 16 + 32, i * 16 + 32)
                pair(i * 2 + 3, 2, i * 16 + 32, i * 16 + 48)
            pair(NP1 - 2, 0, 4 * NE, 8 * NP1)
            pair(NP1 - 1, 2, 4 * NE, None)
            at_(NP1 - 1, 1)
            for s in (2, 3):
                pe.wait_ge(sem(f"down_landed{s}"), 4 * NE)
            dn(NP1 - 1, 2)
            pe.wait_ge(sem("overflow_known"), 1)
            more = pe.value_load(OVN[0:1, 0:1], min_val=0, max_val=XBLK)
            with pe.If(more > 0):
                with pe.Fori(0, XPAIR) as i:
                    active = pe.value_load(OVA[0:1, bass.ds(i, 1)], min_val=0, max_val=1)
                    with pe.If(active > 0):
                        m = i + NP1
                        pe.wait_ge(sem("more_landed"), i * 16 + 16)
                        xp(m, 0)
                        pe.wait_ge(sem("more_weights_landed"), i * 96 + 96)
                        pe.wait_ge(sem("xp_free"), m * 2 + 2)
                        gu(m, 0, 0)
                        gu(m, 0, 1)
                        at_(m, 0)
                        dn(m, 0)

        @block.scalar
        def _(act):
            step = [0]

            def link(ins):
                step[0] += 1
                ins.then_inc(sem("act_step"), 1)
                act.wait_ge(sem("act_step"), step[0])

            A = nc.scalar.activation
            drained(act, "par")
            A(SILC, par("c"), ACT.Silu).then_inc(sem("silc"), 1)
            act.wait_ge(sem("silc"), 1)
            for i in range(NT):
                if i == 0:
                    act.wait_ge(sem("x_landed"), 16)
                link(A(K[:, 0:2, :].rearrange("p a s -> p (a s)"), X[:, i, :], ACT.Square, accum_out=SS[:, i:i + 1]))
            nc.scalar.copy(SS[:, 0:4], SS[:, 0:4]).then_inc(sem("x_ss"), 1)
            act.wait_ge(sem("x_ss"), 1)
            act.wait_ge(sem("x_var"), 1)
            A(RSTD, SS, ACT.Sqrt).then_inc(sem("x_sqrt"), 1)
            act.wait_ge(sem("x_sqrt"), 1)
            act.wait_ge(sem("x_rstd"), 1)
            for i in range(NT):
                nc.scalar.activation(X[:, i, :], X[:, i, :], ACT.Copy, scale=RSTD[:, i:i + 1]).then_inc(sem("xn"), 1)
                act.wait_ge(sem("xn"), i + 1)
            drained(act, "ada3")
            for j in range(1, ND, 2):
                full(act, f"xT{j}")
                A(HT[:, j, :], bank(f"xT{j}"), ACT.Identity, bias=MODB1[:, j:j + 1], scale=MODA1[:, j:j + 1]).then_inc(psum_free[bank_of(f"xT{j}")], 1)
                drained(act, f"xT{j}")

            for k, t in enumerate((SIN, COS)):
                act.wait_ge(sem("angle"), k + 1)
                A(t, t, ACT.Sin).then_inc(sem("sincos"), 1)
                act.wait_ge(sem("sincos"), k + 1)

            def latent(name, tiles, dst, sq0, n):
                for t in range(tiles):
                    job = f"{name}{t}"
                    full(act, job)
                    link(nc.scalar.copy(dst[:, t, :], bank(job)))
                    A(SQ[:, sq0 + t, :], bank(job), ACT.Square).then_inc(psum_free[bank_of(job)], 1)
                    drained(act, job)
                act.wait_ge(sem("lat_var"), n)
                A(TR[:, n - 1, :], TR[:, n - 1, :], ACT.Sqrt).then_inc(sem("lat_sqrt"), 1)
                act.wait_ge(sem("lat_sqrt"), n)
            latent("cq", 3, CQ, 0, 1)
            latent("ckv", 2, CKV, 3, 2)
            for j in range(NZ):
                full(act, f"z{j}")
                if j >= 4:
                    act.wait_ge(sem("zs"), j - 3)
                nc.scalar.copy(RAW[:, j % 4, 1:], bank(f"z{j}")).then_inc(psum_free[bank_of(f"z{j}")], 1)
                drained(act, f"z{j}")
            act.wait_ge(sem("zs"), 13)
            A(ZS[0:64, 12, :], ZS[0:64, 12, :], ACT.Tanh).then_inc(sem("lowrank"), 1)
            act.wait_ge(sem("lowrank"), 1)
            act.wait_ge(sem("zs"), 14)
            A(ZS[:, 13, :], ZS[:, 13, :], ACT.Sigmoid).then_inc(sem("lowrank"), 1)
            act.wait_ge(sem("lowrank"), 2)
            for name, dst in (("qn", Q), ("kn", K)):
                for j in range(4):
                    full(act, f"{name}{j}")
                    b = bank(f"{name}{j}")
                    link(nc.scalar.copy(dst[0:64, 2 * j, :], b[0:64, :]))
                    nc.scalar.copy(dst[0:64, 2 * j + 1, :], b[64:128, :]).then_inc(psum_free[bank_of(f"{name}{j}")], 1)
                    drained(act, f"{name}{j}")
            for i in range(NT):
                full(act, f"v{i}")
                nc.scalar.copy(V[:, i, :], bank(f"v{i}")).then_inc(psum_free[bank_of(f"v{i}")], 1)
                drained(act, f"v{i}")
            for u in range(len(UNITS) + LAG):
                if u < len(UNITS):
                    hd, q = UNITS[u]
                    job = f"s{hd}_{q}"
                    n = (q + 1) * P
                    act.wait_ge(sem("row_max"), u + 1)
                    if u >= NPR:
                        full(act, "t%d_%d" % UNITS[u - NPR])
                    A(PR[:, u % NPR, 0:n], bank(job)[:, 0:n], ACT.Exp, bias=NMX[:, u:u + 1], scale=ATT_SCALE,
                      accum_out=RSUM[:, u:u + 1]).then_inc(psum_free[bank_of(job)], 1)
                    drained(act, job)
                if u >= LAG:
                    hd, q = UNITS[u - LAG]
                    job = f"t{hd}_{q}"
                    full(act, job)
                    if q == 0 and hd >= 2:
                        full(act, f"o{hd - 2}")
                    nc.scalar.copy(PT[:, hd % 2, 0:q + 1, q * P:(q + 1) * P], bank(job)[:, 0:(q + 1) * P].rearrange("p (k t) -> p k t", t=P)).then_inc(psum_free[bank_of(job)], 1)
                    drained(act, job)
            def gate(name, dst, vec):
                for j in range(NJ):
                    job = f"{name}{j}"
                    full(act, job)
                    A(dst[:, j, :], bank(job), ACT.Sigmoid, bias=par(vec, j)).then_inc(psum_free[bank_of(job)], 1)
                    drained(act, job)
            gate("uw", SW, "decay_bias")
            for j in range(NJ):
                act.wait_ge(sem("kk0"), j + 1)
                A(T1[:, j, :], KK[:, j, :], ACT.Square).then_inc(sem("kk_sq"), 1)
                act.wait_ge(sem("kk_sq"), j + 1)
            gate("ua", AA, "a_bias")
            for j in range(NJ):
                full(act, f"kss{j}")
                A(T1[:, j, :], bank(f"kss{j}"), ACT.Sqrt).then_inc(psum_free[bank_of(f"kss{j}")], 1)
                drained(act, f"kss{j}")
            for j in range(NJ):
                full(act, f"ug{j}")
                nc.scalar.copy(G[:, j, :], bank(f"ug{j}")).then_inc(psum_free[bank_of(f"ug{j}")], 1)
                drained(act, f"ug{j}")
            act.wait_ge(sem("decay"), 1)
            A(FDEC, FDEC, ACT.Exp, scale=DECAY).then_inc(sem("e_f"), 1)
            act.wait_ge(sem("e_f"), 1)
            act.wait_ge(sem("decay"), 2)
            A(SW, SW, ACT.Exp, scale=DECAY).then_inc(sem("e_a"), 1)
            act.wait_ge(sem("e_a"), 1)
            act.wait_ge(sem("kkn"), 1)
            A(T1, CUM, ACT.Exp, scale=DECAY).then_inc(sem("e_r"), 1)
            act.wait_ge(sem("e_r"), 1)
            act.wait_ge(sem("r_done"), 1)
            A(T1, CUM, ACT.Exp, scale=-DECAY).then_inc(sem("e_b"), 1)
            act.wait_ge(sem("e_b"), 1)

            for c in range(NC):
                for n in range(3):
                    full(act, f"tok{c}_{n}")
                    nc.scalar.copy(TOK[n], bank(f"tok{c}_{n}")).then_inc(psum_free[bank_of(f"tok{c}_{n}")], 1)
                    drained(act, f"tok{c}_{n}")
                for g in range(2):
                    full(act, f"x{c}_{g}")
                    nc.scalar.copy(XI[:, 4 * g:4 * g + 4].rearrange("p a b -> p (a b)"), bank(f"x{c}_{g}")).then_inc(psum_free[bank_of(f"x{c}_{g}")], 1)
                    drained(act, f"x{c}_{g}")
                for l in range(1, LEVELS):
                    for g in range(2):
                        job = f"p{c}_{l}_{g}"
                        full(act, job)
                        nc.scalar.copy(P1[:, 4 * g:4 * g + 4].rearrange("p a b -> p (a b)"), bank(job)).then_inc(psum_free[bank_of(job)], 1)
                        drained(act, job)
                for g in range(2):
                    job = f"rhs{c}_{g}"
                    full(act, job)
                    nc.scalar.copy(RHS[:, 4 * g:4 * g + 4].rearrange("p a b -> p (a b)"), bank(job)[:, 0:256]).then_inc(psum_free[bank_of(job)], 1)
                    drained(act, job)
                for g in range(2):
                    job = f"y{c}_{g}"
                    full(act, job)
                    r = slice(64 * g, 64 * g + 64)
                    nc.scalar.copy(YT[r, :, c * CH:(c + 1) * CH], bank(job)[r].rearrange("p (j t) -> p j t", t=CH)).then_inc(psum_free[bank_of(job)], 1)
                    drained(act, job)
            for j in range(NJ):
                act.wait_ge(sem("y_c"), j + 1)
                A(T1[:, j, :], YT[:, j, :], ACT.Square).then_inc(sem("y_sq"), 1)
                act.wait_ge(sem("y_sq"), j + 1)
            for j in range(NJ):
                act.wait_ge(sem("y_var"), j + 1)
                A(KK[:, j, :], KK[:, j, :], ACT.Sqrt).then_inc(sem("y_sqrt"), 1)
                act.wait_ge(sem("y_sqrt"), j + 1)
            act.wait_ge(sem("rwkv_out"), 1)
            for hf in range(2):
                for name, dst in (("ga", GA), ("gb", GB)):
                    for j in range(4):
                        job = f"{name}{hf}_{j}"
                        full(act, job)
                        if hf:
                            act.wait_ge(sem("mix"), j + 1)
                        A(dst[:, j, :], bank(job), ACT.Sigmoid).then_inc(psum_free[bank_of(job)], 1)
                        drained(act, job)
            for i in range(NT + 1):
                if i < NT:
                    for n in range(2):
                        job = f"yo{i}_{n}"
                        full(act, job)
                        link(A(JUNK[:, n * 512:(n + 1) * 512], bank(job), ACT.Square, accum_out=SSY[:, 2 * i + n:2 * i + n + 1]))
                    nc.scalar.copy(SS4[:, i:i + 1], SSY[:, 2 * i:2 * i + 1]).then_inc(sem("y_ss"), 1)
                    act.wait_ge(sem("y_ss"), i + 1)
                    act.wait_ge(sem("yo_var"), i + 1)
                    A(SS4[:, i:i + 1], SS4[:, i:i + 1], ACT.Sqrt).then_inc(sem("yo_sqrt"), 1)
                    act.wait_ge(sem("yo_sqrt"), i + 1)
                if i > 0:
                    act.wait_ge(sem("x1"), i)
                    link(A(JUNK, X[:, i - 1, :], ACT.Square, accum_out=SS2[:, i - 1:i]))
                    nc.scalar.copy(SS2[:, i - 1:i], SS2[:, i - 1:i]).then_inc(sem("x1_ss"), 1)
                    act.wait_ge(sem("x1_ss"), i)
                    act.wait_ge(sem("x1_var"), i)
                    A(RS2[:, i - 1:i], SS2[:, i - 1:i], ACT.Sqrt).then_inc(sem("x1_sqrt"), 1)
                    act.wait_ge(sem("x1_sqrt"), i)
            for j in range(1, ND, 2):
                full(act, f"hT{j}")
                A(HT[:, j, :], bank(f"hT{j}"), ACT.Identity, bias=MODB2[:, j:j + 1], scale=MODA2[:, j:j + 1]).then_inc(psum_free[bank_of(f"hT{j}")], 1)
                drained(act, f"hT{j}")
            act.wait_ge(sem("gmax"), 1)
            A(GEXP, GEXP, ACT.Exp).then_inc(sem("gexp"), 1)
            act.wait_ge(sem("gexp"), 1)
            act.wait_ge(sem("emax"), 1)
            A(E21, E21, ACT.Exp).then_inc(sem("eexp"), 1)
            act.wait_ge(sem("eexp"), 1)

            def silu(m, p):
                act.wait_ge(sem("gu_full"), m * 2 + 2)
                A(SIL[:, p, :], ps[:, GU_BANK[p], 0:FF], ACT.Silu).then_inc(sem("sil_ready"), 1)

            def take_x(m, s):
                for n in range(2):
                    act.wait_ge(sem("xp_full"), m * 2 + n + 1)
                    for k in range(4 * n, 4 * n + 4):
                        ins = A(HG[:, s, k, :], ps[:, X_BANKS[n], (k % 4) * P:(k % 4 + 1) * P], ACT.Identity, bias=MODB2[:, k:k + 1],
                                scale=MODA2[:, k:k + 1])
                    ins.then_inc(sem("xp_free"), 1)

            def take_y(m, p):
                act.wait_ge(sem("dn_full"), m * 2 + 2)
                act.wait_ge(sem("sr_ready"), m + 1)
                A(YB[:, p, 512:], ps[:, DN_BANK[1], :], ACT.Copy, scale=SR[:, p, 2:3].bitcast(F32)).then_inc(sem("dn_free1"), 1)

            def pair(m, p):
                silu(m, p)
                take_y(m, p)
                take_x(m + 2, p)
            take_x(0, 0)
            take_x(1, 1)
            with act.Fori(0, NE // NB - 1) as i:
                pair(i * 2, 0)
                pair(i * 2 + 1, 1)
            for m in (NP1 - 2, NP1 - 1):
                silu(m, m % 2)
                take_y(m, m % 2)
            act.wait_ge(sem("overflow_known"), 1)
            more = act.value_load(OVN[0:1, 0:1], min_val=0, max_val=XBLK)
            with act.If(more > 0):
                with act.Fori(0, XPAIR) as i:
                    active = act.value_load(OVA[0:1, bass.ds(i, 1)], min_val=0, max_val=1)
                    with act.If(active > 0):
                        m = i + NP1
                        take_x(m, 0)
                        silu(m, 0)
                        take_y(m, 0)
            for i in range(NT):
                act.wait_ge(sem("y_fin"), i + 1)
                link(A(JUNK, YS[:, i, :], ACT.Square, accum_out=SS[:, i:i + 1]))
                nc.scalar.copy(SS[:, i:i + 1], SS[:, i:i + 1]).then_inc(sem("fin_ss"), 1)
                act.wait_ge(sem("fin_ss"), i + 1)
                act.wait_ge(sem("fin_var"), i + 1)
                A(SS[:, i:i + 1], SS[:, i:i + 1], ACT.Sqrt).then_inc(sem("fin_sqrt"), 1)
                act.wait_ge(sem("fin_sqrt"), i + 1)

        @block.vector
        def _(dve):
            step = [0]

            def link(ins):
                step[0] += 1
                ins.then_inc(sem("dve_step"), 1)
                dve.wait_ge(sem("dve_step"), step[0])

            v = nc.vector
            dve.wait_ge(sem("iota"), 2)
            link(v.tensor_tensor(IDXX, IDXP, IDXF, ALU.bitwise_xor))
            link(v.tensor_copy(XU, IDXX))
            link(v.tensor_scalar(IDENT, XU, 0.5, None, ALU.is_lt))
            link(v.tensor_scalar(BO, XU, 63.5, None, ALU.is_lt))
            link(v.tensor_scalar(BOM, BO, 1.0 / 64, None, ALU.mult))
            link(v.tensor_tensor(MASK2[:, 0, :], IDXF, IDXP, ALU.is_gt))
            link(v.tensor_tensor(MASK2[:, 1, :], IDXF, IDXP, ALU.is_ge))
            link(v.tensor_tensor(XU, XU, MASK2[:, 0, :], ALU.mult))
            for l in range(LEVELS):
                link(v.tensor_scalar(MASKS[:, l, :], XU, 2 ** l - 0.5, None, ALU.is_gt))
                link(v.tensor_scalar(TR[:, 0, 0:P], XU, 2 ** (l + 1) - 0.5, None, ALU.is_gt))
                link(v.tensor_tensor(MASKS[:, l, :], MASKS[:, l, :], TR[:, 0, 0:P], ALU.subtract))
            link(v.tensor_scalar(IDXX[:, 0:1], IDXP[:, 0:1], 16, None, ALU.bitwise_and))
            link(v.tensor_copy(SIGN, IDXX[:, 0:1]))
            v.tensor_scalar(SIGN, SIGN, 0.125, -1.0, ALU.mult, ALU.add).then_inc(sem("masks"), 1)
            dve.wait_ge(sem("masks"), 1)
            full(dve, "par")
            v.tensor_copy(PAR[:, 0:NROWS], bank("par")[:, 0:NROWS]).then_inc(psum_free[bank_of("par")], 1)
            drained(dve, "par")
            link(v.tensor_scalar(OMKA, par("k_a"), -1.0, 1.0, ALU.mult, ALU.add))
            dve.wait_ge(sem("silc"), 1)

            def ada_products(c):
                if c < 8:
                    wait_weights(dve, f"ada{c}")
                else:
                    dve.wait_ge(sem("modw_landed"), 16 * (c - 7))
                if c >= 2:
                    full(dve, f"ada{c - 2}")
                w, a = (wbuf(f"ada{c}", ND, 512), ACC[:, c % 2, :]) if c < 8 else (MODW, ACC2[:, c % 2, :])
                link(v.tensor_scalar(a, w[:, 0, :], SILC[:, 0:1], None, ALU.mult))
                for k in range(1, ND):
                    ins = v.scalar_tensor_tensor(a, w[:, k, :], SILC[:, k:k + 1], a, ALU.mult, ALU.add)
                    if k < ND - 1:
                        link(ins)
                    else:
                        ins.then_inc(sem("ada_ready"), 1)
                        dve.wait_ge(sem("ada_ready"), c + 1)

            def ada_take(c):
                job = f"ada{c}"
                full(dve, job)
                hf = c % 2
                b = bank(job)
                bias = par("b_ada")[:, 4 * c:4 * c + 4]
                s = slice(4 * hf, 4 * hf + 4)
                kind = c // 2
                if kind in (0, 3):
                    v.tensor_tensor((MODB1 if kind == 0 else MODB2)[:, s], b[:, 0:4], bias, ALU.add).then_inc(psum_free[bank_of(job)], 1)
                    drained(dve, job)
                elif kind in (1, 4):
                    m, gv = (MODA1, par("g_pre_mix")) if kind == 1 else (MODA2, par("g_pre_ffn"))
                    link(v.tensor_tensor(m[:, s], b[:, 0:4], bias, ALU.add))
                    v.scalar_tensor_tensor(m[:, s], m[:, s], 1.0, gv[:, s], ALU.add, ALU.mult).then_inc(psum_free[bank_of(job)], 1)
                    drained(dve, job)
                else:
                    dve.wait_ge(sem("grow_landed"), 32)
                    gr = GROW[:, 0 if kind == 2 else 1, hf * 512:(hf + 1) * 512]
                    v.tensor_tensor(gr, b, gr, ALU.mult).then_inc(psum_free[bank_of(job)], 1)
                    drained(dve, job)

            ada_products(0)
            ada_products(1)
            dve.wait_ge(sem("x_ss"), 1)
            v.tensor_scalar(SS, SS, 1.0 / D, RMS_EPS, ALU.mult, ALU.add).then_inc(sem("x_var"), 1)
            dve.wait_ge(sem("x_var"), 1)
            dve.wait_ge(sem("x_sqrt"), 1)
            v.reciprocal(RSTD, RSTD).then_inc(sem("x_rstd"), 1)
            dve.wait_ge(sem("x_rstd"), 1)
            ada_take(0)
            ada_take(1)
            ada_products(2)
            ada_take(2)
            ada_products(3)
            ada_take(3)
            for j in range(0, ND, 2):
                full(dve, f"xT{j}")
                v.tensor_scalar(HT[:, j, :], bank(f"xT{j}"), MODA1[:, j:j + 1], MODB1[:, j:j + 1], ALU.mult, ALU.add).then_inc(psum_free[bank_of(f"xT{j}")], 1)
                drained(dve, f"xT{j}")
            dve.wait_ge(sem("pos_landed"), 16)
            ang, n, t = TR[:, 2, :], TR[:, 3, :], TR[:, 4, :]
            link(v.tensor_copy(ang, POSI))
            link(v.tensor_scalar(ang, ang, par("inv_freq"), None, ALU.mult))
            for k, dst in enumerate((SIN, COS)):
                link(v.tensor_scalar(n, ang, 1.0 / TWO_PI, 0.25 * k, ALU.mult, ALU.add))
                link(v.tensor_scalar(n, n, ROUND, None, ALU.add))
                link(v.tensor_scalar(n, n, ROUND, None, ALU.subtract))
                link(v.scalar_tensor_tensor(t, n, -TP1, ang, ALU.mult, ALU.add))
                link(v.scalar_tensor_tensor(t, n, -TP2, t, ALU.mult, ALU.add))
                link(v.scalar_tensor_tensor(t, n, -TP3, t, ALU.mult, ALU.add))
                link(v.tensor_scalar(t, t, 0.5 * math.pi * k, math.pi, ALU.add, ALU.min))
                v.tensor_scalar(dst, t, -3.1415925, None, ALU.max).then_inc(sem("angle"), 1)
                dve.wait_ge(sem("angle"), k + 1)
            dve.wait_ge(sem("sincos"), 2)
            link(v.tensor_scalar(SIN, SIN, SIGN, None, ALU.mult))

            def latent(job, n, dst, tiles, width, vec, name):
                full(dve, job)
                t = TR[:, n - 1, :]
                v.tensor_scalar(t, bank(job), 1.0 / width, RMS_EPS, ALU.mult, ALU.add).then_inc(psum_free[bank_of(job)], 1)
                drained(dve, job)
                ins = v.tensor_copy(t[:, 0:1], t[:, 0:1])
                ins.then_inc(sem("lat_var"), 1)
                dve.wait_ge(sem("lat_var"), n)
                dve.wait_ge(sem("lat_sqrt"), n)
                link(v.reciprocal(t, t))
                for k in range(tiles):
                    ins = v.scalar_tensor_tensor(dst[:, k, :], dst[:, k, :], par(vec, k), t, ALU.mult, ALU.mult)
                    if k < tiles - 1:
                        link(ins)
                    else:
                        ins.then_inc(sem(name), 1)
                        dve.wait_ge(sem(name), 1)
            latent("cqss", 1, CQ, 3, QR, "g_cq", "cqn")
            latent("ckvss", 2, CKV, 2, KVR, "g_ckv", "ckvn")
            full(dve, "kr")
            v.tensor_tensor(TR[64:96, 2, :], bank("kr")[64:96], COS[64:96], ALU.mult).then_inc(psum_free[bank_of("kr")], 1)
            drained(dve, "kr")
            full(dve, "krs")
            v.tensor_tensor(TR[64:96, 3, :], bank("krs")[64:96], SIN[64:96], ALU.mult).then_inc(psum_free[bank_of("krs")], 1)
            drained(dve, "krs")
            v.tensor_tensor(K[64:96, 0, :], TR[64:96, 2, :], TR[64:96, 3, :], ALU.add).then_inc(sem("k_rope0"), 1)
            dve.wait_ge(sem("k_rope0"), 1)
            ada_products(4)

            def shift(j):
                drained(dve, f"z{j}")
                raw = RAW[:, j % 4, :]
                link(v.tensor_tensor(ZS[:, j, :], raw[:, 0:S], raw[:, 1:], ALU.subtract))
                v.scalar_tensor_tensor(ZS[:, j, :], ZS[:, j, :], par("mu_shift", j), raw[:, 1:], ALU.mult, ALU.add).then_inc(sem("zs"), 1)
                dve.wait_ge(sem("zs"), j + 1)
            for n in range(3):
                for j in range(4 * n, 4 * n + 4):
                    shift(j)
                ada_take(4 + n)
                ada_products(5 + n)
            shift(12)
            shift(13)
            for t in range(2):
                full(dve, f"qr{t}")
                v.tensor_tensor(TR[:, 2, :], bank(f"qr{t}"), COS, ALU.mult).then_inc(psum_free[bank_of(f"qr{t}")], 1)
                drained(dve, f"qr{t}")
                full(dve, f"qs{t}")
                v.tensor_tensor(TR[:, 3, :], bank(f"qs{t}"), SIN, ALU.mult).then_inc(psum_free[bank_of(f"qs{t}")], 1)
                drained(dve, f"qs{t}")
                for j in range(4):
                    r = slice(32 * j, 32 * j + 32)
                    v.tensor_tensor(Q[64:96, 4 * t + j, :], TR[r, 2, :], TR[r, 3, :], ALU.add).then_inc(sem("q_rope"), 1)
                    dve.wait_ge(sem("q_rope"), 4 * t + j + 1)
            ada_take(7)
            for u in range(len(UNITS) + LAG):
                if u < len(UNITS):
                    hd, q = UNITS[u]
                    full(dve, f"s{hd}_{q}")
                    link(v.tensor_reduce(MX[:, u:u + 1], bank(f"s{hd}_{q}")[:, 0:(q + 1) * P], AX.X, ALU.max))
                    v.tensor_scalar(NMX[:, u:u + 1], MX[:, u:u + 1], -ATT_SCALE, None, ALU.mult).then_inc(sem("row_max"), 1)
                    dve.wait_ge(sem("row_max"), u + 1)
                if 1 <= u <= len(UNITS):
                    w = u - 1
                    hd, q = UNITS[w]
                    drained(dve, f"s{hd}_{q}")
                    p = PR[:, w % NPR, 0:(q + 1) * P]
                    link(v.reciprocal(RINV[:, w:w + 1], RSUM[:, w:w + 1]))
                    v.tensor_scalar(p, p, RINV[:, w:w + 1], None, ALU.mult).then_inc(sem("p_ready"), 1)
                    dve.wait_ge(sem("p_ready"), w + 1)
                if u >= LAG:
                    hd, q = UNITS[u - LAG]
                    if q == NT - 1:
                        full(dve, f"o{hd}")
                        r = slice(64 * (hd % 2), 64 * (hd % 2) + 64)
                        v.tensor_copy(OT[r, hd // 2, :], bank(f"o{hd}")[r]).then_inc(psum_free[bank_of(f"o{hd}")], 1)
                        drained(dve, f"o{hd}")
            for j in range(NJ):
                if j == 0:
                    drained(dve, f"t{HEADS - 1}_{NT - 1}")
                v.tensor_scalar(KK[:, j, :], KZ[:, j, :], par("k_k", j), None, ALU.mult).then_inc(sem("kk0"), 1)
                dve.wait_ge(sem("kk0"), j + 1)
            full(dve, "uw0")
            link(v.memset(RESET, 1.0))
            link(v.memset(RESET.rearrange("p j (c t) -> p (j c) t", t=CH)[:, :, 0:1], 0.0))
            for j in range(NJ):
                drained(dve, f"uw{j}")
            link(v.tensor_tensor_scan(CUM.rearrange("p j s -> p (j s)"), RESET.rearrange("p j s -> p (j s)"),
                                     SW.rearrange("p j s -> p (j s)"), 0.0, ALU.mult, ALU.add))
            cum = CUM.rearrange("p j (c t) -> p (j c) t", t=CH)
            mid = MID.rearrange("p j c -> p (j c)")
            link(v.tensor_copy(mid.unsqueeze(2), cum[:, :, CH // 2:CH // 2 + 1]))
            link(v.tensor_tensor(cum, cum, mid.unsqueeze(2).to_broadcast([P, NJ * NC, CH]), ALU.subtract))
            link(v.tensor_copy(FDEC.rearrange("p j c -> p (j c)").unsqueeze(2), cum[:, :, CH - 1:CH]))
            v.tensor_tensor(FDEC[:, :, 0:NC - 1], FDEC[:, :, 0:NC - 1], MID[:, :, 1:NC], ALU.add).then_inc(sem("decay"), 1)
            dve.wait_ge(sem("decay"), 1)
            v.tensor_tensor(SW, CUM, SW, ALU.subtract).then_inc(sem("decay"), 1)
            dve.wait_ge(sem("decay"), 2)
            for j in range(NJ):
                drained(dve, f"kss{j}")
                link(v.tensor_scalar(T1[:, j, :], T1[:, j, :], 1e-12, None, ALU.max))
                link(v.reciprocal(T1[:, j, :], T1[:, j, :]))
                ins = v.tensor_tensor(KK[:, j, :], KK[:, j, :], T1[:, j, :], ALU.mult)
                if j < NJ - 1:
                    link(ins)
                else:
                    ins.then_inc(sem("kkn"), 1)
                    dve.wait_ge(sem("kkn"), 1)
            a4 = AR.rearrange("p j c a t -> p (j c) a t")
            fold = lambda x: x.rearrange("p j (c t) -> p (j c) t", t=CH)
            dve.wait_ge(sem("e_a"), 1)
            link(v.scalar_tensor_tensor(a4[:, :, 0, :], fold(KK), -1.0, fold(SW), ALU.mult, ALU.mult))
            for j in range(NJ):
                drained(dve, f"ua{j}")
            link(v.tensor_tensor(KK, KK, AA, ALU.mult))
            dve.wait_ge(sem("e_r"), 1)
            v.tensor_tensor(a4[:, :, 1, :], fold(RZ), fold(T1), ALU.mult).then_inc(sem("r_done"), 1)
            dve.wait_ge(sem("r_done"), 1)
            for j in range(NJ):
                dve.wait_ge(sem("k_scaled"), j + 1)
                v.scalar_tensor_tensor(RZ[:, j, :], RZ[:, j, :], par("r_k", j), KZ[:, j, :], ALU.mult, ALU.mult).then_inc(sem("rk"), 1)
                dve.wait_ge(sem("rk"), j + 1)
            dve.wait_ge(sem("e_b"), 1)
            link(v.tensor_tensor(BT, KK, T1, ALU.mult))
            dve.wait_ge(sem("e_f"), 1)
            for j in range(NJ):
                drained(dve, f"ug{j}")
            v.tensor_tensor(KT, KZ, T1, ALU.mult).then_inc(sem("rwkv_in"), 1)
            dve.wait_ge(sem("rwkv_in"), 1)
            for j in range(NJ):
                full(dve, f"bon{j}")
                v.tensor_tensor(BONUS[:, j, :], bank(f"bon{j}"), VZ[:, j, :], ALU.mult).then_inc(psum_free[bank_of(f"bon{j}")], 1)
                drained(dve, f"bon{j}")
            for c in range(NC):
                for g in range(2):
                    for name, dst in (("mr", MR), ("nr", NR)):
                        for n in range(2):
                            job = f"{name}{c}_{g}_{n}"
                            full(dve, job)
                            q = 4 * g + 2 * n
                            v.tensor_tensor(dst[:, q:q + 2, :], bank(job).rearrange("p (h t) -> p h t", h=2), MASK2.rearrange("p a t -> p (a t)").unsqueeze(1).to_broadcast([P, 2, 2 * CH]), ALU.mult).then_inc(psum_free[bank_of(job)], 1)
                            drained(dve, job)
                for l in range(1, LEVELS):
                    for name, dst in (("dx", XI), ("dt", XT)):
                        if name == "dx" and l == LEVELS - 1:
                            continue
                        for g in range(2):
                            job = f"{name}{c}_{l}_{g}"
                            full(dve, job)
                            d = dst[:, 4 * g:4 * g + 4, :].rearrange("p a b -> p (a b)")
                            v.tensor_tensor(d, bank(job), d, ALU.add).then_inc(psum_free[bank_of(job)], 1)
                            drained(dve, job)
                full(dve, f"sa{c}")
                v.tensor_copy(SA.rearrange("p a b -> p (a b)"), bank(f"sa{c}")).then_inc(psum_free[bank_of(f"sa{c}")], 1)
                drained(dve, f"sa{c}")
                if c < NC - 1:
                    job = f"st{c}"
                    full(dve, job)
                    b = bank(job)[:, 0:NJ * VD].rearrange("p (j v) -> p j v", v=VD)
                    f = FDEC[:, :, c:c + 1].to_broadcast([P, NJ, VD])
                    if c == 0:
                        v.tensor_tensor(ST, b, f, ALU.mult).then_inc(psum_free[bank_of(job)], 1)
                        drained(dve, job)
                    else:
                        link(v.tensor_tensor(ST, b, ST, ALU.add))
                        v.tensor_tensor(ST, ST, f, ALU.mult).then_inc(psum_free[bank_of(job)], 1)
                        drained(dve, job)
            for j in range(NJ):
                full(dve, f"gm{j}")
                v.tensor_tensor(YT[:, j, :], YT[:, j, :], bank(f"gm{j}"), ALU.subtract).then_inc(psum_free[bank_of(f"gm{j}")], 1)
                drained(dve, f"gm{j}")
                v.tensor_copy(MX[:, 1:2], MX[:, 1:2]).then_inc(sem("y_c"), 1)
                dve.wait_ge(sem("y_c"), j + 1)
            for j in range(NJ):
                full(dve, f"gv{j}")
                v.tensor_scalar(KK[:, j, :], bank(f"gv{j}"), GN_EPS, None, ALU.add).then_inc(psum_free[bank_of(f"gv{j}")], 1)
                drained(dve, f"gv{j}")
                v.tensor_copy(MX[:, 1:2], MX[:, 1:2]).then_inc(sem("y_var"), 1)
                dve.wait_ge(sem("y_var"), j + 1)
            for j in range(NJ):
                dve.wait_ge(sem("y_sqrt"), j + 1)
                link(v.reciprocal(KK[:, j, :], KK[:, j, :]))
                link(v.tensor_tensor(YT[:, j, :], YT[:, j, :], KK[:, j, :], ALU.mult))
                link(v.tensor_scalar(YT[:, j, :], YT[:, j, :], par("lnx_w", j), par("lnx_b", j), ALU.mult, ALU.add))
                link(v.tensor_tensor(YT[:, j, :], YT[:, j, :], BONUS[:, j, :], ALU.add))
                ins = v.tensor_tensor(YT[:, j, :], YT[:, j, :], G[:, j, :], ALU.mult)
                if j < NJ - 1:
                    link(ins)
                else:
                    ins.then_inc(sem("rwkv_out"), 1)
                    dve.wait_ge(sem("rwkv_out"), 1)
            for hf in range(2):
                if hf == 0:
                    ada_products(8)
                ada_take(8 + hf)
                if hf:
                    ada_products(10)
                for j in range(4):
                    job = f"om{hf}_{j}"
                    full(dve, job)
                    drained(dve, f"gb{hf}_{j}")
                    v.tensor_tensor(GA[:, j, :], bank(job), GA[:, j, :], ALU.mult).then_inc(psum_free[bank_of(job)], 1)
                    drained(dve, job)
                for j in range(4):
                    job = f"or{hf}_{j}"
                    full(dve, job)
                    v.tensor_tensor(GB[:, j, :], bank(job), GB[:, j, :], ALU.mult).then_inc(psum_free[bank_of(job)], 1)
                    drained(dve, job)
                    v.tensor_tensor(MIX[:, 4 * hf + j, :], GA[:, j, :], GB[:, j, :], ALU.add).then_inc(sem("mix"), 1)
                    dve.wait_ge(sem("mix"), 4 * hf + j + 1)
                ada_products(9 if hf == 0 else 11)
            dve.wait_ge(sem("x_landed"), 32)
            for i in range(NT + 1):
                if i < NT:
                    dve.wait_ge(sem("y_ss"), i + 1)
                    link(v.tensor_tensor(SS4[:, i:i + 1], SSY[:, 2 * i:2 * i + 1], SSY[:, 2 * i + 1:2 * i + 2], ALU.add))
                    v.tensor_scalar(SS4[:, i:i + 1], SS4[:, i:i + 1], 1.0 / D, RMS_EPS, ALU.mult, ALU.add).then_inc(sem("yo_var"), 1)
                    dve.wait_ge(sem("yo_var"), i + 1)
                    dve.wait_ge(sem("yo_sqrt"), i + 1)
                    link(v.reciprocal(SS4[:, i:i + 1], SS4[:, i:i + 1]))
                    for n in range(2):
                        job = f"yo{i}_{n}"
                        xs = X[:, i, n * 512:(n + 1) * 512]
                        v.scalar_tensor_tensor(TUP, bank(job), SS4[:, i:i + 1], GROW[:, 0, n * 512:(n + 1) * 512], ALU.mult, ALU.mult).then_inc(psum_free[bank_of(job)], 1)
                        drained(dve, job)
                        ins = v.tensor_tensor(xs, xs, TUP, ALU.add)
                        if n == 0:
                            link(ins)
                        else:
                            ins.then_inc(sem("x1"), 1)
                            dve.wait_ge(sem("x1"), i + 1)
                if i == 1:
                    ada_take(10)
                    ada_take(11)
                if i > 0:
                    dve.wait_ge(sem("x1_ss"), i)
                    v.tensor_scalar(SS2[:, i - 1:i], SS2[:, i - 1:i], 1.0 / D, RMS_EPS, ALU.mult, ALU.add).then_inc(sem("x1_var"), 1)
                    dve.wait_ge(sem("x1_var"), i)
                    dve.wait_ge(sem("x1_sqrt"), i)
                    link(v.reciprocal(RS2[:, i - 1:i], RS2[:, i - 1:i]))
                    v.tensor_scalar(XN2[:, i - 1, :], X[:, i - 1, :], RS2[:, i - 1:i], None, ALU.mult).then_inc(sem("xn2"), 1)
                    dve.wait_ge(sem("xn2"), i)
            for j in range(0, ND, 2):
                full(dve, f"hT{j}")
                v.tensor_scalar(HT[:, j, :], bank(f"hT{j}"), MODA2[:, j:j + 1], MODB2[:, j:j + 1], ALU.mult, ALU.add).then_inc(psum_free[bank_of(f"hT{j}")], 1)
                drained(dve, f"hT{j}")
            for n in range(8):
                link(v.memset(RANKW[:, n:n + 1], float(8 - n)))
            dve.wait_ge(sem("route_iota"), 3)
            link(v.tensor_copy(EIDX, EIDI))
            link(v.tensor_copy(BIDX, BIDI))
            link(v.memset(UNIT, 1.0))
            link(v.memset(REC, 0))
            link(v.tensor_copy(REC[:, :, :, 0], TOK4))
            for k in range(2):
                link(v.tensor_scalar(REC[:, k, :, 1], TOK4[:, k], 2.0, float(k), ALU.mult, ALU.add))
            full(dve, "lgT")
            v.tensor_copy(LT[0:36, :], bank("lgT")[0:36, :]).then_inc(psum_free[bank_of("lgT")], 1)
            drained(dve, "lgT")
            full(dve, "lg")
            v.tensor_copy(LOGITS.rearrange("p i e -> p (i e)"), bank("lg")[:, 0:NT * 36]).then_inc(psum_free[bank_of("lg")], 1)
            drained(dve, "lg")
            gl, el = LOGITS[:, :, 0:NG], LOGITS[:, :, NG:].rearrange("p i (g e) -> p i g e", e=EG)

            def first_max(vals, n, mx, hot):
                link(v.tensor_reduce(mx, vals, AX.X, ALU.max))
                link(v.tensor_tensor(hot, vals, mx.unsqueeze(2).to_broadcast([P, NT, n]), ALU.is_equal))
                link(v.tensor_tensor(hot, hot, RANKW[:, 8 - n:8].unsqueeze(1).to_broadcast([P, NT, n]), ALU.mult))
                link(v.tensor_reduce(TMX, hot, AX.X, ALU.max))
                link(v.tensor_tensor(hot, hot, TMX.unsqueeze(2).to_broadcast([P, NT, n]), ALU.is_equal))
            first_max(gl, NG, GMX, GHOT)
            v.tensor_tensor(GEXP, gl, GMX.unsqueeze(2).to_broadcast([P, NT, NG]), ALU.subtract).then_inc(sem("gmax"), 1)
            dve.wait_ge(sem("gmax"), 1)
            dve.wait_ge(sem("gexp"), 1)
            link(v.tensor_reduce(PSEL, GEXP, AX.X, ALU.add))
            link(v.reciprocal(PSEL, PSEL))
            e4 = STMP.rearrange("p a b c -> p (a b c)")[:, 0:NT * NE].rearrange("p (i g e) -> p i g e", g=NG, e=EG)
            link(v.tensor_tensor(e4, el, GHOT.unsqueeze(3).to_broadcast([P, NT, NG, EG]), ALU.mult))
            link(v.tensor_reduce(EIN, e4.rearrange("p i g e -> p i e g"), AX.X, ALU.add))
            first_max(EIN, EG, EMX1, HOT1)
            link(v.scalar_tensor_tensor(ETMP, HOT1, NEG, EIN, ALU.mult, ALU.add))
            first_max(ETMP, EG, EMX2, HOT2)
            v.tensor_tensor(E21, EMX2, EMX1, ALU.subtract).then_inc(sem("emax"), 1)
            dve.wait_ge(sem("emax"), 1)
            for k in range(2):
                link(v.tensor_tensor(SEL[:, k].rearrange("p i (g e) -> p i g e", e=EG), HOTS[:, k].unsqueeze(2).to_broadcast([P, NT, NG, EG]),
                                     GHOT.unsqueeze(3).to_broadcast([P, NT, NG, EG]), ALU.mult))
            v.tensor_tensor(SEL[:, 2], SEL[:, 0], SEL[:, 1], ALU.add).then_inc(sem("sel"), 1)
            dve.wait_ge(sem("eexp"), 1)
            link(v.tensor_scalar(W1, E21, 1.0, None, ALU.add))
            link(v.reciprocal(W1, W1))
            link(v.tensor_tensor(W1, W1, PSEL, ALU.mult))
            link(v.tensor_tensor(E21, E21, W1, ALU.mult))
            link(v.tensor_copy(REC[:, :, :, 2].bitcast(F32), W12))

            def of_choice(dst, src):
                link(v.tensor_tensor(STMP, SEL[:, 0:2], src, ALU.mult))
                link(v.tensor_reduce(dst, STMP, AX.X, ALU.add))
            every = lambda x: x.unsqueeze(1).unsqueeze(1).to_broadcast([P, 2, NT, NE])
            of_choice(EK, every(EIDX))
            full(dve, "rank")
            link(v.tensor_copy(RANK.rearrange("p i e -> p (i e)"), bank("rank")[:, 0:NT * NE]))
            v.tensor_copy(CNT, bank("rank")[:, NT * NE:(NT + 1) * NE]).then_inc(psum_free[bank_of("rank")], 1)
            drained(dve, "rank")

            def whole(out_, x, less):
                link(v.tensor_scalar(out_, x, 1.0 / CAP, -(less + 0.5 * (CAP - 1)) / CAP, ALU.mult, ALU.add))
                link(v.tensor_scalar(out_, out_, ROUND, None, ALU.add))
                link(v.tensor_scalar(out_, out_, ROUND, 0.0, ALU.subtract, ALU.max))
            whole(EXTRA, CNT, 1)
            link(v.tensor_tensor_scan(INCL, UNIT, EXTRA, 0.0, ALU.mult, ALU.add))
            link(v.tensor_tensor(EXTRA, INCL, EXTRA, ALU.subtract))
            link(v.scalar_tensor_tensor(EXTRA, EXTRA, NE - 1.0, EIDX, ALU.add, ALU.subtract))
            of_choice(XK, every(EXTRA))
            of_choice(RK, RANK.unsqueeze(1).to_broadcast([P, 2, NT, NE]))
            whole(QK, RK, 0)
            link(v.tensor_tensor(XK, XK, QK, ALU.add))
            link(v.scalar_tensor_tensor(XK, QK, 1.0, XK, ALU.min, ALU.mult))
            link(v.tensor_tensor(XK, XK, EK, ALU.add))
            link(v.scalar_tensor_tensor(RK, QK, -float(CAP), RK, ALU.mult, ALU.add))
            link(v.tensor_scalar(HK, XK, 0.5, -0.25, ALU.mult, ALU.add))
            link(v.tensor_scalar(HK, HK, ROUND, None, ALU.add))
            link(v.tensor_scalar(HK, HK, ROUND, None, ALU.subtract))
            link(v.scalar_tensor_tensor(RK, XK, float(CAP), RK, ALU.mult, ALU.add))
            link(v.scalar_tensor_tensor(RK, HK, -2.0 * CAP, RK, ALU.mult, ALU.add))
            link(v.scalar_tensor_tensor(RK, RK, float(NPAIR), HK, ALU.mult, ALU.add))
            v.tensor_copy(ROWI, RK).then_inc(sem("records"), 1)
            dve.wait_ge(sem("records"), 1)
            link(v.tensor_tensor(OVT, INCL.unsqueeze(1).to_broadcast([P, XBLK, NE]), BIDX.unsqueeze(2).to_broadcast([P, XBLK, NE]), ALU.is_le))
            link(v.tensor_reduce(OVS, OVT, AX.X, ALU.add))
            link(v.tensor_scalar(OVS, OVS, NE - 1.0, None, ALU.min))
            link(v.tensor_copy(OVE, OVS))
            link(v.tensor_scalar(OVS, BIDX, 2.0, None, ALU.mult))
            link(v.tensor_scalar(OVS, OVS, INCL[:, NE - 1:NE], None, ALU.is_lt))
            link(v.tensor_copy(OVA, OVS))
            v.tensor_copy(OVN, INCL[:, NE - 1:NE]).then_inc(sem("overflow_known"), 1)

            def pair(m, p):
                dve.wait_ge(sem("sil_ready"), m + 1)
                v.tensor_tensor(ACTB[:, p, :], ps[:, GU_BANK[p], FF:], SIL[:, p, :], ALU.mult).then_inc(sem("act_ready"), 1)
                dve.wait_ge(sem("at_full"), m + 1)
                v.tensor_copy(ACTT[:, p].rearrange("p k t -> p (k t)"), ps[:, AT_BANK, 0:2 * P]).then_inc(sem("at_free"), 1)
                dve.wait_ge(sem("dn_full"), m * 2 + 1)
                dve.wait_ge(sem("sr_ready"), m + 1)
                v.tensor_scalar(YB[:, p, 0:512], ps[:, DN_BANK[0], :], SR[:, p, 2:3].bitcast(F32), None, ALU.mult).then_inc(sem("dn_free0"), 1)
            with dve.Fori(0, NE // NB) as i:
                pair(i * 2, 0)
                pair(i * 2 + 1, 1)
            more = dve.value_load(OVN[0:1, 0:1], min_val=0, max_val=XBLK)
            with dve.If(more > 0):
                with dve.Fori(0, XPAIR) as i:
                    active = dve.value_load(OVA[0:1, bass.ds(i, 1)], min_val=0, max_val=1)
                    with dve.If(active > 0):
                        pair(i + NP1, 0)
            for i in range(NT + 1):
                if i < NT:
                    dve.wait_ge(sem(f"rows_landed{i}"), 16)
                    v.tensor_tensor(YS[:, i, :], YL[:, i, 0, :], YL[:, i, 1, :], ALU.add).then_inc(sem("y_fin"), 1)
                if i > 0:
                    j = i - 1
                    s1 = SS[:, j:j + 1]
                    dve.wait_ge(sem("fin_ss"), j + 1)
                    v.tensor_scalar(s1, s1, 1.0 / D, RMS_EPS, ALU.mult, ALU.add).then_inc(sem("fin_var"), 1)
                    dve.wait_ge(sem("fin_var"), j + 1)
                    dve.wait_ge(sem("fin_sqrt"), j + 1)
                    link(v.reciprocal(s1, s1))
                    link(v.scalar_tensor_tensor(YS[:, j, :], YS[:, j, :], s1, GROW[:, 1, :], ALU.mult, ALU.mult))
                    v.tensor_tensor(X[:, j, :], X[:, j, :], YS[:, j, :], ALU.add).then_inc(sem("out_ready"), 1)
                    dve.wait_ge(sem("out_ready"), j + 1)


_INS = ['x', 'c', 'positions', 'w_ada', 'b_ada', 'g_pre_mix', 'g_post_mix', 'g_pre_ffn', 'g_post_ffn',
        'w_in', 'g_cq', 'w_uq', 'g_ckv', 'w_ukv', 'w_o_mla', 'mu_shift', 'w_decay_up', 'decay_bias',
        'w_a_up', 'a_bias', 'w_g_up', 'k_k', 'k_a', 'r_k', 'lnx_w', 'lnx_b', 'w_o_rwkv', 'w_out',
        'w_router_group', 'b_router_group', 'w_router_expert', 'b_router_expert',
        'w_exp_gate', 'w_exp_up', 'w_exp_down']


def kernel(**inputs):
    import numpy as _np
    import concourse.bacc as _bacc
    from concourse import mybir as _mybir
    from concourse.bass_utils import run_bass_kernel_spmd as _run

    nc = _bacc.Bacc("TRN2", target_bir_lowering=False, num_devices=1)
    arrays, aps = {}, {}
    for name in _INS:
        a = _np.ascontiguousarray(inputs[name])
        arrays[f"in_{name}"] = a
        aps[name] = nc.dram_tensor(f"in_{name}", a.shape, _mybir.dt.from_np(a.dtype), kind="ExternalInput").ap()
    freq = _np.tile((ROPE_THETA ** (-_np.arange(0, ROPE, 2) / ROPE)).astype(_np.float32), 128 // (ROPE // 2))[None, :]
    arrays["rope_inv_freq"] = freq
    aps["inv_freq"] = nc.dram_tensor("rope_inv_freq", freq.shape, _mybir.dt.float32, kind="ExternalInput").ap()
    out = nc.dram_tensor("out_0", (1, S, D), _mybir.dt.float32, kind="ExternalOutput").ap()
    layer(nc, aps, out)
    r = _run(nc, [arrays], core_ids=[0])
    return r.results[0]["out_0"]
```
